# Optimizing a Trainium2 kernel written in Bass

```python
import jax, jax.numpy as jnp
from jax import lax
import numpy as np
import math

D_MODEL = 1024
BATCH = 1
SEQ = 512
DEPTH = 2

CTX_LEN = 256
GRID_W = 64
D_MIX = D_MODEL
W_ATTN = D_MIX // 4
W_FOURIER = D_MIX // 4
W_CONV = D_MIX // 4
W_POOL = D_MIX // 4
HEAD_DIM = 64
N_Q_HEADS = W_ATTN // HEAD_DIM
N_KV_HEADS = 2
Q_PER_KV = N_Q_HEADS // N_KV_HEADS
N_FOURIER_HEADS = 4
FOURIER_HEAD_DIM = W_FOURIER // N_FOURIER_HEADS
CONV_WIDTH = 31
POOL_WINDOWS = (2, 4, 8, 16)
POOL_GROUP = W_POOL // len(POOL_WINDOWS)
D_FF = -(-(8 * D_MODEL) // (3 * 256)) * 256
ROPE_THETA = 10000.0
Q_BLOCK = 128
EPS = 1e-6
ATTN_SCALE = HEAD_DIM ** -0.5

OFF_Q = 0
OFF_K = OFF_Q + N_Q_HEADS * HEAD_DIM
OFF_V = OFF_K + N_KV_HEADS * HEAD_DIM
OFF_F = OFF_V + N_KV_HEADS * HEAD_DIM
OFF_C = OFF_F + W_FOURIER
OFF_P = OFF_C + 2 * W_CONV
D_IN = OFF_P + W_POOL


def rms_norm(x, g):
    xf = x.astype(jnp.float32)
    y = xf * lax.rsqrt(jnp.mean(xf * xf, axis=-1, keepdims=True) + EPS)
    return (y * g.astype(jnp.float32)).astype(x.dtype)

def layer_norm(x, g, b):
    xf = x.astype(jnp.float32)
    xc = xf - jnp.mean(xf, axis=-1, keepdims=True)
    y = xc * lax.rsqrt(jnp.mean(xc * xc, axis=-1, keepdims=True) + EPS)
    return (y * g.astype(jnp.float32) + b.astype(jnp.float32)).astype(x.dtype)

def axial_rope_tables(n, dtype):
    rows = n // GRID_W
    row = jnp.repeat(jnp.arange(rows, dtype=jnp.float32), GRID_W)
    col = jnp.tile(jnp.arange(GRID_W, dtype=jnp.float32), rows)
    n_freq = HEAD_DIM // 4
    inv_freq = ROPE_THETA ** (-jnp.arange(n_freq, dtype=jnp.float32) / n_freq)
    ang = jnp.concatenate([row[:, None] * inv_freq, col[:, None] * inv_freq], axis=-1)
    return jnp.cos(ang).astype(dtype), jnp.sin(ang).astype(dtype)

def apply_rope(x, cos, sin):
    xp = x.reshape(x.shape[:-1] + (HEAD_DIM // 2, 2))
    x0, x1 = xp[..., 0], xp[..., 1]
    cs = cos[None, :, None, :]
    sn = sin[None, :, None, :]
    return jnp.stack([x0 * cs - x1 * sn, x0 * sn + x1 * cs], axis=-1).reshape(x.shape)

def q_heads(pq, q_g):
    b, n, _ = pq.shape
    return rms_norm(pq.reshape(b, n, N_Q_HEADS, HEAD_DIM), q_g)

def kv_heads(pkv, k_g):
    b, n, _ = pkv.shape
    kv = pkv.reshape(b, n, 2, N_KV_HEADS, HEAD_DIM)
    return rms_norm(kv[:, :, 0], k_g), kv[:, :, 1]

def attend(q, k, v):
    b, nq = q.shape[:2]
    qg = q.reshape(b, nq, N_KV_HEADS, Q_PER_KV, HEAD_DIM)
    s = jnp.einsum('bqhgd,bkhd->bhgqk', qg, k).astype(jnp.float32) * ATTN_SCALE
    p = jax.nn.softmax(s, axis=-1).astype(v.dtype)
    o = jnp.einsum('bhgqk,bkhd->bqhgd', p, v)
    return o.reshape(b, nq, N_Q_HEADS * HEAD_DIM)

def attend_query_blocks(q, k, v):
    b, n = q.shape[:2]
    nb = n // Q_BLOCK
    qb = jnp.swapaxes(q.reshape(b, nb, Q_BLOCK, N_Q_HEADS, HEAD_DIM), 0, 1)
    ob = lax.map(lambda qi: attend(qi, k, v), qb)
    return jnp.swapaxes(ob, 0, 1).reshape(b, n, N_Q_HEADS * HEAD_DIM)

def fourier_mixer(u, w_f):
    b, n, _ = u.shape
    uf = u.astype(jnp.float32).reshape(b, n, N_FOURIER_HEADS, FOURIER_HEAD_DIM)
    y = jnp.fft.fft2(uf, axes=(1, 3), norm='ortho').real
    return y.reshape(b, n, W_FOURIER).astype(u.dtype) @ w_f

def conv_module(a, dw_w, dw_b, ln_g, ln_b, w_pw):
    glu = a[..., :W_CONV] * jax.nn.sigmoid(a[..., W_CONV:])
    y = lax.conv_general_dilated(
        glu, dw_w[:, None, :], window_strides=(1,),
        padding=[(CONV_WIDTH // 2, CONV_WIDTH // 2)],
        dimension_numbers=('NWC', 'WIO', 'NWC'),
        feature_group_count=W_CONV) + dw_b
    y = jax.nn.silu(layer_norm(y, ln_g, ln_b))
    return y @ w_pw

def pool_mixer(u, w_pool, scale):
    b, n, _ = u.shape
    uf = u.astype(jnp.float32)
    csum = jnp.concatenate([jnp.zeros((b, 1, W_POOL), jnp.float32), jnp.cumsum(uf, axis=1)], axis=1)
    t = jnp.arange(n)
    groups = []
    for gi, win in enumerate(POOL_WINDOWS):
        sl = slice(gi * POOL_GROUP, (gi + 1) * POOL_GROUP)
        lo = jnp.clip(t - win // 2, 0, n)
        hi = jnp.clip(t - win // 2 + win, 0, n)
        cs = csum[..., sl]
        cnt = (hi - lo).astype(jnp.float32)[None, :, None]
        mean = (jnp.take(cs, hi, axis=1) - jnp.take(cs, lo, axis=1)) / cnt
        groups.append(mean - uf[..., sl])
    y = jnp.stack(groups, axis=2).astype(u.dtype)
    y = jnp.einsum('blgc,gcd->blgd', y, w_pool).reshape(b, n, W_POOL)
    return y * scale

def swiglu(x, w_in, w_out):
    a, g = jnp.split(x @ w_in, 2, axis=-1)
    return (jax.nn.silu(a) * g) @ w_out

def mixers_and_ffn(x, p, attn, gate1, shift2, scale2, gate2, g2, w_f, dw_w, dw_b,
                   ln_g, ln_b, w_pw, w_pl, pl_scale, w_o, w_fi, w_fo):
    four = fourier_mixer(p[..., OFF_F:OFF_C], w_f)
    conv = conv_module(p[..., OFF_C:OFF_P], dw_w, dw_b, ln_g, ln_b, w_pw)
    pool = pool_mixer(p[..., OFF_P:], w_pl, pl_scale)
    mix = jnp.concatenate([attn, four, conv, pool], axis=-1) @ w_o
    x = x + gate1 * mix
    xn = rms_norm(x, g2) * (1 + scale2) + shift2
    return x + gate2 * swiglu(xn, w_fi, w_fo)

def first_inputs(seed: int = 0) -> dict:
    key = jax.random.key(seed)
    ks = jax.random.split(key, 24)
    f32 = jnp.float32
    L = DEPTH
    D = D_MODEL

    def nrm(k, shape, scale):
        return jax.random.normal(k, shape, f32) * scale

    return {
        'x': nrm(ks[0], (BATCH, SEQ, D), 1.0),
        'c': nrm(ks[1], (BATCH, D), 1.0),
        'ctx': nrm(ks[2], (BATCH, CTX_LEN, D), 1.0),
        'c_ctx': nrm(ks[3], (D,), 1.0),
        'w_mod': nrm(ks[4], (L, D, 6 * D), D ** -0.5),
        'b_mod': nrm(ks[5], (L, 6 * D), 0.02),
        'g_norm1': 1.0 + nrm(ks[6], (L, D), 0.02),
        'g_norm2': 1.0 + nrm(ks[7], (L, D), 0.02),
        'w_in': nrm(ks[8], (L, D, D_IN), D ** -0.5),
        'q_norm_g': 1.0 + nrm(ks[9], (L, HEAD_DIM), 0.02),
        'k_norm_g': 1.0 + nrm(ks[10], (L, HEAD_DIM), 0.02),
        'w_fourier': nrm(ks[11], (L, W_FOURIER, W_FOURIER), W_FOURIER ** -0.5),
        'conv_dw_w': nrm(ks[12], (L, CONV_WIDTH, W_CONV), CONV_WIDTH ** -0.5),
        'conv_dw_b': nrm(ks[13], (L, W_CONV), 0.02),
        'conv_ln_g': 1.0 + nrm(ks[14], (L, W_CONV), 0.02),
        'conv_ln_b': nrm(ks[15], (L, W_CONV), 0.02),
        'w_conv_pw': nrm(ks[16], (L, W_CONV, W_CONV), W_CONV ** -0.5),
        'w_pool': nrm(ks[17], (L, len(POOL_WINDOWS), POOL_GROUP, POOL_GROUP), POOL_GROUP ** -0.5),
        'pool_scale': 1.0 + nrm(ks[18], (L, W_POOL), 0.02),
        'w_out': nrm(ks[19], (L, D_MIX, D), D_MIX ** -0.5),
        'w_ffn_in': nrm(ks[20], (L, D, 2 * D_FF), D ** -0.5),
        'w_ffn_out': nrm(ks[21], (L, D_FF, D), D_FF ** -0.5),
    }

def first_block(x, c, ctx, c_ctx, w_mod, b_mod, g_norm1, g_norm2, w_in, q_norm_g, k_norm_g,
              w_fourier, conv_dw_w, conv_dw_b, conv_ln_g, conv_ln_b, w_conv_pw, w_pool,
              pool_scale, w_out, w_ffn_in, w_ffn_out):
    n = x.shape[1]
    cos, sin = axial_rope_tables(n, x.dtype)
    h = ctx
    sc = jax.nn.silu(c)
    scc = jax.nn.silu(c_ctx)
    for l in range(DEPTH):
        last = l == DEPTH - 1
        mod = jnp.split(sc @ w_mod[l] + b_mod[l], 6, axis=-1)
        shift1, scale1, gate1, shift2, scale2, gate2 = [m[:, None, :] for m in mod]
        n_ctx_mod = 2 if last else 6
        mod_c = jnp.split(scc @ w_mod[l][:, :n_ctx_mod * D_MODEL] + b_mod[l][:n_ctx_mod * D_MODEL], n_ctx_mod)

        hn = rms_norm(h, g_norm1[l]) * (1 + mod_c[1]) + mod_c[0]
        if last:
            kc, vc = kv_heads(hn @ w_in[l][:, OFF_K:OFF_F], k_norm_g[l])
        else:
            pc = hn @ w_in[l]
            qc = q_heads(pc[..., OFF_Q:OFF_K], q_norm_g[l])
            kc, vc = kv_heads(pc[..., OFF_K:OFF_F], k_norm_g[l])

        xn = rms_norm(x, g_norm1[l]) * (1 + scale1) + shift1
        p = xn @ w_in[l]
        q = apply_rope(q_heads(p[..., OFF_Q:OFF_K], q_norm_g[l]), cos, sin)
        k, v = kv_heads(p[..., OFF_K:OFF_F], k_norm_g[l])
        k = apply_rope(k, cos, sin)
        attn = attend_query_blocks(q, jnp.concatenate([kc, k], axis=1), jnp.concatenate([vc, v], axis=1))
        x_new = mixers_and_ffn(x, p, attn, gate1, shift2, scale2, gate2, g_norm2[l],
                               w_fourier[l], conv_dw_w[l], conv_dw_b[l], conv_ln_g[l], conv_ln_b[l],
                               w_conv_pw[l], w_pool[l], pool_scale[l], w_out[l], w_ffn_in[l], w_ffn_out[l])
        if not last:
            attn_c = attend(qc, kc, vc)
            h = mixers_and_ffn(h, pc, attn_c, mod_c[2], mod_c[3], mod_c[4], mod_c[5], g_norm2[l],
                               w_fourier[l], conv_dw_w[l], conv_dw_b[l], conv_ln_g[l], conv_ln_b[l],
                               w_conv_pw[l], w_pool[l], pool_scale[l], w_out[l], w_ffn_in[l], w_ffn_out[l])
        x = x_new
    return x


RET_HEADS = 8
RET_DK = 64
RET_DV = 128
RET_CHUNK = 128
CONV_W = 1024
CONV_K = 3
MLA_HEADS = 8
MLA_NOPE = 128
MLA_ROPE = 64
MLA_DV = 128
Q_LORA = 384
KV_LORA = 256
ATTN_BLOCK = 128
ROPE_BASE = 10000.0
N_EVEN = (DEPTH + 1) // 2
N_ODD = DEPTH // 2

RET_QK = RET_HEADS * RET_DK
RET_V = RET_HEADS * RET_DV
EVEN_SPLITS = (RET_QK, RET_QK, RET_V, RET_V, CONV_W, CONV_W, CONV_W, CONV_W)
EVEN_IN = sum(EVEN_SPLITS)
EVEN_MIX = RET_V + CONV_W
MLA_QK = MLA_NOPE + MLA_ROPE
MLA_V = MLA_HEADS * MLA_DV
ODD_SPLITS = (Q_LORA, KV_LORA, MLA_ROPE, MLA_V)
ODD_IN = sum(ODD_SPLITS)


def rms_norm_2(x, g):
    xf = x.astype(jnp.float32)
    y = xf * lax.rsqrt(jnp.mean(xf * xf, axis=-1, keepdims=True) + EPS)
    return (y * g.astype(jnp.float32)).astype(x.dtype)

def rope(x, positions):
    d = x.shape[-1]
    inv = ROPE_BASE ** (-jnp.arange(0, d, 2, dtype=jnp.float32) / d)
    ang = positions.astype(jnp.float32)[..., None] * inv
    cos = jnp.cos(ang)[:, :, None, :]
    sin = jnp.sin(ang)[:, :, None, :]
    xf = x.astype(jnp.float32)
    x1, x2 = xf[..., : d // 2], xf[..., d // 2:]
    out = jnp.concatenate([x1 * cos - x2 * sin, x1 * sin + x2 * cos], axis=-1)
    return out.astype(x.dtype)

def split_cols(h, sizes):
    return jnp.split(h, np.cumsum(sizes)[:-1].tolist(), axis=-1)

def retention(q, k, v):
    b, s, h, dk = q.shape
    dv = v.shape[-1]
    c = RET_CHUNK
    n = s // c
    dt = q.dtype
    log_gamma = jnp.log1p(-jnp.exp2(-5.0 - jnp.arange(h, dtype=jnp.float32)))
    i = jnp.arange(c, dtype=jnp.float32)
    rel = i[:, None] - i[None, :]
    intra = jnp.where(rel >= 0, jnp.exp(log_gamma[:, None, None] * jnp.maximum(rel, 0.0)), 0.0).astype(dt)
    xi = jnp.exp(log_gamma[:, None] * (i + 1.0)).astype(dt)
    zeta = jnp.exp(log_gamma[:, None] * (c - 1.0 - i)).astype(dt)
    gamma_c = jnp.exp(log_gamma * c).astype(dt)
    qc = q.reshape(b, n, c, h, dk)
    kc = k.reshape(b, n, c, h, dk)
    vc = v.reshape(b, n, c, h, dv)
    scores = jnp.einsum('bnihd,bnjhd->bnhij', qc, kc) * intra
    inner = jnp.einsum('bnhij,bnjhe->bnihe', scores, vc)
    kv = jnp.einsum('bnjhd,hj,bnjhe->nbhde', kc, zeta, vc)

    def step(state, kv_i):
        return gamma_c[None, :, None, None] * state + kv_i, state

    _, prev = lax.scan(step, jnp.zeros((b, h, dk, dv), dt), kv)
    cross = jnp.einsum('bnihd,nbhde,hi->bnihe', qc, prev, xi)
    return (inner + cross).reshape(b, s, h, dv)

def short_conv(u, w, bias):
    s = u.shape[1]
    up = jnp.pad(u, ((0, 0), (CONV_K - 1, 0), (0, 0)))
    out = up[:, 0:s] * w[0]
    for tap in range(1, CONV_K):
        out = out + up[:, tap:tap + s] * w[tap]
    return out + bias

def even_layer(h, positions, w_in, conv_w, conv_b, gn, w_out):
    b, s, _ = h.shape
    q, k, v, g_ret, cb, cc, cx, g_conv = split_cols(h @ w_in, EVEN_SPLITS)
    q = rope(q.reshape(b, s, RET_HEADS, RET_DK), positions)
    k = rope(k.reshape(b, s, RET_HEADS, RET_DK), positions) * (RET_DK ** -0.5)
    v = v.reshape(b, s, RET_HEADS, RET_DV)
    r = retention(q, k, v)
    r = rms_norm_2(r, gn.reshape(RET_HEADS, RET_DV)).reshape(b, s, RET_V)
    y_conv = cb * short_conv(cc * cx, conv_w, conv_b)
    mix = jnp.concatenate([r * jax.nn.silu(g_ret), y_conv * jax.nn.silu(g_conv)], axis=-1)
    return mix @ w_out

def causal_mla_attention(q_nope, q_rope, k_nope, k_rope, v):
    s = q_nope.shape[1]
    scale = MLA_QK ** -0.5
    outs = []
    for blk in range(s // ATTN_BLOCK):
        lo, hi = blk * ATTN_BLOCK, (blk + 1) * ATTN_BLOCK
        sc = (jnp.einsum('bqhd,bkhd->bhqk', q_nope[:, lo:hi].astype(jnp.float32), k_nope[:, :hi].astype(jnp.float32))
              + jnp.einsum('bqhd,bkd->bhqk', q_rope[:, lo:hi].astype(jnp.float32), k_rope[:, :hi].astype(jnp.float32))) * scale
        qpos = lo + jnp.arange(ATTN_BLOCK)
        kpos = jnp.arange(hi)
        sc = jnp.where(kpos[None, :] <= qpos[:, None], sc, -jnp.inf)
        p = jax.nn.softmax(sc, axis=-1).astype(v.dtype)
        outs.append(jnp.einsum('bhqk,bkhd->bqhd', p, v[:, :hi]))
    return jnp.concatenate(outs, axis=1)

def odd_layer(h, positions, w_in, q_a_norm, w_qb, kv_a_norm, w_kvb, w_out):
    b, s, _ = h.shape
    cq, ckv, k_rope, gate = split_cols(h @ w_in, ODD_SPLITS)
    q = (rms_norm_2(cq, q_a_norm) @ w_qb).reshape(b, s, MLA_HEADS, MLA_QK)
    q_nope = q[..., :MLA_NOPE]
    q_rope = rope(q[..., MLA_NOPE:], positions)
    kv = (rms_norm_2(ckv, kv_a_norm) @ w_kvb).reshape(b, s, MLA_HEADS, MLA_NOPE + MLA_DV)
    k_nope, v = kv[..., :MLA_NOPE], kv[..., MLA_NOPE:]
    k_rope = rope(k_rope[:, :, None, :], positions)[:, :, 0]
    o = causal_mla_attention(q_nope, q_rope, k_nope, k_rope, v)
    return (o.reshape(b, s, MLA_V) * jax.nn.silu(gate)) @ w_out

def second_inputs(seed: int = 0) -> dict:
    key = jax.random.key(seed)
    ks = jax.random.split(key, 16)
    f32 = jnp.float32
    nrm = lambda k, shape, scale: jax.random.normal(k, shape, f32) * scale
    x = jax.random.normal(ks[0], (BATCH, SEQ, D_MODEL), f32)
    offsets = jax.random.randint(ks[1], (BATCH, 1), 0, 1024, dtype=jnp.int32)
    positions = (offsets + jnp.arange(SEQ, dtype=jnp.int32)[None, :]).astype(jnp.int32)
    pre_norm = 1.0 + nrm(ks[2], (DEPTH, D_MODEL), 0.02)
    post_norm = 1.0 + nrm(ks[3], (DEPTH, D_MODEL), 0.02)
    even_w_in = nrm(ks[4], (N_EVEN, D_MODEL, EVEN_IN), D_MODEL ** -0.5)
    even_conv_w = nrm(ks[5], (N_EVEN, CONV_K, CONV_W), CONV_K ** -0.5)
    even_conv_b = nrm(ks[6], (N_EVEN, CONV_W), 0.01)
    ret_gn = 1.0 + nrm(ks[7], (N_EVEN, RET_V), 0.02)
    even_w_out = nrm(ks[8], (N_EVEN, EVEN_MIX, D_MODEL), EVEN_MIX ** -0.5)
    odd_w_in = nrm(ks[9], (N_ODD, D_MODEL, ODD_IN), D_MODEL ** -0.5)
    q_a_norm = 1.0 + nrm(ks[10], (N_ODD, Q_LORA), 0.02)
    w_qb = nrm(ks[11], (N_ODD, Q_LORA, MLA_HEADS * MLA_QK), Q_LORA ** -0.5)
    kv_a_norm = 1.0 + nrm(ks[12], (N_ODD, KV_LORA), 0.02)
    w_kvb = nrm(ks[13], (N_ODD, KV_LORA, MLA_HEADS * (MLA_NOPE + MLA_DV)), KV_LORA ** -0.5)
    odd_w_out = nrm(ks[14], (N_ODD, MLA_V, D_MODEL), MLA_V ** -0.5)
    return {"x": x, "positions": positions, "pre_norm": pre_norm, "post_norm": post_norm,
            "even_w_in": even_w_in, "even_conv_w": even_conv_w, "even_conv_b": even_conv_b,
            "ret_gn": ret_gn, "even_w_out": even_w_out, "odd_w_in": odd_w_in,
            "q_a_norm": q_a_norm, "w_qb": w_qb, "kv_a_norm": kv_a_norm, "w_kvb": w_kvb,
            "odd_w_out": odd_w_out}

def second_block(x, positions, pre_norm, post_norm, even_w_in, even_conv_w, even_conv_b, ret_gn,
              even_w_out, odd_w_in, q_a_norm, w_qb, kv_a_norm, w_kvb, odd_w_out):
    h = x
    for layer in range(DEPTH):
        u = rms_norm_2(h, pre_norm[layer])
        if layer % 2 == 0:
            e = layer // 2
            y = even_layer(u, positions, even_w_in[e], even_conv_w[e], even_conv_b[e], ret_gn[e], even_w_out[e])
        else:
            o = layer // 2
            y = odd_layer(u, positions, odd_w_in[o], q_a_norm[o], w_qb[o], kv_a_norm[o], w_kvb[o], odd_w_out[o])
        h = h + rms_norm_2(y, post_norm[layer])
    return h


def setup_inputs(seed=0):
    out = dict(first_inputs(seed))
    for name, value in second_inputs(seed + 1).items():
        if name != "x":
            out[name + "_2"] = value
    return out


def reference(
    x, c, ctx, c_ctx, w_mod, b_mod, g_norm1, g_norm2, w_in, q_norm_g, k_norm_g, w_fourier,
    conv_dw_w, conv_dw_b, conv_ln_g, conv_ln_b, w_conv_pw, w_pool, pool_scale, w_out, w_ffn_in,
    w_ffn_out, positions_2, pre_norm_2, post_norm_2, even_w_in_2, even_conv_w_2, even_conv_b_2,
    ret_gn_2, even_w_out_2, odd_w_in_2, q_a_norm_2, w_qb_2, kv_a_norm_2, w_kvb_2, odd_w_out_2,
):
    x = first_block(
        x, c, ctx, c_ctx, w_mod, b_mod, g_norm1, g_norm2, w_in, q_norm_g, k_norm_g, w_fourier,
        conv_dw_w, conv_dw_b, conv_ln_g, conv_ln_b, w_conv_pw, w_pool, pool_scale, w_out,
        w_ffn_in, w_ffn_out,
    )
    return second_block(
        x, positions_2, pre_norm_2, post_norm_2, even_w_in_2, even_conv_w_2, even_conv_b_2,
        ret_gn_2, even_w_out_2, odd_w_in_2, q_a_norm_2, w_qb_2, kv_a_norm_2, w_kvb_2,
        odd_w_out_2,
    )


_drawn_inputs = setup_inputs


def setup_inputs(seed=0):
    import zlib

    import numpy as np

    out = dict(_drawn_inputs(seed))
    spreads = {}
    factors = {'g_norm1': 3.294,
     'q_norm_g': 8.0,
     'k_norm_g': 8.0,
     'conv_dw_b': 4.54,
     'conv_ln_g': 6.771,
     'conv_ln_b': 6.039,
     'pool_scale': 5.072,
     'post_norm_2': 3.716,
     'even_conv_b_2': 30.727,
     'ret_gn_2': 6.412,
     'q_a_norm_2': 8.0,
     'kv_a_norm_2': 4.925}
    for name, (base, spread) in spreads.items():
        noise = np.random.default_rng([zlib.crc32(name.encode()), seed]).standard_normal(out[name].shape)
        drawn = base * np.exp(spread * noise) if base else spread * noise
        out[name] = __import__('jax').numpy.asarray(drawn.astype(out[name].dtype))
    for name, factor in factors.items():
        out[name] = (out[name] * factor).astype(out[name].dtype)
    return out
```

```python
from contextlib import ExitStack

import numpy as np

import concourse.bass as bass
from concourse import mybir

F32 = mybir.dt.float32
F32R = mybir.dt.float32r
I32 = mybir.dt.int32
ALU = mybir.AluOpType
ACT = mybir.ActivationFunctionType
AX = mybir.AxisListType

P = 128
NX, NC = 512, 256
NT = NX + NC
DC = 8
FH = 11
EPS = 1e-6
RAW = 4
CONV = 31
HALO = CONV // 2
POOLPAD = 8
SEGS = [(0, NX), (NX, NC)]
GLU_AT = [HALO, NX + 3 * HALO]
GLU_W = NT + 4 * HALO
PP_AT = [POOLPAD, NX + 3 * POOLPAD]
PP_W = NT + 4 * POOLPAD



class Gemm:
    def __init__(self, name, kc, n, j0, at):
        self.name, self.kc, self.n, self.j0, self.at = name, kc, n, j0, at


def plan():
    gemms, used = [], {}
    j = 0
    for name, kc, n in (
        [x for l in range(2) for x in (
            (f"win{l}", 8, 13), (f"wout{l}", 8, 8),
            (f"fin{l}0", 8, 2 * FH), (f"fout{l}0", FH, 8),
            (f"fin{l}1", 8, 2 * FH), (f"fout{l}1", FH, 8))]
        + [("eqk", 8, 8), ("ev", 8, 8), ("eg", 8, 8), ("eout0", 8, 8), ("econv", 8, 32), ("eout1", 8, 8),
           ("oin", 8, 14), ("oq", 3, 12), ("ok", 2, 8), ("ov", 2, 8), ("oout", 8, 8)]
    ):
        gemms.append(Gemm(name, kc, n, j, used.get(kc, 0)))
        used[kc] = used.get(kc, 0) + n
        j += n
    return gemms


GEMMS = plan()
GEMM = {g.name: g for g in GEMMS}
NPANEL = sum(g.n for g in GEMMS)
KC_OF = [g.kc for g in GEMMS for _ in range(g.n)]

PAR = {}


def _par_layout():
    at = 0
    for l in range(2):
        for name, w in (("bmod", 96), ("g1", 8), ("g2", 8), ("qg", 1), ("kg", 1), ("dw", 2 * CONV), ("dwb", 2),
                        ("lng", 2), ("lnb", 2), ("psc", 2)):
            PAR[name + str(l)] = (at, w)
            at += w
    for name, w in (("pre", 16), ("post", 16), ("cw", 24), ("cb", 8), ("gn", 8), ("qa", 3), ("kva", 2), ("c", 16)):
        PAR[name] = (at, w)
        at += w
    return at


NPAR = _par_layout()

CON = {}


def _con_layout():
    at = 0
    for name, w in (("ident", 128), ("ones", 128), ("blk", 128), ("perm1", 128), ("perm2", 128), ("mask", 128),
                    ("invw", 2), ("edge", 32), ("inv", 1), ("eps", 1)):
        CON[name] = (at, w)
        at += w
    return at


NCON = _con_layout()


def wait(eng, sem, value):
    if isinstance(value, int) and value <= 0:
        return
    eng.wait_ge(sem, value)


def build_program(nc, d):
    stack = ExitStack()
    with stack:
        base = nc.sbuf_base
        top = [(base + 63) // 64 * 64]

        def at(name, shape, dt, offset):
            return nc.alloc_sbuf_tensor_at(name, [P, shape], dt, offset=offset)

        def sb(name, width, dt=F32):
            t = at(name, width, dt, top[0])
            top[0] += (width * 4 + 63) // 64 * 64
            return t

        Xf = sb("resid", DC * NT)
        X = Xf[:, :].rearrange("p (c t) -> p c t", c=DC)
        xhi_t, xlo_t = sb("operand_hi", DC * NT, F32R), sb("operand_lo", DC * NT, F32R)
        XH = xhi_t[:, :].rearrange("p (c t) -> p c t", c=DC)
        XL = xlo_t[:, :].rearrange("p (c t) -> p c t", c=DC)
        raw = [sb(f"raw{s}", FH * P) for s in range(RAW)]
        whi = [sb(f"whi{s}", FH * P, F32R) for s in range(2)]
        wlo = [sb(f"wlo{s}", FH * P, F32R) for s in range(2)]
        mraw = [sb(f"modraw{s}", DC * P) for s in range(2)]
        par = sb("par", NPAR)
        con = sb("con", NCON)
        cosT, sinT = sb("cosT", NX), sb("sinT", NX)
        modT = sb("modT", 96)
        afac = sb("afac", 32)
        sc = sb("silu_c", 16)
        stat = sb("stat", 24)
        region = top[0]

        def pa(name):
            a, w = PAR[name]
            return par[:, a:a + w]

        def co(name):
            a, w = CON[name]
            return con[:, a:a + w]

        ident, ones, blk = co("ident"), co("ones"), co("blk")

        def phase():
            top[0] = region

        phase()
        projf = sb("proj", 6 * NT)
        PR = projf[:, :].rearrange("p (c t) -> p c t", c=6)
        vtok = sb("vtok", NT)
        gluf = sb("glu", 2 * GLU_W)
        glu = gluf[:, :].rearrange("p (c t) -> p c t", c=2)
        accf = sb("conv_acc", 2 * NT)
        acc = accf[:, :].rearrange("p (c t) -> p c t", c=2)
        ppf = sb("pool_in", 2 * PP_W)
        pp = ppf[:, :].rearrange("p (c t) -> p c t", c=2)
        pA = sb("pool_a", PP_W)
        smallw = sb("smallw", 1536)
        dftd = smallw[:, 1280:1536]
        wf = smallw[:, 0:512].rearrange("p (k m) -> p k m", k=2)
        wpw = smallw[:, 512:1024].rearrange("p (k m) -> p k m", k=2)
        wpl = smallw[:, 1024:1280].rearrange("p (k m) -> p k m", k=2)
        zone = top[0] = max(top[0], region + 24 * NX * 4)
        W = [sb(f"work{s}", NT) for s in range(8)]
        endA = top[0]
        pB = at("pool_b", PP_W, F32, zone + 5120 * 4)
        ftok = at("fourier_tok", 6 * 512, F32, zone)
        dft = [at(f"dft{s}", 1024, F32, zone + (3072 + 1024 * s) * 4) for s in range(2)]

        phase()
        hhi_t, hlo_t = sb("hidden_hi", FH * NT, F32R), sb("hidden_lo", FH * NT, F32R)
        HH = hhi_t[:, :].rearrange("p (c t) -> p c t", c=FH)
        HL = hlo_t[:, :].rearrange("p (c t) -> p c t", c=FH)
        fsilu, fh = sb("ffn_silu", NT), sb("ffn_h", NT)
        endB = top[0]

        phase()
        QK = sb("ret_qk", 8 * NX)[:, :].rearrange("p (c t) -> p c t", c=8)
        VE = sb("ret_v", 4 * 1024)[:, :].rearrange("p (b f) -> p b f", b=4)
        RT = sb("ret_r", 8 * NX)[:, :].rearrange("p (c t) -> p c t", c=8)
        MH = at("mix_hi", 8 * NX, F32R, region)[:, :].rearrange("p (c t) -> p c t", c=8)
        ML = at("mix_lo", 8 * NX, F32R, region + 8 * NX * 4)[:, :].rearrange("p (c t) -> p c t", c=8)
        Y = at("layer_y", 8 * NX, F32, region + 16 * NX * 4)[:, :].rearrange("p (c t) -> p c t", c=8)
        assert zone >= top[0]
        decay = [at(f"decay{s}", NX, F32, zone + s * NX * 4) for s in range(2)]
        scT = [at(f"scoresT{s}", 1280, F32, zone + (2 * NX + 1280 * s) * 4) for s in range(2)]
        ce_c, ce_u, ce_y, ce_s, ce_z = (at(n, NX + 2, F32, zone + i * 2112) for i, n in enumerate(("ce_c", "ce_u", "ce_y", "ce_s", "ce_z")))

        phase()
        QN = sb("q_nope", 8 * NX)[:, :].rearrange("p (c t) -> p c t", c=8)
        KN = sb("k_nope", 8 * NX)[:, :].rearrange("p (c t) -> p c t", c=8)
        VO = sb("v_lat", 4 * 1024)[:, :].rearrange("p (b f) -> p b f", b=4)
        SG = sb("silu_gate", 8 * NX)[:, :].rearrange("p (c t) -> p c t", c=8)
        QR = X[:, :, NX:NT]
        kr = sb("k_rope", NX)
        dprobs = [sb(f"dprobs{s}", NX) for s in range(2)]
        dprobsT = [sb(f"dprobsT{s}", NX) for s in range(2)]
        LAT = at("latent", 5 * NX, F32, region + 8 * NX * 4)[:, :].rearrange("p (c t) -> p c t", c=5)
        WL = [at(f"work_latent{s}", NX, F32, region + s * NX * 4) for s in range(8)]
        WY = [at(f"work_out{s}", NX, F32, region + (8 + s) * NX * 4) for s in range(8)]
        Y2 = at("layer_y2", 8 * NX, F32, region)[:, :].rearrange("p (c t) -> p c t", c=8)
        endD = top[0]

        def ps(name, width):
            return stack.enter_context(nc.psum_tensor(name, [P, width], F32))
        G = [ps("prod0", 1024), ps("prod1", 1024)]
        M0, M1, MM = ps("misc0", 1024), ps("misc1", 512), ps("misc2", 512)

        def sem(name):
            return stack.enter_context(nc.semaphore(name))

        raw_landed = [sem(f"raw_landed{s}") for s in range(RAW)]
        hi_ready, lo_ready = sem("hi_ready"), sem("lo_ready")
        panel_done = sem("panel_done")
        bank_free = [sem("bank_free0"), sem("bank_free1")]
        mod_landed = [sem("mod_landed0"), sem("mod_landed1")]
        mod_used, mod_ready, c_ready = sem("mod_used"), sem("mod_ready"), sem("c_ready")
        par_landed, x_landed, small_landed = sem("par_landed"), sem("x_landed"), sem("small_landed")
        rope_landed, out_landed = sem("rope_landed"), sem("out_landed")
        sq_ready, sq_used, sd_ready, rs_ready = sem("sq_ready"), sem("sq_used"), sem("sd_ready"), sem("rs_ready")
        t_ready, y_ready = sem("t_ready"), sem("y_ready")
        operand_hi, operand_lo = sem("operand_hi"), sem("operand_lo")
        resid_ready = sem("resid_ready")
        conv_tick, dve_step, act_step = sem("conv_tick"), sem("dve_step"), sem("act_step")
        ft_ready, ft_copied, dft_landed, dft_used, fy_copied = (
            sem("ft_ready"), sem("ft_copied"), [sem("dft_landed0"), sem("dft_landed1")], sem("dft_used"), sem("fy_copied"))
        mp_ready = sem("mp_ready")
        qk_normed, rot_ready, rope_done = sem("qk_normed"), sem("rot_ready"), sem("rope_done")
        scores_ready, negmax_ready, exp_done = sem("scores_ready"), sem("negmax_ready"), sem("exp_done")
        probs_ready, probsT_ready, probsT_copied, pv_done = (
            sem("probs_ready"), sem("probsT_ready"), sem("probsT_copied"), sem("pv_done"))
        gated = sem("gated")
        ln_sum, ln_centered, ln_scaled, ln_act, pool_ready = (
            sem("ln_sum"), sem("ln_centered"), sem("ln_scaled"), sem("ln_act"), sem("pool_ready"))
        h_hi, h_lo = sem("h_hi"), sem("h_lo")
        decay_landed, ret_scores, ret_masked, ret_pv, ret_copied, ret_normed = (
            [sem("decay_landed0"), sem("decay_landed1")], sem("ret_scores"), sem("ret_masked"), sem("ret_pv"), sem("ret_copied"), sem("ret_normed"))
        ce_tick, trig = sem("ce_tick"), sem("trig")


        def where(g, i, u):
            jj = g.j0 + u
            return jj + 4 * i, jj % 2, jj // 2 + 2 * i, jj % RAW, jj // RAW + i

        def each_panel(eng, g, body):
            full = (g.n - 2) // 4 if g.n > 16 else 1
            for u in range(min(4, g.n)):
                body(0, u)
            if full > 1:
                with eng.Fori(1, full) as i:
                    for u in range(4):
                        body(i, u)
            for p in range(4 * full, g.n):
                body(p // 4, p % 4)

        def freed(eng, j):
            wait(eng, bank_free[j % 2], j // 2 + 1)

        def last(name):
            return GEMM[name].j0 + GEMM[name].n - 1

        def tok(l):
            return (NT, SEGS) if l == 0 else (NX, SEGS[:1])

        def win_width(l, p):
            return NT if l == 0 or p >= 10 else NX

        def units1(l):
            out = [(h, 128 * b, 0, NT) for h in range(4) for b in range(4)]
            if l == 0:
                out += [(h, NX + 128 * b, NX, NC) for h in range(4) for b in range(2)]
            return out

        def head_ends(units):
            ends, start = {}, 0
            for n, u in enumerate(units):
                if n + 1 == len(units) or units[n + 1][0] != u[0]:
                    ends[n] = (u[0], units[start][1], u[1] + 128 - units[start][1])
                    start = n + 1
            return ends

        units2 = [(h, 128 * b, 0, 128 * (b + 1)) for h in range(8) for b in range(4)]
        RET_AT = [(0, 0, 512), (1, 512, 384), (3, 896, 128), (2, 1024, 256)]

        block = stack.enter_context(nc.Block())

        @block.sync
        def _(sp):
            sp.dma_start(par[:, :], d["par"]).then_inc(par_landed, 16)
            sp.dma_start(con[:, :], d["con"]).then_inc(par_landed, 16)
            sp.dma_start(X[:, :, :], d["xt"]).then_inc(x_landed, 16)

            def mod_panel(l, m, parity):
                wait(sp, mod_used, 48 * l + m - 1)
                sp.dma_start(mraw[parity][:, :], d["wmod"][48 * l + m]).then_inc(mod_landed[parity], 16)

            def panels(name, mod=None):
                g = GEMM[name]

                def body(i, u):
                    j, _, _, slot, _ = where(g, i, u)
                    wait(sp, lo_ready, j - RAW + 1)
                    sp.dma_start(raw[slot][:, 0:g.kc * P], d[f"w{g.kc}"][g.at + 4 * i + u]).then_inc(raw_landed[slot], 16)
                    if mod is not None:
                        mod_panel(1, mod + 4 * i + u, (mod + u) % 2)

                each_panel(sp, g, body)

            for m in range(2):
                mod_panel(0, m, m % 2)
            with sp.Fori(1, 24) as i:
                for u in range(2):
                    mod_panel(0, 2 * i + u, u)
            for l in range(2):
                panels(f"win{l}")
                panels(f"wout{l}")
                panels(f"fin{l}0", 0 if l == 0 else None)
                panels(f"fout{l}0")
                panels(f"fin{l}1", 2 * FH if l == 0 else None)
                if l == 0:
                    for m in range(4 * FH, 48):
                        mod_panel(1, m, m % 2)
                panels(f"fout{l}1")
            for g in GEMMS[12:]:
                panels(g.name)
            for c in range(DC):
                sp.wait_ge(resid_ready, DC + c + 1)
                sp.dma_start(d["out"][:, c, :], X[:, c, 0:NX]).then_inc(out_landed, 16)
            sp.wait_ge(out_landed, 16 * DC)

        @block.gpsimd
        def _(pool):
            for g in GEMMS:
                def body(i, u, g=g):
                    j, b, _, slot, _ = where(g, i, u)
                    w = g.kc * P
                    pool.wait_ge(hi_ready, j + 1)
                    nc.gpsimd.tensor_tensor(wlo[b][:, 0:w], raw[slot][:, 0:w], whi[b][:, 0:w].bitcast(F32),
                                            ALU.subtract).then_inc(lo_ready, 1)
                each_panel(pool, g, body)

        @block.tensor
        def _(pe):
            n = dict(sq=0, inst=0, op=0, mp=0, rope=0, unit=0, ln=0, ret=0)

            xh, xl = (lambda k: XH[:, k, :]), (lambda k: XL[:, k, :])

            def big(name, xh, xl, width, swap=False, ready=0, mod=None):
                g = GEMM[name]

                def body(i, u):
                    j, b, used, _, _ = where(g, i, u)
                    p = 4 * i + u
                    pe.wait_ge(lo_ready, j + 1)
                    wait(pe, bank_free[b], used)
                    first = isinstance(p, int) and p == 0
                    tw = width(p) if callable(width) else width
                    if swap(p) if callable(swap) else swap:
                        if first:
                            wait(pe, operand_lo, ready)
                        for t in range(tw // P):
                            cols = slice(t * P, (t + 1) * P)
                            for k in range(g.kc):
                                for q, (a, w) in enumerate(((xh(k), whi), (xl(k), whi), (xh(k), wlo))):
                                    mm = pe.matmul(G[b][:, cols], a[:, cols], w[b][:, k * P:(k + 1) * P],
                                                   start=(k == 0 and q == 0), stop=(k == g.kc - 1 and q == 2))
                    else:
                        segs = [s for s in SEGS if s[0] < tw]
                        for k in range(g.kc):
                            if first:
                                wait(pe, operand_lo, ready - g.kc + k + 1)
                            for q, (w, a) in enumerate(((whi, xh(k)), (whi, xl(k)), (wlo, xh(k)))):
                                for t0, tn in segs:
                                    mm = pe.matmul(G[b][:, t0:t0 + tn], w[b][:, k * P:(k + 1) * P], a[:, t0:t0 + tn],
                                                   start=(k == 0 and q == 0), stop=(k == g.kc - 1 and q == 2))
                    mm.then_inc(panel_done, 1)
                    if mod is not None:
                        mod_panel(1, mod + 4 * i + u, (mod + u) % 2, (mod + u) // 2 + 2 * i)

                each_panel(pe, g, body)

            def mod_panel(l, m, parity, pair):
                pe.wait_ge(mod_landed[parity], 16 * (24 * l + pair + 1))
                for k in range(DC):
                    mm = pe.matmul(MM[:, bass.ds(96 * l + 2 * m, 2)], mraw[parity][:, k * P:(k + 1) * P],
                                   sc[:, 2 * k:2 * k + 2], start=(k == 0), stop=(k == DC - 1))
                mm.then_inc(mod_used, 1)

            def rms(nchunks, width, sq_tiles, weights):
                wait(pe, sd_ready, n["inst"])
                for c in range(nchunks):
                    pe.wait_ge(sq_ready, n["sq"] + 1)
                    for t0, tn in [s for s in SEGS if s[0] < width]:
                        mm = pe.matmul(M0[:, t0:t0 + tn], weights, sq_tiles[n["sq"] % 2][:, t0:t0 + tn],
                                       start=(c == 0), stop=(c == nchunks - 1))
                    mm.then_inc(sq_used, 1)
                    n["sq"] += 1
                n["inst"] += 1

            def small_product(weights, source, segs, kc, m):
                wait(pe, operand_lo, n["op"])
                for k in range(kc):
                    for s, (t0, tn) in enumerate(segs):
                        mm = pe.matmul(M0[:, t0:t0 + tn], weights(k, m), source(k, s), start=(k == 0), stop=(k == kc - 1))
                mm.then_inc(mp_ready, 1)
                n["op"] += 1

            def rotate(chunk, perm):
                wait(pe, rope_done, n["rope"])
                o = M1[:, 0:NX] if len(chunk.shape) == 2 else M1[:, 0:NX].rearrange("p (a t) -> p a t", a=2)
                pe.matmul(o, perm, chunk, start=True, stop=True).then_inc(rot_ready, 1)
                n["rope"] += 1

            def attention(units, score, value, out, keys_tiles, ops_free):
                ends = head_ends(units)
                base = n["unit"]

                def scores(i):
                    wait(pe, exp_done, base + i - 1 if i >= 2 else base)
                    for mm in score(units[i], G[i % 2]):
                        pass
                    mm.then_inc(scores_ready, 1)

                def turn(i):
                    pe.wait_ge(probs_ready, base + i + 1)
                    wait(pe, probsT_copied, base + i)
                    for kb in range(units[i][3] // P):
                        mm = pe.transpose(M0[:, kb * P:(kb + 1) * P], keys_tiles[0][i % 2][:, kb * P:(kb + 1) * P], ident)
                    mm.then_inc(probsT_ready, 1)

                def weigh(i):
                    h, q0, k0, nk = units[i]
                    pe.wait_ge(probsT_copied, base + i + 1)
                    first = i == 0 or units[i - 1][0] != h
                    if first:
                        done = sum(1 for e in ends if e < i)
                        wait(pe, operand_lo, n["op"] + done - ops_free + 1)
                    o = out(h, q0)
                    for kb in range(nk // P):
                        mm = pe.matmul(o, value(h, k0 // P + kb), keys_tiles[1][i % 2][:, kb * P:(kb + 1) * P],
                                       start=(kb == 0), stop=(kb == nk // P - 1))
                    mm.then_inc(pv_done, 1)

                scores(0)
                for i in range(len(units)):
                    if i + 1 < len(units):
                        scores(i + 1)
                    turn(i)
                    if i >= 1:
                        weigh(i - 1)
                weigh(len(units) - 1)
                n["unit"] += len(units)
                n["op"] += len(ends)

            pe.wait_ge(c_ready, 1)
            for m in range(2):
                mod_panel(0, m, m, 0)
            with pe.Fori(1, 24) as i:
                for u in range(2):
                    mod_panel(0, 2 * i + u, u, i)

            for l in range(2):
                width, segs = tok(l)
                rms(DC, NT, W, ones)
                n["op"] += DC
                big(f"win{l}", xh, xl, lambda p, l=l: win_width(l, p), swap=lambda p: p == 12, ready=n["op"])
                g = GEMM[f"win{l}"]

                freed(pe, g.j0 + 7)
                pe.wait_ge(small_landed, 16 * (l + 1))
                wait(pe, sd_ready, n["inst"])
                nb = width // P
                fb = 6 * l
                for tb in range(nb):
                    wait(pe, ft_copied, fb + tb - 1)
                    for c in range(2):
                        mm = pe.matmul(M0[:, 512 * (tb % 2) + 256 * c:512 * (tb % 2) + 256 * c + 256],
                                       PR[:, c, tb * P:(tb + 1) * P], dftd, start=True, stop=True)
                    mm.then_inc(ft_ready, 1)
                freed(pe, g.j0 + g.n - 1)
                freed(pe, g.j0 + g.n - 2)
                for tb in range(nb):
                    pe.wait_ge(ft_copied, fb + tb + 1)
                    pe.wait_ge(dft_landed[tb % 2], 16 * ((fb + tb) // 2 + 1))
                    t0, tn = SEGS[tb // 4]
                    lastb = tb == 3 or tb == 5
                    for c in range(2):
                        for q in range(2):
                            mm = pe.matmul(G[c][:, t0:t0 + tn], ftok[:, tb * 512 + c * 256 + q * P:tb * 512 + c * 256 + (q + 1) * P],
                                           dft[tb % 2][:, q * tn:(q + 1) * tn], start=(tb in (0, 4) and q == 0),
                                           stop=(lastb and q == 1))
                    mm.then_inc(dft_used, 1)
                pe.wait_ge(fy_copied, 2 * (l + 1))
                for m in range(2):
                    small_product(lambda k, m: wf[:, k, m * P:(m + 1) * P], lambda k, s: PR[:, k, segs[s][0]:segs[s][0] + segs[s][1]],
                                  segs, 2, m)
                wait(pe, operand_lo, n["op"])

                for c in range(2, 6):
                    freed(pe, g.j0 + 6 + c)
                    rms(1, NT if l == 0 or c >= 4 else NX, W, blk)
                    pe.wait_ge(qk_normed, 4 * l + c - 1)
                    rotate(PR[:, c, 0:NX], co("perm1"))
                pe.wait_ge(rope_done, n["rope"])

                def score1(unit, o):
                    h, q0, k0, nk = unit
                    part = slice(64 * (h % 2), 64 * (h % 2) + 64)
                    for c0 in range(0, nk, NX):
                        cn = min(NX, nk - c0)
                        yield pe.matmul(o[:, c0:c0 + cn], PR[part, 2 + h // 2, q0:q0 + P],
                                        PR[part, 4 + h // 2, k0 + c0:k0 + c0 + cn], start=True, stop=True)

                attention(units1(l), score1,
                          lambda h, kb: vtok[:, kb * P + 64 * (h // 2):kb * P + 64 * (h // 2) + 64],
                          lambda h, q0: M1[64 * (h % 2):64 * (h % 2) + 64, q0 % NX:q0 % NX + P],
                          (W[0:2], W[2:4]), 2)
                wait(pe, operand_lo, n["op"])

                pe.wait_ge(conv_tick, CONV * (2 * len(segs)) + (CONV * 4 if l else 0))
                for c in range(2):
                    for t0, tn in segs:
                        mm = pe.matmul(M0[:, t0:t0 + tn], ones, acc[:, c, t0:t0 + tn], start=(c == 0), stop=(c == 1))
                mm.then_inc(ln_sum, 1)
                rms(2, width, W, ones)
                pe.wait_ge(ln_act, 2 * (l + 1))
                for m in range(2):
                    small_product(lambda k, m: wpw[:, k, m * P:(m + 1) * P], lambda k, s: acc[:, k, segs[s][0]:segs[s][0] + segs[s][1]],
                                  segs, 2, m)
                pe.wait_ge(pool_ready, 2 * (l + 1))
                for m in range(2):
                    small_product(lambda k, m: wpl[:, m, :], lambda k, s: pp[:, m, PP_AT[s]:PP_AT[s] + segs[s][1]], segs, 1, m)

                big(f"wout{l}", xh, xl, width, ready=n["op"])
                rms(DC, width, W, ones)
                n["op"] += DC
                for half in range(2):
                    big(f"fin{l}{half}", xh, xl, width, ready=n["op"],
                        mod=2 * FH * half if l == 0 else None)
                    if l == 0 and half == 1:
                        for m in range(4 * FH, 48):
                            mod_panel(1, m, m % 2, m // 2)
                    pe.wait_ge(h_lo, FH * (2 * l + half + 1))
                    big(f"fout{l}{half}", lambda k: HH[:, k, :], lambda k: HL[:, k, :], width, ready=n["op"])

            rms(DC, NX, W, ones)
            n["op"] += DC
            big("eqk", xh, xl, NX, ready=n["op"])
            big("ev", xh, xl, NX, swap=True, ready=n["op"])
            for c in range(8):
                rotate(QK[:, c, :], co("perm2"))
            freed(pe, last("ev"))
            freed(pe, last("ev") - 1)
            pe.wait_ge(rope_done, n["rope"])

            def ret_score(h):
                part = slice(64 * (h % 2), 64 * (h % 2) + 64)
                wait(pe, ret_masked, h - 1)
                for jb, c0, cn in RET_AT:
                    o = G[h % 2][:, c0:c0 + cn] if c0 < 1024 else M0[:, 512 * (h % 2):512 * (h % 2) + cn]
                    mm = pe.matmul(o, QK[part, 4 + h // 2, jb * P:(jb + 1) * P], QK[part, h // 2, jb * P:NX],
                                   start=True, stop=True)
                mm.then_inc(ret_scores, 1)

            ret_score(0)
            for h in range(8):
                if h < 7:
                    ret_score(h + 1)
                pe.wait_ge(ret_masked, h + 1)
                wait(pe, ret_copied, h - 1)
                o = (M1, MM)[h % 2]
                for q, (jb, c0, cn) in enumerate(RET_AT):
                    mm = pe.matmul(o[:, jb * P:NX], VE[:, jb, h * P:(h + 1) * P], scT[h % 2][:, c0:c0 + cn],
                                   start=(q == 0), stop=(q == 3))
                mm.then_inc(ret_pv, 1)
            for h in range(8):
                rms(1, NX, W, ones)
            big("eg", xh, xl, NX, ready=n["op"])
            n["op"] += 8
            big("eout0", lambda k: MH[:, k, :], lambda k: ML[:, k, :], NX, ready=n["op"])
            big("econv", xh, xl, NX, ready=n["op"])
            n["op"] += 8
            big("eout1", lambda k: MH[:, k, :], lambda k: ML[:, k, :], NX, ready=n["op"])
            rms(DC, NX, W, ones)

            rms(DC, NX, W, ones)
            n["op"] += DC
            big("oin", xh, xl, NX, ready=n["op"])
            freed(pe, GEMM["oin"].j0 + 5)
            rms(3, NX, WL, ones)
            rms(2, NX, WL, ones)
            n["op"] += 5
            rotate(kr[:, 0:NX], co("perm2"))
            big("oq", xh, xl, NX, ready=n["op"] - 2)
            for c in range(4):
                freed(pe, GEMM["oq"].j0 + 8 + c)
                rotate(QR[:, 2 * c:2 * c + 2, :], co("perm2"))
            big("ok", lambda k: XH[:, 3 + k, :], lambda k: XL[:, 3 + k, :], NX, ready=n["op"])
            big("ov", lambda k: XH[:, 3 + k, :], lambda k: XL[:, 3 + k, :], NX, swap=True, ready=n["op"])
            freed(pe, last("ov"))
            freed(pe, last("ov") - 1)
            pe.wait_ge(rope_done, n["rope"])

            def score2(unit, o):
                h, q0, _, nk = unit
                part = slice(64 * (h % 2), 64 * (h % 2) + 64)
                yield pe.matmul(o[:, 0:nk], QN[:, h, q0:q0 + P], KN[:, h, 0:nk], start=True, stop=False)
                piece = QR[part, 2 * (h // 2) + q0 // 256, q0 % 256:q0 % 256 + P]
                yield pe.matmul(o[:, 0:nk], piece, kr[part, 0:nk], start=False, stop=True)

            attention(units2, score2, lambda h, kb: VO[:, kb, h * P:(h + 1) * P],
                      lambda h, q0: (M1, MM)[h % 2][:, q0:q0 + P], (dprobs, dprobsT), 2)
            big("oout", xh, xl, NX, ready=n["op"])
            rms(DC, NX, WY, ones)

        @block.scalar
        def _(act):
            n = dict(sq=0, inst=0, op=0, mp=0, t=0, y=0, unit=0)
            eps = co("eps")

            def high(j_static, rnd):
                if j_static >= NPANEL:
                    return
                w = KC_OF[j_static] * P
                act.wait_ge(raw_landed[j_static % RAW], 16 * (rnd + 1))
                nc.scalar.activation(whi[j_static % 2][:, 0:w], raw[j_static % RAW][:, 0:w], ACT.Copy).then_inc(hi_ready, 1)

            def stage(name, evac=None, after=None):
                g = GEMM[name]

                def body(i, u):
                    j, b, _, _, _ = where(g, i, u)
                    act.wait_ge(panel_done, j + 1)
                    if evac is not None:
                        evac(i, u, G[b], bank_free[b])
                    js = g.j0 + u + (4 * i if isinstance(i, int) else 4)
                    high(js + 2, (g.j0 + u + 2) // RAW + i)
                    if after is not None:
                        after(i, u)

                each_panel(act, g, body)

            def rms(sources, width, Wt, ready):
                for c, src in enumerate(sources):
                    ready(c)
                    wait(act, sq_used, n["sq"] - 1)
                    nc.scalar.activation(Wt[n["sq"] % 2][:, 0:width], src, ACT.Square).then_inc(sq_ready, 1)
                    n["sq"] += 1

            def root(width, Wt, dim):
                act.wait_ge(sq_used, n["sq"])
                wait(act, rs_ready, n["inst"])
                nc.scalar.activation(Wt[2 + n["inst"] % 2][:, 0:width], M0[:, 0:width], ACT.Sqrt, bias=eps,
                                     scale=1.0 / dim).then_inc(sd_ready, 1)
                n["inst"] += 1

            def high_operand(dst, src, scale=None):
                if scale is None:
                    nc.scalar.activation(dst, src, ACT.Copy).then_inc(operand_hi, 1)
                else:
                    nc.scalar.activation(dst, src, ACT.Copy, scale=scale).then_inc(operand_hi, 1)
                n["op"] += 1

            def norm_mod(l, which, width, ready):
                rms([X[:, c, 0:width] for c in range(DC)], width, W, ready)
                act.wait_ge(mod_ready, l + 1)
                root(width, W, 1024)
                for c in range(DC):
                    act.wait_ge(t_ready, n["t"] + 1)
                    wait(act, operand_lo, n["op"] - 1)
                    y = W[6 + c % 2]
                    for s, (t0, tn) in enumerate([s for s in SEGS if s[0] < width]):
                        a = 16 * which + 8 * s + c
                        m = 2 * ((24 if which else 0) + c) + s
                        ins = nc.scalar.activation(y[:, t0:t0 + tn], W[4 + c % 2][:, t0:t0 + tn], ACT.Identity,
                                                   scale=afac[:, a:a + 1], bias=modT[:, m:m + 1])
                    ins.then_inc(y_ready, 1)
                    n["t"] += 1
                    n["y"] += 1
                    act.wait_ge(y_ready, n["y"])
                    high_operand(XH[:, c, 0:width], y[:, 0:width])

            def norm_plain(sources, dim, Wt, ready, dst):
                rms(sources, NX, Wt, ready)
                root(NX, Wt, dim)
                for c in range(len(sources)):
                    act.wait_ge(t_ready, n["t"] + 1)
                    n["t"] += 1
                    high_operand(XH[:, dst + c, 0:NX], Wt[6 + c % 2][:, 0:NX])

            def mix_out(dst, width, scale=None):
                act.wait_ge(mp_ready, n["mp"] + 1)
                n["mp"] += 1
                high_operand(dst[:, 0:width], M0[:, 0:width], scale)

            def attention(units, scale, tiles, finish):
                ends = head_ends(units)
                base = n["unit"]

                def exps(i):
                    nk = units[i][3]
                    act.wait_ge(negmax_ready, base + i + 1)
                    wait(act, probsT_ready, base + i - 1 if i >= 2 else base)
                    s = (base + i) % 4
                    nc.scalar.activation(tiles[0][i % 2][:, 0:nk], G[i % 2][:, 0:nk], ACT.Exp, bias=stat[:, 4 + s:5 + s],
                                         scale=scale, accum_out=stat[:, 8 + s:9 + s]).then_inc(exp_done, 1)

                def copies(i):
                    nk = units[i][3]
                    act.wait_ge(probsT_ready, base + i + 1)
                    wait(act, pv_done, base + i - 1 if i >= 2 else base)
                    nc.scalar.activation(tiles[1][i % 2][:, 0:nk], M0[:, 0:nk], ACT.Copy).then_inc(probsT_copied, 1)

                def end(i):
                    if i in ends:
                        act.wait_ge(pv_done, base + i + 1)
                        finish(*ends[i])

                exps(0)
                for i in range(len(units)):
                    if i + 1 < len(units):
                        exps(i + 1)
                    copies(i)
                    if i >= 1:
                        end(i - 1)
                end(len(units) - 1)
                n["unit"] += len(units)

            act.dma_start(cosT[:, :], d["cosx"]).then_inc(rope_landed, 16)
            act.dma_start(sinT[:, :], d["sinx"]).then_inc(rope_landed, 16)
            act.wait_ge(par_landed, 32)
            nc.scalar.activation(sc[:, 0:16], pa("c"), ACT.Silu).then_inc(c_ready, 1)
            high(0, 0)
            high(1, 0)
            act.wait_ge(x_landed, 16)

            for l in range(2):
                width, segs = tok(l)
                nseg = len(segs)

                def whole(c, l=l):
                    if l == 1 and c == 0:
                        freed(act, last("fout01"))
                        freed(act, last("fout01") - 1)
                norm_mod(l, 0, NT, whole)
                act.dma_start(smallw[:, :], d["small"][l]).then_inc(small_landed, 16)

                def win_out(i, u, src, free, l=l, segs=segs):
                    p = 4 * i + u
                    tw = win_width(l, p)
                    if p in (0, 2):
                        if p == 2:
                            freed(act, GEMM[f"win{l}"].j0 + 1)
                        ins = nc.scalar.activation(pA[:, 0:tw], src[:, 0:tw], ACT.Sigmoid)
                    elif p in (1, 3):
                        return
                    elif p in (4, 5):
                        for s, (t0, tn) in enumerate(segs):
                            ins = nc.scalar.activation(pp[:, p - 4, PP_AT[s]:PP_AT[s] + tn], src[:, t0:t0 + tn], ACT.Copy)
                    elif p < 12:
                        ins = nc.scalar.activation(PR[:, p - 6, 0:tw], src[:, 0:tw], ACT.Copy)
                    else:
                        ins = nc.scalar.activation(vtok[:, 0:tw], src[:, 0:tw], ACT.Copy)
                    ins.then_inc(free, 1)

                stage(f"win{l}", win_out)

                nb, fb = width // P, 6 * l
                for tb in range(2):
                    act.dma_start(dft[tb][:, 0:1024], d["dftx"][tb]).then_inc(dft_landed[tb % 2], 16)
                for tb in range(nb):
                    act.wait_ge(ft_ready, fb + tb + 1)
                    nc.scalar.activation(ftok[:, tb * 512:(tb + 1) * 512], M0[:, 512 * (tb % 2):512 * (tb % 2) + 512],
                                         ACT.Copy).then_inc(ft_copied, 1)
                for tb in range(2, nb):
                    act.wait_ge(dft_used, fb + tb - 1)
                    if tb < 4:
                        act.dma_start(dft[tb % 2][:, 0:1024], d["dftx"][tb]).then_inc(dft_landed[tb % 2], 16)
                    else:
                        act.dma_start(dft[tb % 2][:, 0:512], d["dftc"][tb - 4]).then_inc(dft_landed[tb % 2], 16)
                act.wait_ge(dft_used, fb + nb)
                for c in range(2):
                    nc.scalar.activation(PR[:, c, 0:width], G[c][:, 0:width], ACT.Copy).then_inc(fy_copied, 1)
                for m in range(2):
                    mix_out(XH[:, 2 + m, :], width)

                for c in range(2, 6):
                    tw = NT if l == 0 or c >= 4 else NX
                    rms([PR[:, c, 0:tw]], tw, W, lambda _, c=c: freed(act, GEMM[f"win{l}"].j0 + 6 + c))
                    root(tw, W, 64)

                def finish1(h, q0, qn):
                    part = slice(64 * (h % 2), 64 * (h % 2) + 64)
                    high_operand(XH[part, h // 2, q0:q0 + qn], M1[part, 0:qn])

                attention(units1(l), 0.125, (W[0:2], W[2:4]), finish1)

                act.wait_ge(ln_centered, l + 1)
                rms([acc[:, c, 0:width] for c in range(2)], width, W, lambda c: None)
                root(width, W, 256)
                for c in range(2):
                    act.wait_ge(ln_scaled, 2 * l + c + 1)
                    nc.scalar.activation(acc[:, c, 0:width], acc[:, c, 0:width], ACT.Silu, scale=pa(f"lng{l}")[:, c:c + 1],
                                         bias=pa(f"lnb{l}")[:, c:c + 1]).then_inc(ln_act, 1)
                for m in range(2):
                    mix_out(XH[:, 4 + m, :], width)
                for m in range(2):
                    mix_out(XH[:, 6 + m, :], width, pa(f"psc{l}")[:, m:m + 1])

                stage(f"wout{l}")
                norm_mod(l, 1, width, lambda c, l=l: freed(act, GEMM[f"wout{l}"].j0 + c))

                for half in range(2):
                    g = GEMM[f"fin{l}{half}"]

                    def silu(i, u, src, free, g=g):
                        if u % 2 == 0:
                            wait(act, bank_free[(g.j0 + u - 1) % 2], (g.j0 + u - 1) // 2 + 2 * i + 1)
                            nc.scalar.activation(fsilu[:, 0:width], src[:, 0:width], ACT.Silu).then_inc(free, 1)

                    def hidden(i, u, g=g):
                        if u % 2:
                            _, b, used, _, _ = where(g, i, u)
                            act.wait_ge(bank_free[b], used + 1)
                            nc.scalar.activation(HH[:, 2 * i + u // 2, 0:width], fh[:, 0:width], ACT.Copy).then_inc(h_hi, 1)

                    stage(g.name, silu, hidden)
                    stage(f"fout{l}{half}")

            act.wait_ge(rope_done, 8)
            act.dma_start(sinT[:, :].bitcast(I32), d["pos"]).then_inc(rope_landed, 16)
            norm_plain([X[:, c, 0:NX] for c in range(DC)], 1024, W,
                       lambda c: (freed(act, last("fout11")), freed(act, last("fout11") - 1)) if c == 0 else None, 0)
            act.wait_ge(trig, 2)
            nc.scalar.activation(sinT[:, :], W[0][:, 0:NX], ACT.Sin).then_inc(act_step, 1)
            nc.scalar.activation(cosT[:, :], W[1][:, 0:NX], ACT.Sin).then_inc(act_step, 1)
            stage("eqk", lambda i, u, src, free: nc.scalar.activation(QK[:, 4 * i + u, :], src[:, 0:NX], ACT.Copy).then_inc(free, 1))
            for h in range(2):
                act.dma_start(decay[h][:, :], d["decay"][h]).then_inc(decay_landed[h], 16)

            def v_out(i, u, src, free):
                p = 4 * i + u
                nc.scalar.activation(VE[:, :, p * P:(p + 1) * P], src[:, 0:NX].rearrange("p (b f) -> p b f", b=4),
                                     ACT.Copy).then_inc(free, 1)
            stage("ev", v_out)
            for h in range(8):
                act.wait_ge(ret_pv, h + 1)
                nc.scalar.activation(RT[:, h, :], (M1, MM)[h % 2][:, 0:NX], ACT.Copy).then_inc(ret_copied, 1)
                if h + 2 < 8:
                    act.wait_ge(ret_masked, h + 1)
                    act.dma_start(decay[h % 2][:, :], d["decay"][h + 2]).then_inc(decay_landed[h % 2], 16)
            for h in range(8):
                rms([RT[:, h, :]], NX, W, lambda _: act.wait_ge(ret_copied, 8))
                root(NX, W, 128)

            def eg_out(i, u, src, free):
                wait(act, t_ready, n["t"] - 1)
                nc.scalar.activation(W[4 + u % 2][:, 0:NX], src[:, 0:NX], ACT.Silu).then_inc(free, 1)

            def eg_high(i, u):
                act.wait_ge(t_ready, n["t"] + 1)
                n["t"] += 1
                high_operand(MH[:, 4 * i + u, :], W[6 + u % 2][:, 0:NX])
            stage("eg", eg_out, eg_high)
            stage("eout0")
            t0, op0 = n["t"], n["op"]

            def ce_out(i, u, src, free):
                if u == 3:
                    wait(act, t_ready, t0 + i)
                    nc.scalar.activation(ce_s[:, 0:NX], src[:, 0:NX], ACT.Silu).then_inc(free, 1)

            def ce_high(i, u):
                if u == 3:
                    act.wait_ge(t_ready, t0 + i + 1)
                    nc.scalar.activation(MH[:, i, :], ce_z[:, 0:NX], ACT.Copy).then_inc(operand_hi, 1)
            stage("econv", ce_out, ce_high)
            n["t"] += 8
            n["op"] += 8
            stage("eout1")
            rms([Y[:, c, :] for c in range(DC)], NX, W, lambda c: freed(act, last("eout1") - 7 + c))
            root(NX, W, 1024)

            norm_plain([X[:, c, 0:NX] for c in range(DC)], 1024, W, lambda c: act.wait_ge(resid_ready, c + 1), 0)

            def oin_out(i, u, src, free):
                p = 4 * i + u
                dst = LAT[:, p, :] if p < 5 else kr[:, 0:NX] if p == 5 else SG[:, p - 6, :]
                nc.scalar.activation(dst, src[:, 0:NX], ACT.Silu if p > 5 else ACT.Copy).then_inc(free, 1)
            stage("oin", oin_out)
            norm_plain([LAT[:, c, :] for c in range(3)], 384, WL, lambda c: freed(act, GEMM["oin"].j0 + c), 0)
            norm_plain([LAT[:, c, :] for c in range(3, 5)], 256, WL, lambda c: freed(act, GEMM["oin"].j0 + 3 + c), 3)

            def oq_out(i, u, src, free):
                p = 4 * i + u
                if p < 8:
                    nc.scalar.activation(QN[:, p, :], src[:, 0:NX], ACT.Copy).then_inc(free, 1)
                else:
                    nc.scalar.activation(QR[:, 2 * (p - 8):2 * (p - 8) + 2, :],
                                         src[:, 0:NX].rearrange("p (a t) -> p a t", a=2), ACT.Copy).then_inc(free, 1)
            act.wait_ge(operand_lo, n["op"])
            stage("oq", oq_out)
            stage("ok", lambda i, u, src, free: nc.scalar.activation(KN[:, 4 * i + u, :], src[:, 0:NX], ACT.Copy).then_inc(free, 1))

            def vo_out(i, u, src, free):
                p = 4 * i + u
                nc.scalar.activation(VO[:, :, p * P:(p + 1) * P], src[:, 0:NX].rearrange("p (b f) -> p b f", b=4),
                                     ACT.Copy).then_inc(free, 1)
            stage("ov", vo_out)
            gates = [0]

            def finish2(h, q0, qn):
                gates[0] += 1
                act.wait_ge(gated, gates[0])
                high_operand(XH[:, h, 0:NX], SG[:, h, :])
            attention(units2, 192.0 ** -0.5, (dprobs, dprobsT), finish2)
            stage("oout")
            rms([Y2[:, c, :] for c in range(DC)], NX, WY, lambda c: freed(act, last("oout") - 7 + c))
            root(NX, WY, 1024)

        @block.vector
        def _(dve):
            n = dict(inst=0, op=0, t=0, y=0, step=0, mp=0, rope=0, unit=0, qk=0, gate=0)

            def link(ins):
                n["step"] += 1
                ins.then_inc(dve_step, 1)
                dve.wait_ge(dve_step, n["step"])

            def invert(width, Wt):
                dve.wait_ge(sd_ready, n["inst"] + 1)
                r = Wt[2 + n["inst"] % 2][:, 0:width]
                nc.vector.reciprocal(r, r).then_inc(rs_ready, 1)
                n["inst"] += 1
                dve.wait_ge(rs_ready, n["inst"])
                return r

            def low_operand(dst, src, hi, scale=None):
                dve.wait_ge(operand_hi, n["op"] + 1)
                if scale is None:
                    ins = nc.vector.tensor_tensor(dst, src, hi.bitcast(F32), ALU.subtract)
                else:
                    ins = nc.vector.scalar_tensor_tensor(dst, src, scale, hi.bitcast(F32), ALU.mult, ALU.subtract)
                ins.then_inc(operand_lo, 1)
                n["op"] += 1

            def norm_mod(width):
                r = invert(width, W)
                for c in range(DC + 1):
                    if c < DC:
                        wait(dve, y_ready, n["y"] + c - 1)
                        nc.vector.tensor_tensor(W[4 + c % 2][:, 0:width], X[:, c, 0:width], r, ALU.mult).then_inc(t_ready, 1)
                        n["t"] += 1
                    if c:
                        low_operand(XL[:, c - 1, 0:width], W[6 + (c - 1) % 2][:, 0:width], XH[:, c - 1, 0:width])
                n["y"] += DC

            def norm_plain(sources, gain, Wt, dst):
                r = invert(NX, Wt)
                k = len(sources)
                for c in range(k + 1):
                    if c < k:
                        wait(dve, operand_lo, n["op"] - (1 if c < 2 else 0))
                        nc.vector.scalar_tensor_tensor(Wt[6 + c % 2][:, 0:NX], sources[c], gain[:, c:c + 1], r,
                                                       ALU.mult, ALU.mult).then_inc(t_ready, 1)
                        n["t"] += 1
                    if c:
                        low_operand(XL[:, dst + c - 1, 0:NX], Wt[6 + (c - 1) % 2][:, 0:NX], XH[:, dst + c - 1, 0:NX])

            def norm_post(Yt, gain, Wt):
                r = invert(NX, Wt)
                for c in range(DC):
                    t = Wt[4 + c % 2][:, 0:NX]
                    link(nc.vector.scalar_tensor_tensor(t, Yt[:, c, :], gain[:, c:c + 1], r, ALU.mult, ALU.mult))
                    nc.vector.tensor_tensor(X[:, c, 0:NX], X[:, c, 0:NX], t, ALU.add).then_inc(resid_ready, 1)

            def rope(chunk, tmp, three=False):
                view = (lambda a: a.rearrange("p (a t) -> p a t", a=2)) if three else (lambda a: a)
                dve.wait_ge(rot_ready, n["rope"] + 1)
                n["rope"] += 1
                link(nc.vector.tensor_tensor(view(tmp), view(M1[:, 0:NX]), view(sinT[:, :]), ALU.mult))
                link(nc.vector.tensor_tensor(chunk, chunk, view(cosT[:, :]), ALU.mult))
                nc.vector.tensor_tensor(chunk, chunk, view(tmp), ALU.add).then_inc(rope_done, 1)

            def modulation(l):
                dve.wait_ge(mod_used, 48 * (l + 1))
                link(nc.vector.tensor_tensor(modT[:, :], MM[:, 96 * l:96 * l + 96], pa(f"bmod{l}"), ALU.add))
                m3 = modT[:, :].rearrange("p (m s) -> p m s", s=2)
                for which, m0, gain in ((0, 8, f"g1{l}"), (1, 32, f"g2{l}")):
                    for s in range(2):
                        ins = nc.vector.scalar_tensor_tensor(afac[:, 16 * which + 8 * s:16 * which + 8 * s + 8],
                                                             m3[:, m0:m0 + 8, s], 1.0, pa(gain), ALU.add, ALU.mult)
                ins.then_inc(mod_ready, 1)

            def gated_add(name, segs, m0):
                g = GEMM[name]
                for p in range(g.n):
                    j, b, _, _, _ = where(g, 0, p)
                    dve.wait_ge(panel_done, j + 1)
                    for s, (t0, tn) in enumerate(segs):
                        col = 2 * (m0 + p) + s
                        ins = nc.vector.scalar_tensor_tensor(X[:, p, t0:t0 + tn], G[b][:, t0:t0 + tn], modT[:, col:col + 1],
                                                             X[:, p, t0:t0 + tn], ALU.mult, ALU.add)
                    ins.then_inc(bank_free[b], 1)

            def attention(units, scale, tiles, finish, masked):
                ends = head_ends(units)
                base = n["unit"]

                def tops(i):
                    nk = units[i][3]
                    s = (base + i) % 4
                    dve.wait_ge(scores_ready, base + i + 1)
                    if masked:
                        diag = G[i % 2][:, nk - P:nk]
                        link(nc.vector.tensor_tensor(diag, diag, co("mask"), ALU.add))
                    link(nc.vector.tensor_reduce(stat[:, s:s + 1], G[i % 2][:, 0:nk], AX.X, ALU.max))
                    nc.vector.tensor_scalar(stat[:, 4 + s:5 + s], stat[:, s:s + 1], -scale, None, ALU.mult).then_inc(negmax_ready, 1)

                def norms(i):
                    nk = units[i][3]
                    s = (base + i) % 4
                    t = tiles[0][i % 2][:, 0:nk]
                    dve.wait_ge(exp_done, base + i + 1)
                    link(nc.vector.reciprocal(stat[:, 12 + s:13 + s], stat[:, 8 + s:9 + s]))
                    nc.vector.tensor_scalar(t, t, stat[:, 12 + s:13 + s], None, ALU.mult).then_inc(probs_ready, 1)

                tops(0)
                for i in range(len(units)):
                    if i + 1 < len(units):
                        tops(i + 1)
                    norms(i)
                    if i - 1 in ends:
                        finish(base + i, *ends[i - 1])
                finish(base + len(units), *ends[len(units) - 1])
                n["unit"] += len(units)

            dve.wait_ge(par_landed, 32)
            dve.wait_ge(x_landed, 16)
            modulation(0)
            for l in range(2):
                width, segs = tok(l)
                norm_mod(NT)
                g = GEMM[f"win{l}"]
                for c in range(2):
                    for a, b_ in ((0, HALO), (GLU_AT[0] + NX, GLU_AT[1]), (GLU_AT[1] + NC, GLU_W)):
                        nc.vector.memset(glu[:, c, a:b_], 0.0)
                    for a, b_ in ((0, POOLPAD), (PP_AT[0] + NX, PP_AT[1]), (PP_AT[1] + NC, PP_W)):
                        ins = nc.vector.memset(pp[:, c, a:b_], 0.0)
                    if l == 1:
                        nc.vector.memset(glu[:, c, GLU_AT[1]:GLU_AT[1] + NC], 0.0)
                        ins = nc.vector.memset(pp[:, c, PP_AT[1]:PP_AT[1] + NC], 0.0)
                link(ins)
                for c in range(2):
                    j, b = g.j0 + 2 * c + 1, (g.j0 + 2 * c + 1) % 2
                    dve.wait_ge(panel_done, j + 1)
                    freed(dve, j - 1)
                    for s, (t0, tn) in enumerate(segs):
                        ins = nc.vector.tensor_tensor(glu[:, c, GLU_AT[s]:GLU_AT[s] + tn], G[b][:, t0:t0 + tn],
                                                      pA[:, t0:t0 + tn], ALU.mult)
                    ins.then_inc(bank_free[b], 1)
                freed(dve, g.j0 + 1)
                freed(dve, g.j0 + 3)

                runs = [(c, s, t0, tn) for c in range(2) for s, (t0, tn) in enumerate(segs)]
                per, base = len(runs), (CONV * 4 if l else 0)
                dwa, dwba = PAR[f"dw{l}"][0], PAR[f"dwb{l}"][0]
                for c, s, t0, tn in runs:
                    a = GLU_AT[s] - HALO
                    nc.vector.tensor_scalar(acc[:, c, t0:t0 + tn], glu[:, c, a:a + tn], par[:, dwa + c * CONV:dwa + c * CONV + 1],
                                            par[:, dwba + c:dwba + c + 1], ALU.mult, ALU.add).then_inc(conv_tick, 1)
                with dve.Fori(1, CONV) as tap:
                    for k, (c, s, t0, tn) in enumerate(runs):
                        dve.wait_ge(conv_tick, per * tap + (base - per + k + 1))
                        nc.vector.scalar_tensor_tensor(acc[:, c, t0:t0 + tn], glu[:, c, bass.ds(tap + (GLU_AT[s] - HALO), tn)],
                                                       par[:, bass.ds(tap + (dwa + c * CONV), 1)], acc[:, c, t0:t0 + tn],
                                                       ALU.mult, ALU.add).then_inc(conv_tick, 1)

                for c in range(2):
                    freed(dve, g.j0 + 4 + c)
                    u, hi_part, lo_part = pp[:, c, :], slice(64, P), slice(0, 64)
                    e = PP_W
                    link(nc.vector.tensor_tensor(pA[:, 1:e], u[:, 0:e - 1], u[:, 1:e], ALU.add))
                    if c == 0:
                        nc.vector.tensor_tensor(pB[hi_part, 2:e - 2], pA[hi_part, 1:e - 3], pA[hi_part, 3:e - 1], ALU.add)
                        link(nc.vector.tensor_copy(pB[lo_part, 2:e - 2], pA[lo_part, 2:e - 2]))
                    else:
                        link(nc.vector.tensor_tensor(pB[:, 2:e - 2], pA[:, 1:e - 3], pA[:, 3:e - 1], ALU.add))
                        link(nc.vector.tensor_tensor(pA[:, 4:e - 4], pB[:, 2:e - 6], pB[:, 6:e - 2], ALU.add))
                        nc.vector.tensor_tensor(pB[hi_part, 8:e - 8], pA[hi_part, 4:e - 12], pA[hi_part, 12:e - 4], ALU.add)
                        link(nc.vector.tensor_copy(pB[lo_part, 8:e - 8], pA[lo_part, 8:e - 8]))
                    for s, (t0, tn) in enumerate(segs):
                        a = PP_AT[s]
                        for side, q in enumerate((a, a + tn - 8)):
                            tab = co("edge")[:, 16 * c + 8 * side:16 * c + 8 * side + 8]
                            ins = nc.vector.tensor_tensor(pB[:, q:q + 8], pB[:, q:q + 8], tab, ALU.mult)
                    link(ins)
                    for s, (t0, tn) in enumerate(segs):
                        a = PP_AT[s]
                        ins = nc.vector.scalar_tensor_tensor(pp[:, c, a:a + tn], pB[:, a:a + tn], co("invw")[:, c:c + 1],
                                                             pp[:, c, a:a + tn], ALU.mult, ALU.subtract)
                    ins.then_inc(pool_ready, 1)
                dve.wait_ge(pool_ready, 2 * (l + 1))

                for m in range(2):
                    low_operand(XL[:, 2 + m, 0:width], M0[:, 0:width], XH[:, 2 + m, 0:width])

                dve.wait_ge(rope_landed, 32)
                for c in range(2, 6):
                    tw = NT if l == 0 or c >= 4 else NX
                    r = invert(tw, W)
                    nc.vector.scalar_tensor_tensor(PR[:, c, 0:tw], PR[:, c, 0:tw], pa(f"qg{l}" if c < 4 else f"kg{l}"), r,
                                                   ALU.mult, ALU.mult).then_inc(qk_normed, 1)
                    n["qk"] += 1
                    rope(PR[:, c, 0:NX], W[4][:, 0:NX])

                def finish1(_, h, q0, qn):
                    part = slice(64 * (h % 2), 64 * (h % 2) + 64)
                    low_operand(XL[part, h // 2, q0:q0 + qn], M1[part, 0:qn], XH[part, h // 2, q0:q0 + qn])

                attention(units1(l), 0.125, (W[0:2], W[2:4]), finish1, False)

                dve.wait_ge(ln_sum, l + 1)
                for c in range(2):
                    ins = nc.vector.scalar_tensor_tensor(acc[:, c, 0:width], M0[:, 0:width], -1.0 / 256, acc[:, c, 0:width],
                                                         ALU.mult, ALU.add)
                ins.then_inc(ln_centered, 1)
                dve.wait_ge(ln_centered, l + 1)
                r = invert(width, W)
                for c in range(2):
                    nc.vector.tensor_tensor(acc[:, c, 0:width], acc[:, c, 0:width], r, ALU.mult).then_inc(ln_scaled, 1)
                for m in range(2):
                    low_operand(XL[:, 4 + m, 0:width], M0[:, 0:width], XH[:, 4 + m, 0:width])
                for m in range(2):
                    low_operand(XL[:, 6 + m, 0:width], M0[:, 0:width], XH[:, 6 + m, 0:width], pa(f"psc{l}")[:, m:m + 1])

                gated_add(f"wout{l}", segs, 16)
                freed(dve, last(f"wout{l}"))
                freed(dve, last(f"wout{l}") - 1)
                norm_mod(width)
                for half in range(2):
                    g = GEMM[f"fin{l}{half}"]

                    def hidden(i, u, g=g, l=l, half=half):
                        if u % 2 == 0:
                            return
                        j, b, used, _, _ = where(g, i, u)
                        e = FH * (2 * l + half) + 2 * i + u // 2
                        dve.wait_ge(panel_done, j + 1)
                        dve.wait_ge(bank_free[1 - b], (g.j0 + u - 1) // 2 + 2 * i + 1)
                        wait(dve, h_lo, e)
                        nc.vector.tensor_tensor(fh[:, 0:width], fsilu[:, 0:width], G[b][:, 0:width], ALU.mult).then_inc(bank_free[b], 1)
                        dve.wait_ge(h_hi, e + 1)
                        c = 2 * i + u // 2
                        nc.vector.tensor_tensor(HL[:, c, 0:width], fh[:, 0:width], HH[:, c, 0:width].bitcast(F32),
                                                ALU.subtract).then_inc(h_lo, 1)
                    each_panel(dve, g, hidden)
                    gated_add(f"fout{l}{half}", segs, 40)
                freed(dve, last(f"fout{l}1"))
                freed(dve, last(f"fout{l}1") - 1)
                if l == 0:
                    modulation(1)

            norm_plain([X[:, c, 0:NX] for c in range(DC)], pa("pre")[:, 0:8], W, 0)
            dve.wait_ge(rope_landed, 48)
            ang, k_, turns = W[4][:, 0:NX], W[5][:, 0:NX], W[6][:, 0:NX]
            magic = 1.5 * 2.0 ** 23
            tau = (6.28125, 0.0019350051879882812, 3.019915981956753e-07)
            link(nc.vector.tensor_copy(ang, sinT[:, :].bitcast(I32)))
            link(nc.vector.tensor_scalar(ang, ang, co("inv"), None, ALU.mult))
            for s in range(2):
                r = W[s][:, 0:NX]
                link(nc.vector.tensor_scalar(turns, ang, 1.0 / (2.0 * np.pi), 0.25 * s, ALU.mult, ALU.add))
                link(nc.vector.tensor_scalar(turns, turns, magic, None, ALU.add))
                link(nc.vector.tensor_scalar(k_, turns, -magic, None, ALU.add))
                link(nc.vector.scalar_tensor_tensor(r, k_, -tau[0], ang, ALU.mult, ALU.add))
                link(nc.vector.scalar_tensor_tensor(r, k_, -tau[1], r, ALU.mult, ALU.add))
                link(nc.vector.scalar_tensor_tensor(r, k_, -tau[2], r, ALU.mult, ALU.add))
                if s:
                    link(nc.vector.tensor_scalar(r, r, float(np.pi / 2), None, ALU.add))
                nc.vector.tensor_scalar(r, r, 3.1415925, -3.1415925, ALU.min, ALU.max).then_inc(trig, 1)
            dve.wait_ge(act_step, 2)
            for c in range(8):
                freed(dve, GEMM["eqk"].j0 + c)
                rope(QK[:, c, :], W[4][:, 0:NX])

            for h in range(8):
                dve.wait_ge(ret_scores, h + 1)
                dve.wait_ge(decay_landed[h % 2], 16 * (h // 2 + 1))
                wait(dve, ret_pv, h - 1)
                for jb, c0, cn in RET_AT:
                    src = G[h % 2][:, c0:c0 + cn] if c0 < 1024 else M0[:, 512 * (h % 2):512 * (h % 2) + cn]
                    ins = nc.vector.tensor_tensor(scT[h % 2][:, c0:c0 + cn], src, decay[h % 2][:, 0:cn], ALU.mult)
                ins.then_inc(ret_masked, 1)
            for h in range(8):
                r = invert(NX, W)
                nc.vector.scalar_tensor_tensor(RT[:, h, :], RT[:, h, :], pa("gn")[:, h:h + 1], r, ALU.mult,
                                               ALU.mult).then_inc(ret_normed, 1)
            dve.wait_ge(ret_normed, 8)
            g = GEMM["eg"]
            for p in range(8):
                freed(dve, g.j0 + p)
                wait(dve, operand_lo, n["op"])
                nc.vector.tensor_tensor(W[6 + p % 2][:, 0:NX], W[4 + p % 2][:, 0:NX], RT[:, p, :], ALU.mult).then_inc(t_ready, 1)
                n["t"] += 1
                low_operand(ML[:, p, :], W[6 + p % 2][:, 0:NX], MH[:, p, :])
            g = GEMM["eout0"]
            for p in range(8):
                j, b = g.j0 + p, (g.j0 + p) % 2
                dve.wait_ge(panel_done, j + 1)
                nc.vector.tensor_copy(Y[:, p, :], G[b][:, 0:NX]).then_inc(bank_free[b], 1)

            g = GEMM["econv"]
            t0, op0, cwa, cba = n["t"], n["op"], PAR["cw"][0], PAR["cb"][0]
            link(nc.vector.memset(ce_u[:, 0:2], 0.0))

            def short_conv(i, u):
                j, b, used, _, _ = where(g, i, u)
                if u < 3:
                    dve.wait_ge(panel_done, j + 1)
                if u == 0:
                    dve.wait_ge(t_ready, t0 + i)
                    nc.vector.tensor_copy(ce_c[:, 0:NX], G[b][:, 0:NX]).then_inc(bank_free[b], 1)
                elif u == 1:
                    dve.wait_ge(bank_free[1 - b], (g.j0 + u - 1) // 2 + 2 * i + 1)
                    nc.vector.tensor_tensor(ce_u[:, 2:NX + 2], G[b][:, 0:NX], ce_c[:, 0:NX], ALU.mult).then_inc(bank_free[b], 1)
                    dve.wait_ge(bank_free[b], used + 1)
                    w = [par[:, bass.ds(3 * i + (cwa + t), 1)] for t in range(3)]
                    nc.vector.tensor_scalar(ce_y[:, 0:NX], ce_u[:, 0:NX], w[0], par[:, bass.ds(i + cba, 1)], ALU.mult,
                                            ALU.add).then_inc(ce_tick, 1)
                    for t in (1, 2):
                        dve.wait_ge(ce_tick, 3 * i + t)
                        nc.vector.scalar_tensor_tensor(ce_y[:, 0:NX], ce_u[:, t:NX + t], w[t], ce_y[:, 0:NX], ALU.mult,
                                                       ALU.add).then_inc(ce_tick, 1)
                elif u == 2:
                    dve.wait_ge(ce_tick, 3 * i + 3)
                    nc.vector.tensor_tensor(ce_c[:, 0:NX], G[b][:, 0:NX], ce_y[:, 0:NX], ALU.mult).then_inc(bank_free[b], 1)
                else:
                    dve.wait_ge(bank_free[1 - b], (g.j0 + u - 1) // 2 + 2 * i + 1)
                    dve.wait_ge(bank_free[b], used + 1)
                    dve.wait_ge(operand_lo, op0 + i)
                    nc.vector.tensor_tensor(ce_z[:, 0:NX], ce_c[:, 0:NX], ce_s[:, 0:NX], ALU.mult).then_inc(t_ready, 1)
                    dve.wait_ge(operand_hi, op0 + i + 1)
                    nc.vector.tensor_tensor(ML[:, i, :], ce_z[:, 0:NX], MH[:, i, :].bitcast(F32), ALU.subtract).then_inc(operand_lo, 1)
            each_panel(dve, g, short_conv)
            n["t"] += 8
            n["op"] += 8
            g = GEMM["eout1"]
            freed(dve, last("eout0"))
            freed(dve, last("eout0") - 1)
            for p in range(8):
                j, b = g.j0 + p, (g.j0 + p) % 2
                dve.wait_ge(panel_done, j + 1)
                nc.vector.tensor_tensor(Y[:, p, :], G[b][:, 0:NX], Y[:, p, :], ALU.add).then_inc(bank_free[b], 1)
            freed(dve, last("eout1"))
            freed(dve, last("eout1") - 1)
            norm_post(Y, pa("post")[:, 0:8], W)

            dve.wait_ge(resid_ready, 8)
            norm_plain([X[:, c, 0:NX] for c in range(DC)], pa("pre")[:, 8:16], W, 0)
            norm_plain([LAT[:, c, :] for c in range(3)], pa("qa"), WL, 0)
            norm_plain([LAT[:, c, :] for c in range(3, 5)], pa("kva"), WL, 3)
            rope(kr[:, 0:NX], dprobs[0][:, 0:NX])
            for c in range(4):
                freed(dve, GEMM["oq"].j0 + 8 + c)
                rope(QR[:, 2 * c:2 * c + 2, :], dprobs[0][:, 0:NX], True)

            def finish2(unit, h, q0, qn):
                o = (M1, MM)[h % 2]
                dve.wait_ge(pv_done, unit)
                nc.vector.tensor_tensor(SG[:, h, :], o[:, 0:NX], SG[:, h, :], ALU.mult).then_inc(gated, 1)
                low_operand(XL[:, h, 0:NX], SG[:, h, :], XH[:, h, 0:NX])
            attention(units2, 192.0 ** -0.5, (dprobs, dprobsT), finish2, True)
            g = GEMM["oout"]
            for p in range(8):
                j, b = g.j0 + p, (g.j0 + p) % 2
                dve.wait_ge(panel_done, j + 1)
                nc.vector.tensor_copy(Y2[:, p, :], G[b][:, 0:NX]).then_inc(bank_free[b], 1)
            freed(dve, last("oout"))
            freed(dve, last("oout") - 1)
            norm_post(Y2, pa("post")[:, 8:16], WY)



def chunked(v):
    return np.ascontiguousarray(np.asarray(v).reshape(-1, P).T)


def panel(w, cols):
    w = np.asarray(w)[:, cols]
    return w.reshape(-1, P, P).transpose(1, 0, 2).reshape(P, -1)


def panels(inp):
    by = {}

    def add(name, items):
        g = GEMM[name]
        assert len(items) == g.n, name
        by.setdefault(g.kc, []).extend(items)

    run = lambda a: np.arange(a, a + P)
    for l in range(2):
        w = inp["w_in"][l]
        k0 = np.arange(256, 320)
        cols = [run(1024), run(768), run(1152), run(896), run(1280), run(1408), run(512), run(640), run(0), run(128),
                np.concatenate([k0, k0]), np.concatenate([k0 + 64, k0 + 64]), run(384)]
        add(f"win{l}", [panel(w, c) for c in cols])
        add(f"wout{l}", [panel(inp["w_out"][l], run(P * m)) for m in range(8)])
        for half in range(2):
            add(f"fin{l}{half}", [panel(inp["w_ffn_in"][l], run(2 * FH * P * s + (FH * half + i) * P))
                                  for i in range(FH) for s in range(2)])
            add(f"fout{l}{half}", [panel(inp["w_ffn_out"][l][FH * P * half:FH * P * (half + 1)], run(P * m)) for m in range(8)])
    w = inp["even_w_in_2"][0]
    add("eqk", [panel(w, run(P * c)) for c in range(8)])
    add("ev", [panel(w, run(1024 + P * c)) for c in range(8)])
    add("eg", [panel(w, run(2048 + P * c)) for c in range(8)])
    add("eout0", [panel(inp["even_w_out_2"][0][0:1024], run(P * m)) for m in range(8)])
    add("econv", [panel(w, run(at + P * c)) for c in range(8) for at in (4096, 5120, 3072, 6144)])
    add("eout1", [panel(inp["even_w_out_2"][0][1024:2048], run(P * m)) for m in range(8)])
    w = inp["odd_w_in_2"][0]
    r0 = np.arange(640, 704)
    add("oin", [panel(w, c) for c in [run(P * c) for c in range(5)] + [np.concatenate([r0, r0])] + [run(704 + P * c) for c in range(8)]])
    w = inp["w_qb_2"][0]
    r0 = np.arange(128, 192)
    add("oq", [panel(w, run(192 * h)) for h in range(8)]
        + [panel(w, np.concatenate([r0 + 192 * 2 * c, r0 + 192 * (2 * c + 1)])) for c in range(4)])
    w = inp["w_kvb_2"][0]
    add("ok", [panel(w, run(256 * h)) for h in range(8)])
    add("ov", [panel(w, run(256 * h + P)) for h in range(8)])
    add("oout", [panel(inp["odd_w_out_2"][0], run(P * m)) for m in range(8)])
    return {kc: np.stack(v) for kc, v in by.items()}


def parameters(inp):
    par = np.zeros((P, NPAR), np.float32)

    def put(name, v):
        a, w = PAR[name]
        par[:, a:a + w] = v
    for l in range(2):
        b = chunked(inp["b_mod"][l])
        put(f"bmod{l}", np.repeat(b, 2, axis=1))
        put(f"g1{l}", chunked(inp["g_norm1"][l]))
        put(f"g2{l}", chunked(inp["g_norm2"][l]))
        put(f"qg{l}", np.concatenate([inp["q_norm_g"][l]] * 2)[:, None])
        put(f"kg{l}", np.concatenate([inp["k_norm_g"][l]] * 2)[:, None])
        put(f"dw{l}", inp["conv_dw_w"][l].reshape(CONV, 2, P).transpose(2, 1, 0).reshape(P, -1))
        for key, name in (("dwb", "conv_dw_b"), ("lng", "conv_ln_g"), ("lnb", "conv_ln_b"), ("psc", "pool_scale")):
            put(f"{key}{l}", chunked(inp[name][l]))
    put("pre", np.concatenate([chunked(inp["pre_norm_2"][e]) for e in range(2)], axis=1))
    put("post", np.concatenate([chunked(inp["post_norm_2"][e]) for e in range(2)], axis=1))
    put("cw", inp["even_conv_w_2"][0].reshape(3, 8, P).transpose(2, 1, 0).reshape(P, -1))
    put("cb", chunked(inp["even_conv_b_2"][0]))
    put("gn", chunked(inp["ret_gn_2"][0]))
    put("qa", chunked(inp["q_a_norm_2"][0]))
    put("kva", chunked(inp["kv_a_norm_2"][0]))
    put("c", np.stack([chunked(inp["c"][0]), chunked(inp["c_ctx"])], axis=2).reshape(P, 16))
    return par


def constants():
    con = np.zeros((P, NCON), np.float64)

    def put(name, v):
        a, w = CON[name]
        con[:, a:a + w] = v
    i = np.arange(P)
    put("ident", np.eye(P))
    put("ones", 1.0)
    put("blk", i[:, None] // 64 == i[None, :] // 64)
    perm1, perm2 = np.zeros((P, P)), np.zeros((P, P))
    for m in range(P):
        perm1[m ^ 1, m] = 1.0 if m % 2 else -1.0
        perm2[m ^ 32, m] = 1.0 if m % 64 >= 32 else -1.0
    put("perm1", perm1)
    put("perm2", perm2)
    put("mask", np.where(i[None, :] <= i[:, None], 0.0, -1e30))
    win = np.array([2, 4, 8, 16])[np.stack([i // 64, 2 + i // 64], axis=1)]
    put("invw", 1.0 / win)
    edge = np.ones((P, 2, 2, 8))
    for c in range(2):
        for q in range(8):
            w = win[:, c]
            edge[:, c, 0, q] = w / np.minimum(w, q + w // 2)
            edge[:, c, 1, q] = w / np.minimum(w, 8 - q + w // 2)
    put("edge", edge.reshape(P, 32))
    put("inv", (10000.0 ** (-(np.arange(0, 64, 2, dtype=np.float32)) / np.float32(64)))[i % 32][:, None])
    put("eps", EPS)
    return con.astype(np.float32)


def dft_tables():
    out = []
    for nn in (NX, NC):
        a = 2 * np.pi * (np.outer(np.arange(nn), np.arange(nn)) % nn) / nn
        s = 1.0 / np.sqrt(nn * 64.0)
        t = np.stack([np.cos(a) * s, np.sin(a) * s], axis=1)
        out.append(t.reshape(nn // P, P, 2 * nn).astype(np.float32))
    a = 2 * np.pi * (np.outer(np.arange(64), np.arange(64)) % 64) / 64
    d = np.zeros((2, 64, 2, 2, 64))
    for b in range(2):
        d[b, :, 0, b] = np.cos(a)
        d[b, :, 1, b] = -np.sin(a)
    return out[0], out[1], d.reshape(P, 256).astype(np.float32)


def rope_tables():
    inv = 10000.0 ** (-np.arange(16) / 16.0)
    row, col = np.arange(NX) // 64, np.arange(NX) % 64
    ang = np.concatenate([np.outer(inv, row), np.outer(inv, col)])[(np.arange(P) % 64) // 2]
    return np.cos(ang).astype(np.float32), np.sin(ang).astype(np.float32)


def decay_tables():
    lg = np.log1p(-np.exp2(-5.0 - np.arange(8)))
    rel = np.arange(NX)[None, :] - np.arange(P)[:, None]
    return np.where(rel >= 0, np.exp(lg[:, None, None] * np.maximum(rel, 0)) * 0.125, 0.0).astype(np.float32)


def kernel(**inputs):
    import concourse.bacc as _bacc
    from concourse.bass_utils import run_bass_kernel_spmd as _run

    inp = {k: np.asarray(v) for k, v in inputs.items()}
    w = panels(inp)
    dx, dc, dd = dft_tables()
    cosx, sinx = rope_tables()
    small = np.zeros((2, P, 1536), np.float32)
    for l in range(2):
        small[l, :, 0:512] = inp["w_fourier"][l].reshape(2, P, 256).transpose(1, 0, 2).reshape(P, 512)
        small[l, :, 512:1024] = inp["w_conv_pw"][l].reshape(2, P, 256).transpose(1, 0, 2).reshape(P, 512)
        for q in range(4):
            part, at = 64 * (q % 2), 1024 + P * (q // 2) + 64 * (q % 2)
            small[l, part:part + 64, at:at + 64] = inp["w_pool"][l][q]
        small[l, :, 1280:1536] = dd
    arrays = {
        "par": parameters(inp), "con": constants(),
        "xt": np.concatenate([inp["x"][0], inp["ctx"][0]]).T.reshape(DC, P, NT).transpose(1, 0, 2),
        "wmod": np.stack([panel(inp["w_mod"][l], np.arange(P * m, P * m + P)) for l in range(2) for m in range(48)]),
        "small": small, "dftx": dx, "dftc": dc, "cosx": cosx, "sinx": sinx, "decay": decay_tables(),
        "pos": np.tile(inp["positions_2"].reshape(1, NX), (P, 1)),
    }
    arrays.update({f"w{kc}": v for kc, v in w.items()})
    arrays = {k: np.ascontiguousarray(v) for k, v in arrays.items()}
    nc = _bacc.Bacc("TRN2", target_bir_lowering=False, num_devices=1)
    d = {k: nc.dram_tensor(f"in_{k}", v.shape, mybir.dt.from_np(v.dtype), kind="ExternalInput").ap() for k, v in arrays.items()}
    d["out"] = nc.dram_tensor("out_x", (P, DC, NX), F32, kind="ExternalOutput").ap()
    build_program(nc, d)
    r = _run(nc, [{f"in_{k}": v for k, v in arrays.items()}], core_ids=[0])
    out = r.results[0]["out_x"]
    return np.ascontiguousarray(out.transpose(1, 0, 2).reshape(DC * P, NX).T)[None]
```

```python
from contextlib import ExitStack

import numpy as np

import concourse.bass as bass
from concourse import mybir

F32 = mybir.dt.float32
F32R = mybir.dt.float32r
I32 = mybir.dt.int32
ALU = mybir.AluOpType
ACT = mybir.ActivationFunctionType
AX = mybir.AxisListType

P = 128
NX, NC = 512, 256
NT = NX + NC
DC = 8
FH = 11
EPS = 1e-6
RAW = 4
SBUF_END = 229312
CONV = 31
HALO = CONV // 2
POOLPAD = 8
SEGS = [(0, NX), (NX, NC)]
GLU_AT = [HALO, NX + 3 * HALO]
GLU_W = NT + 4 * HALO
PP_AT = [POOLPAD, NX + 3 * POOLPAD]
PP_W = NT + 4 * POOLPAD



class Gemm:
    def __init__(self, name, kc, n, j0, at):
        self.name, self.kc, self.n, self.j0, self.at = name, kc, n, j0, at


def plan():
    gemms, used = [], {}
    j = 0
    for name, kc, n in (
        [x for l in range(2) for x in (
            (f"win{l}", 8, 13), (f"wout{l}", 8, 8),
            (f"fin{l}0", 8, 2 * FH), (f"fout{l}0", FH, 8),
            (f"fin{l}1", 8, 2 * FH), (f"fout{l}1", FH, 8))]
        + [("eqk", 8, 8), ("ev", 8, 8), ("eg", 8, 8), ("eout0", 8, 8), ("econv", 8, 32), ("eout1", 8, 8),
           ("oin", 8, 14), ("oq", 3, 12), ("ok", 2, 8), ("ov", 2, 8), ("oout", 8, 8)]
    ):
        gemms.append(Gemm(name, kc, n, j, used.get(kc, 0)))
        used[kc] = used.get(kc, 0) + n
        j += n
    return gemms


GEMMS = plan()
GEMM = {g.name: g for g in GEMMS}
MOD_FIRST = 16
MOD_ALL = 40
MOD_STARTS = (0, MOD_FIRST, 40, 62, 70, 92)
JMOD = GEMM["wout0"].j0 + 2


def ring_shift(j):
    return (MOD_FIRST if j < JMOD else MOD_ALL) // RAW


def mod_ring(k):
    return k if k < MOD_FIRST else k + JMOD


NPANEL = sum(g.n for g in GEMMS)
KC_OF = [g.kc for g in GEMMS for _ in range(g.n)]

PAR = {}


def _par_layout():
    at = 0
    for l in range(2):
        PAR[f"mod{l}"] = (at, 96)
        at += 96
    for l in range(2):
        for name, w in (("g1", 8), ("g2", 8), ("qg", 1), ("kg", 1), ("dw", 2 * CONV), ("dwb", 2),
                        ("lng", 2), ("lnb", 2), ("psc", 2)):
            PAR[name + str(l)] = (at, w)
            at += w
    for name, w in (("pre", 16), ("post", 16), ("cw", 24), ("cb", 8), ("gn", 8), ("qa", 3), ("kva", 2)):
        PAR[name] = (at, w)
        at += w
    return at


NPAR = _par_layout()

CON = {}


def _con_layout():
    at = 0
    for name, w in (("ident", 128), ("ones", 128), ("blk", 128), ("perm1", 128), ("perm2", 128), ("mask", 128),
                    ("invw", 2), ("edge", 32), ("inv", 1), ("eps", 1), ("half", 2)):
        CON[name] = (at, w)
        at += w
    return at


NCON = _con_layout()


def wait(eng, sem, value):
    if isinstance(value, int) and value <= 0:
        return
    eng.wait_ge(sem, value)


def build_program(nc, d):
    stack = ExitStack()
    with stack:
        base = nc.sbuf_base
        top = [(base + 63) // 64 * 64]

        def at(name, shape, dt, offset):
            return nc.alloc_sbuf_tensor_at(name, [P, shape], dt, offset=offset)

        def sb(name, width, dt=F32):
            t = at(name, width, dt, top[0])
            top[0] += (width * 4 + 63) // 64 * 64
            return t

        Xf = sb("resid", DC * NT)
        X = Xf[:, :].rearrange("p (c t) -> p c t", c=DC)
        xhi_t, xlo_t = sb("operand_hi", DC * NT, F32R), sb("operand_lo", DC * NT, F32R)
        XH = xhi_t[:, :].rearrange("p (c t) -> p c t", c=DC)
        XL = xlo_t[:, :].rearrange("p (c t) -> p c t", c=DC)
        raw = [sb(f"raw{s}", FH * P) for s in range(RAW)]
        whi = [sb(f"whi{s}", FH * P, F32R) for s in range(2)]
        wlo = [sb(f"wlo{s}", FH * P, F32R) for s in range(2)]
        par = sb("par", NPAR)
        con = sb("con", NCON)
        cosT, sinT = sb("cosT", NX), sb("sinT", NX)
        afac = sb("afac", 32)
        stat = sb("stat", 24)
        sums = sb("mod_sums", 8)
        rootT = sb("rootT", 24)
        region = top[0]
        silu_c = at("silu_c", 2 * DC * P, F32, SBUF_END - 8 * DC * P)
        mod_half = [cosT, sinT]

        def pa(name):
            a, w = PAR[name]
            return par[:, a:a + w]

        def co(name):
            a, w = CON[name]
            return con[:, a:a + w]

        ident, ones, blk = co("ident"), co("ones"), co("blk")

        def phase():
            top[0] = region

        phase()
        projf = sb("proj", 6 * NT)
        PR = projf[:, :].rearrange("p (c t) -> p c t", c=6)
        vtok = sb("vtok", NT)
        gluf = sb("glu", 2 * GLU_W)
        glu = gluf[:, :].rearrange("p (c t) -> p c t", c=2)
        accf = sb("conv_acc", 2 * NT)
        acc = accf[:, :].rearrange("p (c t) -> p c t", c=2)
        ppf = sb("pool_in", 2 * PP_W)
        pp = ppf[:, :].rearrange("p (c t) -> p c t", c=2)
        pA = sb("pool_a", PP_W)
        smallw = sb("smallw", 1536)
        dftd = smallw[:, 1280:1536]
        wf = smallw[:, 0:512].rearrange("p (k m) -> p k m", k=2)
        wpw = smallw[:, 512:1024].rearrange("p (k m) -> p k m", k=2)
        wpl = smallw[:, 1024:1280].rearrange("p (k m) -> p k m", k=2)
        zone = top[0] = max(top[0], region + 24 * NX * 4)
        W = [sb(f"work{s}", NT) for s in range(8)]
        endA = top[0]
        pB = at("pool_b", PP_W, F32, zone + 5120 * 4)
        ftok = at("fourier_tok", 6 * 512, F32, zone)
        dft = [at(f"dft{s}", 1024, F32, zone + (3072 + 1024 * s) * 4) for s in range(2)]

        phase()
        hhi_t, hlo_t = sb("hidden_hi", FH * NT, F32R), sb("hidden_lo", FH * NT, F32R)
        HH = hhi_t[:, :].rearrange("p (c t) -> p c t", c=FH)
        HL = hlo_t[:, :].rearrange("p (c t) -> p c t", c=FH)
        fsilu, fh = sb("ffn_silu", NT), sb("ffn_h", NT)
        endB = top[0]

        phase()
        QK = sb("ret_qk", 8 * NX)[:, :].rearrange("p (c t) -> p c t", c=8)
        VE = sb("ret_v", 4 * 1024)[:, :].rearrange("p (b f) -> p b f", b=4)
        RT = sb("ret_r", 8 * NX)[:, :].rearrange("p (c t) -> p c t", c=8)
        MH = at("mix_hi", 8 * NX, F32R, region)[:, :].rearrange("p (c t) -> p c t", c=8)
        ML = at("mix_lo", 8 * NX, F32R, region + 8 * NX * 4)[:, :].rearrange("p (c t) -> p c t", c=8)
        Y = at("layer_y", 8 * NX, F32, region + 16 * NX * 4)[:, :].rearrange("p (c t) -> p c t", c=8)
        assert zone >= top[0]
        decay = [at(f"decay{s}", NX, F32, zone + s * NX * 4) for s in range(2)]
        scT = [at(f"scoresT{s}", 1280, F32, zone + (2 * NX + 1280 * s) * 4) for s in range(2)]
        ce_c, ce_u, ce_y, ce_s, ce_z = (at(n, NX + 2, F32, zone + i * 2112) for i, n in enumerate(("ce_c", "ce_u", "ce_y", "ce_s", "ce_z")))

        vfE = W[5:7]

        phase()
        QN = sb("q_nope", 8 * NX)[:, :].rearrange("p (c t) -> p c t", c=8)
        KN = sb("k_nope", 8 * NX)[:, :].rearrange("p (c t) -> p c t", c=8)
        VO = sb("v_lat", 4 * 1024)[:, :].rearrange("p (b f) -> p b f", b=4)
        SG = sb("silu_gate", 8 * NX)[:, :].rearrange("p (c t) -> p c t", c=8)
        QR = X[:, :, NX:NT]
        kr = sb("k_rope", NX)
        dprobs = [sb(f"dprobs{s}", NX) for s in range(2)]
        dprobsT = [sb(f"dprobsT{s}", NX) for s in range(2)]
        vfD = dprobs
        LAT = at("latent", 5 * NX, F32, region + 8 * NX * 4)[:, :].rearrange("p (c t) -> p c t", c=5)
        WL = [at(f"work_latent{s}", NX, F32, region + s * NX * 4) for s in range(8)]
        WY = [at(f"work_out{s}", NX, F32, region + (8 + s) * NX * 4) for s in range(8)]
        Y2 = at("layer_y2", 8 * NX, F32, region)[:, :].rearrange("p (c t) -> p c t", c=8)
        endD = top[0]
        assert max(endA, endB) <= SBUF_END - 8 * DC * P and endD <= SBUF_END

        def ps(name, width):
            return stack.enter_context(nc.psum_tensor(name, [P, width], F32))
        G = [ps("prod0", 1024), ps("prod1", 1024)]
        M0, M1, MM = ps("misc0", 1024), ps("misc1", 512), ps("misc2", 512)

        SUMS = 1000

        def sem(name):
            return stack.enter_context(nc.semaphore(name))

        raw_landed = [sem(f"raw_landed{s}") for s in range(RAW)]
        hi_ready, lo_ready = sem("hi_ready"), sem("lo_ready")
        panel_done = sem("panel_done")
        bank_free = [sem("bank_free0"), sem("bank_free1")]
        mod_step, afac_ready, c_ready, c_landed = sem("mod_step"), sem("afac_ready"), sem("c_ready"), sem("c_landed")
        half_landed = [sem("half_landed0"), sem("half_landed1")]
        par_landed, x_landed, small_landed = sem("par_landed"), sem("x_landed"), sem("small_landed")
        rope_landed, out_landed = sem("rope_landed"), sem("out_landed")
        sq_ready, sq_used, sd_ready, rs_ready = sem("sq_ready"), sem("sq_used"), sem("sd_ready"), sem("rs_ready")
        t_ready = sem("t_ready")
        operand_hi, operand_lo = sem("operand_hi"), sem("operand_lo")
        resid_ready = sem("resid_ready")
        conv_tick, dve_step, act_step = sem("conv_tick"), sem("dve_step"), sem("act_step")
        ft_ready, ft_copied, dft_landed, dft_used, fy_copied = (
            sem("ft_ready"), sem("ft_copied"), [sem("dft_landed0"), sem("dft_landed1")], sem("dft_used"), sem("fy_copied"))
        mp_ready, rb_ready, turned, turn_copied = sem("mp_ready"), sem("rb_ready"), sem("turned"), sem("turn_copied")
        qk_normed, rot_ready, rope_done = sem("qk_normed"), sem("rot_ready"), sem("rope_done")
        scores_ready, negmax_ready, exp_done = sem("scores_ready"), sem("negmax_ready"), sem("exp_done")
        probs_ready, probsT_ready, probsT_copied, pv_done = (
            sem("probs_ready"), sem("probsT_ready"), sem("probsT_copied"), sem("pv_done"))
        gated = sem("gated")
        ln_sum, ln_centered, ln_scaled, ln_act, pool_ready = (
            sem("ln_sum"), sem("ln_centered"), sem("ln_scaled"), sem("ln_act"), sem("pool_ready"))
        h_hi, h_lo = sem("h_hi"), sem("h_lo")
        decay_landed, ret_scores, ret_masked, ret_pv, ret_copied, ret_normed = (
            [sem("decay_landed0"), sem("decay_landed1")], sem("ret_scores"), sem("ret_masked"), sem("ret_pv"), sem("ret_copied"), sem("ret_normed"))
        ce_tick, trig = sem("ce_tick"), sem("trig")


        def where(g, i, u):
            jj = g.j0 + u
            shift = ring_shift(jj + 4 * i if isinstance(i, int) else jj + 4)
            return jj + 4 * i, jj % 2, jj // 2 + 2 * i, jj % RAW, jj // RAW + i + shift

        def each_panel(eng, g, body):
            full = (g.n - 2) // 4 if g.n > 16 else 1
            for u in range(min(4, g.n)):
                body(0, u)
            if full > 1:
                with eng.Fori(1, full) as i:
                    for u in range(4):
                        body(i, u)
            for p in range(4 * full, g.n):
                body(p // 4, p % 4)

        def freed(eng, j):
            wait(eng, bank_free[j % 2], j // 2 + 1)

        def last(name):
            return GEMM[name].j0 + GEMM[name].n - 1

        def tok(l):
            return (NT, SEGS) if l == 0 else (NX, SEGS[:1])

        def win_width(l, p):
            return NT if l == 0 or p >= 10 else NX

        def units1(l):
            out = [(h, 128 * b, 0, NT) for h in range(4) for b in range(4)]
            if l == 0:
                out += [(h, NX + 128 * b, NX, NC) for h in range(4) for b in range(2)]
            return out

        def head_ends(units):
            ends, start = {}, 0
            for n, u in enumerate(units):
                if n + 1 == len(units) or units[n + 1][0] != u[0]:
                    ends[n] = (u[0], units[start][1], u[1] + 128 - units[start][1])
                    start = n + 1
            return ends

        units2 = [(h, 128 * b, 0, 128 * (b + 1)) for h in range(8) for b in range(4)]
        RET_AT = [(0, 0, 512), (1, 512, 384), (3, 896, 128), (2, 1024, 256)]

        block = stack.enter_context(nc.Block())

        @block.sync
        def _(sp):
            sp.dma_start(silu_c[:, :], d["c"]).then_inc(c_landed, 16)
            sp.dma_start(par[:, :], d["par"]).then_inc(par_landed, 16)

            def mod_panel(k):
                r = mod_ring(k)
                if k >= MOD_FIRST and k - MOD_FIRST < RAW:
                    wait(sp, lo_ready, JMOD - RAW + (k - MOD_FIRST) + 1)
                else:
                    wait(sp, mod_step, 4 * (k - RAW + 1))
                sp.dma_start(raw[r % RAW][:, 0:DC * P], d["wmod"][k]).then_inc(raw_landed[r % RAW], 16)

            def panels(name, first=0, stop=None):
                g = GEMM[name]

                def body(i, u):
                    j, _, _, slot, _ = where(g, i, u)
                    p = 4 * i + u
                    if isinstance(p, int) and not first <= p < (stop or g.n):
                        return
                    if isinstance(j, int) and j < RAW:
                        wait(sp, mod_step, 4 * (MOD_FIRST - RAW + j + 1))
                    elif isinstance(j, int) and JMOD <= j < JMOD + RAW:
                        wait(sp, mod_step, 4 * (MOD_ALL - RAW + j - JMOD + 1))
                    else:
                        wait(sp, lo_ready, j - RAW + 1)
                    sp.dma_start(raw[slot][:, 0:g.kc * P], d[f"w{g.kc}"][g.at + 4 * i + u]).then_inc(raw_landed[slot], 16)

                each_panel(sp, g, body)

            for k in range(RAW):
                mod_panel(k)
            sp.dma_start(X[:, :, :], d["xt"]).then_inc(x_landed, 16)
            sp.dma_start(con[:, :], d["con"]).then_inc(par_landed, 16)
            for k in range(RAW, MOD_FIRST):
                mod_panel(k)
            panels("win0")
            panels("wout0", 0, 2)
            for k in range(MOD_FIRST, MOD_ALL):
                mod_panel(k)
            panels("wout0", 2)
            for g in GEMMS[2:12]:
                panels(g.name)
            for g in GEMMS[12:]:
                panels(g.name)
            for c in range(DC):
                sp.wait_ge(resid_ready, DC + c + 1)
                sp.dma_start(d["out"][:, c, :], X[:, c, 0:NX]).then_inc(out_landed, 16)
            sp.wait_ge(out_landed, 16 * DC)

        @block.gpsimd
        def _(pool):
            for g in GEMMS:
                def body(i, u, g=g):
                    j, b, _, slot, _ = where(g, i, u)
                    w = g.kc * P
                    pool.wait_ge(hi_ready, j + 1)
                    nc.gpsimd.tensor_tensor(wlo[b][:, 0:w], raw[slot][:, 0:w], whi[b][:, 0:w].bitcast(F32),
                                            ALU.subtract).then_inc(lo_ready, 1)
                each_panel(pool, g, body)

        @block.tensor
        def _(pe):
            n = dict(sq=0, inst=0, op=0, rope=0, unit=0, turn=0)

            xh, xl = (lambda k: XH[:, k, :]), (lambda k: XL[:, k, :])

            def big(name, xh, xl, width, ready=0, after=None):
                g = GEMM[name]

                def body(i, u):
                    j, b, used, _, _ = where(g, i, u)
                    p = 4 * i + u
                    pe.wait_ge(lo_ready, j + 1)
                    wait(pe, bank_free[b], used)
                    first = isinstance(p, int) and p == 0
                    tw = width(p) if callable(width) else width
                    segs = [s for s in SEGS if s[0] < tw]
                    for k in range(g.kc):
                        if first:
                            wait(pe, operand_lo, ready - g.kc + k + 1)
                        for q, (w, a) in enumerate(((whi, xh(k)), (whi, xl(k)), (wlo, xh(k)))):
                            for t0, tn in segs:
                                mm = pe.matmul(G[b][:, t0:t0 + tn], w[b][:, k * P:(k + 1) * P], a[:, t0:t0 + tn],
                                               start=(k == 0 and q == 0), stop=(k == g.kc - 1 and q == 2))
                    mm.then_inc(panel_done, 1)
                    if after is not None:
                        after(p)

                each_panel(pe, g, body)

            def rms(nchunks, width, sq_tiles, by_head=False, free=None):
                h, nb = (2, width // P) if by_head else (1, width // P)
                sel = co("half") if by_head else ones[:, 0:1]
                wait(pe, sd_ready, n["inst"])
                if free is not None:
                    free()
                for c in range(nchunks):
                    pe.wait_ge(sq_ready, n["sq"] + 1)
                    for tb in range(nb):
                        mm = pe.matmul(M0[:, SUMS + h * tb:SUMS + h * tb + h], sq_tiles[n["sq"] % 2][:, tb * P:(tb + 1) * P], sel,
                                       start=(c == 0 and tb == 0), stop=(c == nchunks - 1 and tb == nb - 1),
                                       skip_group_check=True)
                    mm.then_inc(sq_used, 1)
                    n["sq"] += 1
                pe.wait_ge(rs_ready, n["inst"] + 1)
                r = sq_tiles[2 + n["inst"] % 2]
                for tb in range(nb):
                    mm = pe.transpose(M0[:, tb * P:(tb + 1) * P], r[:, tb * P:(tb + 1) * P], ident)
                mm.then_inc(rb_ready, 1)
                n["inst"] += 1

            def turn(src, nb, free):
                free()
                half = 512 * (n["turn"] % 2) if nb == 4 else 0
                for tb in range(nb):
                    mm = pe.transpose(M0[:, half + tb * P:half + (tb + 1) * P], src[:, tb * P:(tb + 1) * P], ident)
                mm.then_inc(turned, 1)
                n["turn"] += 1

            def small_product(weights, source, segs, kc, m):
                wait(pe, operand_lo, n["op"])
                for k in range(kc):
                    for s, (t0, tn) in enumerate(segs):
                        mm = pe.matmul(M0[:, t0:t0 + tn], weights(k, m), source(k, s), start=(k == 0), stop=(k == kc - 1))
                mm.then_inc(mp_ready, 1)
                n["op"] += 1

            def rotate(chunk, perm):
                wait(pe, rope_done, n["rope"])
                o = M1[:, 0:NX] if len(chunk.shape) == 2 else M1[:, 0:NX].rearrange("p (a t) -> p a t", a=2)
                pe.matmul(o, perm, chunk, start=True, stop=True).then_inc(rot_ready, 1)
                n["rope"] += 1

            def attention(units, score, value, out, keys_tiles, ops_free):
                ends = head_ends(units)
                base = n["unit"]

                def scores(i):
                    wait(pe, exp_done, base + i - 1 if i >= 2 else base)
                    for mm in score(units[i], G[i % 2]):
                        pass
                    mm.then_inc(scores_ready, 1)

                def turn(i):
                    pe.wait_ge(probs_ready, base + i + 1)
                    wait(pe, probsT_copied, base + i)
                    for kb in range(units[i][3] // P):
                        mm = pe.transpose(M0[:, kb * P:(kb + 1) * P], keys_tiles[0][i % 2][:, kb * P:(kb + 1) * P], ident)
                    mm.then_inc(probsT_ready, 1)

                def weigh(i):
                    h, q0, k0, nk = units[i]
                    pe.wait_ge(probsT_copied, base + i + 1)
                    first = i == 0 or units[i - 1][0] != h
                    if first:
                        done = sum(1 for e in ends if e < i)
                        wait(pe, operand_lo, n["op"] + done - ops_free + 1)
                    o = out(h, q0)
                    for kb in range(nk // P):
                        mm = pe.matmul(o, value(h, k0 // P + kb), keys_tiles[1][i % 2][:, kb * P:(kb + 1) * P],
                                       start=(kb == 0), stop=(kb == nk // P - 1))
                    mm.then_inc(pv_done, 1)

                scores(0)
                for i in range(len(units)):
                    if i + 1 < len(units):
                        scores(i + 1)
                    turn(i)
                    if i >= 1:
                        weigh(i - 1)
                weigh(len(units) - 1)
                n["unit"] += len(units)
                n["op"] += len(ends)

            pe.wait_ge(par_landed, 32)

            for l in range(2):
                width, segs = tok(l)
                rms(DC, NT, W)
                n["op"] += DC
                big(f"win{l}", xh, xl, lambda p, l=l: win_width(l, p), ready=n["op"])
                g = GEMM[f"win{l}"]

                freed(pe, g.j0 + 7)
                pe.wait_ge(small_landed, 16 * (l + 1))
                freed(pe, g.j0 + 12)
                turn(W[5], NT // P, lambda: None)
                pe.wait_ge(turn_copied, n["turn"])
                nb = width // P
                fb = 6 * l
                for tb in range(nb):
                    wait(pe, ft_copied, fb + tb - 1)
                    for c in range(2):
                        mm = pe.matmul(M0[:, 512 * (tb % 2) + 256 * c:512 * (tb % 2) + 256 * c + 256],
                                       PR[:, c, tb * P:(tb + 1) * P], dftd, start=True, stop=True)
                    mm.then_inc(ft_ready, 1)
                freed(pe, g.j0 + g.n - 1)
                freed(pe, g.j0 + g.n - 2)
                for tb in range(nb):
                    pe.wait_ge(ft_copied, fb + tb + 1)
                    pe.wait_ge(dft_landed[tb % 2], 16 * ((fb + tb) // 2 + 1))
                    t0, tn = SEGS[tb // 4]
                    lastb = tb == 3 or tb == 5
                    for c in range(2):
                        for q in range(2):
                            mm = pe.matmul(G[c][:, t0:t0 + tn], ftok[:, tb * 512 + c * 256 + q * P:tb * 512 + c * 256 + (q + 1) * P],
                                           dft[tb % 2][:, q * tn:(q + 1) * tn], start=(tb in (0, 4) and q == 0),
                                           stop=(lastb and q == 1))
                    mm.then_inc(dft_used, 1)
                pe.wait_ge(fy_copied, 2 * (l + 1))
                for m in range(2):
                    small_product(lambda k, m: wf[:, k, m * P:(m + 1) * P], lambda k, s: PR[:, k, segs[s][0]:segs[s][0] + segs[s][1]],
                                  segs, 2, m)
                wait(pe, operand_lo, n["op"])

                for c in range(2, 6):
                    freed(pe, g.j0 + 6 + c)
                    rms(1, NT if l == 0 or c >= 4 else NX, W, True)
                    pe.wait_ge(qk_normed, 4 * l + c - 1)
                    rotate(PR[:, c, 0:NX], co("perm1"))
                pe.wait_ge(rope_done, n["rope"])

                def score1(unit, o):
                    h, q0, k0, nk = unit
                    part = slice(64 * (h % 2), 64 * (h % 2) + 64)
                    for c0 in range(0, nk, NX):
                        cn = min(NX, nk - c0)
                        yield pe.matmul(o[:, c0:c0 + cn], PR[part, 2 + h // 2, q0:q0 + P],
                                        PR[part, 4 + h // 2, k0 + c0:k0 + c0 + cn], start=True, stop=True)

                attention(units1(l), score1,
                          lambda h, kb: vtok[:, kb * P + 64 * (h // 2):kb * P + 64 * (h // 2) + 64],
                          lambda h, q0: M1[64 * (h % 2):64 * (h % 2) + 64, q0 % NX:q0 % NX + P],
                          (W[0:2], W[2:4]), 2)
                wait(pe, operand_lo, n["op"])

                pe.wait_ge(conv_tick, CONV * (2 * len(segs)) + (CONV * 4 if l else 0))
                for c in range(2):
                    for t0, tn in segs:
                        mm = pe.matmul(M0[:, t0:t0 + tn], ones, acc[:, c, t0:t0 + tn], start=(c == 0), stop=(c == 1))
                mm.then_inc(ln_sum, 1)
                rms(2, width, W)
                pe.wait_ge(ln_act, 2 * (l + 1))
                for m in range(2):
                    small_product(lambda k, m: wpw[:, k, m * P:(m + 1) * P], lambda k, s: acc[:, k, segs[s][0]:segs[s][0] + segs[s][1]],
                                  segs, 2, m)
                pe.wait_ge(pool_ready, 2 * (l + 1))
                for m in range(2):
                    small_product(lambda k, m: wpl[:, m, :], lambda k, s: pp[:, m, PP_AT[s]:PP_AT[s] + segs[s][1]], segs, 1, m)

                big(f"wout{l}", xh, xl, width, ready=n["op"])
                rms(DC, width, W)
                n["op"] += DC
                for half in range(2):
                    big(f"fin{l}{half}", xh, xl, width, ready=n["op"])
                    pe.wait_ge(h_lo, FH * (2 * l + half + 1))
                    big(f"fout{l}{half}", lambda k: HH[:, k, :], lambda k: HL[:, k, :], width, ready=n["op"])

            rms(DC, NX, W)
            n["op"] += DC
            big("eqk", xh, xl, NX, ready=n["op"])

            def turn_value(name, j):
                freed(pe, j)
                turn((vfD if name == "ov" else vfE)[j % 2], NX // P, lambda: wait(pe, turn_copied, n["turn"] - 1))

            def ev_after(p):
                if p >= 1:
                    turn_value("ev", GEMM["ev"].j0 + p - 1)
                rotate(QK[:, p, :], co("perm2"))
            big("ev", xh, xl, NX, ready=n["op"], after=ev_after)
            turn_value("ev", last("ev"))
            pe.wait_ge(turn_copied, n["turn"])
            pe.wait_ge(rope_done, n["rope"])

            def ret_score(h):
                part = slice(64 * (h % 2), 64 * (h % 2) + 64)
                wait(pe, ret_masked, h - 1)
                for jb, c0, cn in RET_AT:
                    o = G[h % 2][:, c0:c0 + cn] if c0 < 1024 else M0[:, 512 * (h % 2):512 * (h % 2) + cn]
                    mm = pe.matmul(o, QK[part, 4 + h // 2, jb * P:(jb + 1) * P], QK[part, h // 2, jb * P:NX],
                                   start=True, stop=True)
                mm.then_inc(ret_scores, 1)

            ret_score(0)
            for h in range(8):
                if h < 7:
                    ret_score(h + 1)
                pe.wait_ge(ret_masked, h + 1)
                wait(pe, ret_copied, h - 1)
                o = (M1, MM)[h % 2]
                for q, (jb, c0, cn) in enumerate(RET_AT):
                    mm = pe.matmul(o[:, jb * P:NX], VE[:, jb, h * P:(h + 1) * P], scT[h % 2][:, c0:c0 + cn],
                                   start=(q == 0), stop=(q == 3))
                mm.then_inc(ret_pv, 1)
            for h in range(8):
                rms(1, NX, W, free=lambda: wait(pe, ret_normed, h))
            big("eg", xh, xl, NX, ready=n["op"])
            n["op"] += 8
            big("eout0", lambda k: MH[:, k, :], lambda k: ML[:, k, :], NX, ready=n["op"])
            big("econv", xh, xl, NX, ready=n["op"])
            n["op"] += 8
            big("eout1", lambda k: MH[:, k, :], lambda k: ML[:, k, :], NX, ready=n["op"])
            rms(DC, NX, W)

            rms(DC, NX, W, free=lambda: pe.wait_ge(resid_ready, 1))
            n["op"] += DC
            big("oin", xh, xl, NX, ready=n["op"])
            freed(pe, GEMM["oin"].j0 + 5)
            rms(3, NX, WL)
            rms(2, NX, WL, free=lambda: pe.wait_ge(t_ready, 8 * DC + 3))
            n["op"] += 5
            rotate(kr[:, 0:NX], co("perm2"))
            big("oq", xh, xl, NX, ready=n["op"] - 2)
            for c in range(4):
                freed(pe, GEMM["oq"].j0 + 8 + c)
                rotate(QR[:, 2 * c:2 * c + 2, :], co("perm2"))
            big("ok", lambda k: XH[:, 3 + k, :], lambda k: XL[:, 3 + k, :], NX, ready=n["op"])
            big("ov", lambda k: XH[:, 3 + k, :], lambda k: XL[:, 3 + k, :], NX, ready=n["op"],
                after=lambda p: turn_value("ov", GEMM["ov"].j0 + p - 1) if p else None)
            turn_value("ov", last("ov"))
            pe.wait_ge(turn_copied, n["turn"])
            pe.wait_ge(rope_done, n["rope"])

            def score2(unit, o):
                h, q0, _, nk = unit
                part = slice(64 * (h % 2), 64 * (h % 2) + 64)
                yield pe.matmul(o[:, 0:nk], QN[:, h, q0:q0 + P], KN[:, h, 0:nk], start=True, stop=False)
                piece = QR[part, 2 * (h // 2) + q0 // 256, q0 % 256:q0 % 256 + P]
                yield pe.matmul(o[:, 0:nk], piece, kr[part, 0:nk], start=False, stop=True)

            attention(units2, score2, lambda h, kb: VO[:, kb, h * P:(h + 1) * P],
                      lambda h, q0: (M1, MM)[h % 2][:, q0:q0 + P], (dprobs, dprobsT), 2)
            big("oout", xh, xl, NX, ready=n["op"])
            rms(DC, NX, WY)

        @block.scalar
        def _(act):
            n = dict(sq=0, inst=0, op=0, mp=0, t=0, unit=0, turn=0)
            eps = co("eps")

            def high(j_static, rnd):
                if j_static >= NPANEL:
                    return
                w = KC_OF[j_static] * P
                act.wait_ge(raw_landed[j_static % RAW], 16 * (rnd + 1))
                nc.scalar.activation(whi[j_static % 2][:, 0:w], raw[j_static % RAW][:, 0:w], ACT.Copy).then_inc(hi_ready, 1)

            def stage(name, evac=None, after=None):
                g = GEMM[name]

                def body(i, u):
                    j, b, _, _, _ = where(g, i, u)
                    act.wait_ge(panel_done, j + 1)
                    if evac is not None:
                        evac(i, u, G[b], bank_free[b])
                    js = g.j0 + u + (4 * i if isinstance(i, int) else 4)
                    high(js + 2, (g.j0 + u + 2) // RAW + i + ring_shift(js + 2))
                    if after is not None:
                        after(i, u)

                each_panel(act, g, body)

            def rms(sources, width, Wt, ready):
                for c, src in enumerate(sources):
                    ready(c)
                    wait(act, sq_used, n["sq"] - 1)
                    nc.scalar.activation(Wt[n["sq"] % 2][:, 0:width], src, ACT.Square).then_inc(sq_ready, 1)
                    n["sq"] += 1

            def root(width, dim, heads=1):
                act.wait_ge(sq_used, n["sq"])
                wait(act, rs_ready, n["inst"] - 1)
                k, a = heads * width // P, 12 * (n["inst"] % 2)
                nc.scalar.activation(rootT[:, a:a + k], M0[:, SUMS:SUMS + k], ACT.Sqrt, bias=eps,
                                     scale=1.0 / dim).then_inc(sd_ready, 1)
                n["inst"] += 1

            def high_operand(dst, src, scale=None):
                if scale is None:
                    nc.scalar.activation(dst, src, ACT.Copy).then_inc(operand_hi, 1)
                else:
                    nc.scalar.activation(dst, src, ACT.Copy, scale=scale).then_inc(operand_hi, 1)
                n["op"] += 1

            def norm_mod(l, which, width, ready):
                rms([X[:, c, 0:width] for c in range(DC)], width, W, ready)
                root(width, 1024)
                for c in range(DC):
                    act.wait_ge(t_ready, n["t"] + 1)
                    n["t"] += 1
                    for s, (t0, tn) in enumerate([s for s in SEGS if s[0] < width]):
                        m = 2 * ((24 if which else 0) + c) + s
                        ins = nc.scalar.activation(XH[:, c, t0:t0 + tn], W[4 + c % 4][:, t0:t0 + tn], ACT.Identity,
                                                   bias=pa(f"mod{l}")[:, m:m + 1])
                    ins.then_inc(operand_hi, 1)
                    n["op"] += 1

            def norm_plain(sources, dim, Wt, ready, dst):
                rms(sources, NX, Wt, ready)
                root(NX, dim)
                for c in range(len(sources)):
                    act.wait_ge(t_ready, n["t"] + 1)
                    n["t"] += 1
                    high_operand(XH[:, dst + c, 0:NX], Wt[6 + c % 2][:, 0:NX])

            def mix_out(dst, width, scale=None):
                act.wait_ge(mp_ready, n["mp"] + 1)
                n["mp"] += 1
                high_operand(dst[:, 0:width], M0[:, 0:width], scale)

            def attention(units, scale, tiles, finish):
                ends = head_ends(units)
                base = n["unit"]

                def exps(i):
                    nk = units[i][3]
                    act.wait_ge(negmax_ready, base + i + 1)
                    wait(act, probsT_ready, base + i - 1 if i >= 2 else base)
                    s = (base + i) % 4
                    nc.scalar.activation(tiles[0][i % 2][:, 0:nk], G[i % 2][:, 0:nk], ACT.Exp, bias=stat[:, 4 + s:5 + s],
                                         scale=scale, accum_out=stat[:, 8 + s:9 + s]).then_inc(exp_done, 1)

                def copies(i):
                    nk = units[i][3]
                    act.wait_ge(probsT_ready, base + i + 1)
                    wait(act, pv_done, base + i - 1 if i >= 2 else base)
                    nc.scalar.activation(tiles[1][i % 2][:, 0:nk], M0[:, 0:nk], ACT.Copy).then_inc(probsT_copied, 1)

                def end(i):
                    if i in ends:
                        act.wait_ge(pv_done, base + i + 1)
                        finish(*ends[i])

                exps(0)
                for i in range(len(units)):
                    if i + 1 < len(units):
                        exps(i + 1)
                    copies(i)
                    if i >= 1:
                        end(i - 1)
                end(len(units) - 1)
                n["unit"] += len(units)

            act.wait_ge(c_landed, 16)
            nc.scalar.activation(silu_c[:, :], silu_c[:, :], ACT.Silu).then_inc(c_ready, 1)
            act.wait_ge(par_landed, 32)
            high(0, ring_shift(0))
            high(1, ring_shift(0))
            act.wait_ge(x_landed, 16)

            for l in range(2):
                width, segs = tok(l)
                nseg = len(segs)

                def whole(c, l=l):
                    if l == 1 and c == 0:
                        freed(act, last("fout01"))
                        freed(act, last("fout01") - 1)
                norm_mod(l, 0, NT, whole)
                act.dma_start(cosT[:, :], d["cosx"]).then_inc(rope_landed, 16)
                act.dma_start(sinT[:, :], d["sinx"]).then_inc(rope_landed, 16)
                act.dma_start(smallw[:, :], d["small"][l]).then_inc(small_landed, 16)

                def win_out(i, u, src, free, l=l, segs=segs):
                    p = 4 * i + u
                    tw = win_width(l, p)
                    if p in (0, 2):
                        if p == 2:
                            freed(act, GEMM[f"win{l}"].j0 + 1)
                        ins = nc.scalar.activation(pA[:, 0:tw], src[:, 0:tw], ACT.Sigmoid)
                    elif p in (1, 3):
                        return
                    elif p in (4, 5):
                        for s, (t0, tn) in enumerate(segs):
                            ins = nc.scalar.activation(pp[:, p - 4, PP_AT[s]:PP_AT[s] + tn], src[:, t0:t0 + tn], ACT.Copy)
                    elif p < 12:
                        ins = nc.scalar.activation(PR[:, p - 6, 0:tw], src[:, 0:tw], ACT.Copy)
                    else:
                        ins = nc.scalar.activation(W[5][:, 0:tw], src[:, 0:tw], ACT.Copy)
                    ins.then_inc(free, 1)

                stage(f"win{l}", win_out)
                n["turn"] += 1
                act.wait_ge(turned, n["turn"])
                nc.scalar.activation(vtok[:, 0:NT], M0[:, 0:NT], ACT.Copy).then_inc(turn_copied, 1)

                nb, fb = width // P, 6 * l
                for tb in range(2):
                    act.dma_start(dft[tb][:, 0:1024], d["dftx"][tb]).then_inc(dft_landed[tb % 2], 16)
                for tb in range(nb):
                    act.wait_ge(ft_ready, fb + tb + 1)
                    nc.scalar.activation(ftok[:, tb * 512:(tb + 1) * 512], M0[:, 512 * (tb % 2):512 * (tb % 2) + 512],
                                         ACT.Copy).then_inc(ft_copied, 1)
                for tb in range(2, nb):
                    act.wait_ge(dft_used, fb + tb - 1)
                    if tb < 4:
                        act.dma_start(dft[tb % 2][:, 0:1024], d["dftx"][tb]).then_inc(dft_landed[tb % 2], 16)
                    else:
                        act.dma_start(dft[tb % 2][:, 0:512], d["dftc"][tb - 4]).then_inc(dft_landed[tb % 2], 16)
                act.wait_ge(dft_used, fb + nb)
                for c in range(2):
                    nc.scalar.activation(PR[:, c, 0:width], G[c][:, 0:width], ACT.Copy).then_inc(fy_copied, 1)
                for m in range(2):
                    mix_out(XH[:, 2 + m, :], width)

                for c in range(2, 6):
                    tw = NT if l == 0 or c >= 4 else NX
                    rms([PR[:, c, 0:tw]], tw, W, lambda _, c=c: freed(act, GEMM[f"win{l}"].j0 + 6 + c))
                    root(tw, 64, 2)

                def finish1(h, q0, qn):
                    part = slice(64 * (h % 2), 64 * (h % 2) + 64)
                    high_operand(XH[part, h // 2, q0:q0 + qn], M1[part, 0:qn])

                attention(units1(l), 0.125, (W[0:2], W[2:4]), finish1)

                act.wait_ge(ln_centered, l + 1)
                rms([acc[:, c, 0:width] for c in range(2)], width, W, lambda c: None)
                root(width, 256)
                for c in range(2):
                    act.wait_ge(ln_scaled, 2 * l + c + 1)
                    nc.scalar.activation(acc[:, c, 0:width], acc[:, c, 0:width], ACT.Silu, scale=pa(f"lng{l}")[:, c:c + 1],
                                         bias=pa(f"lnb{l}")[:, c:c + 1]).then_inc(ln_act, 1)
                for m in range(2):
                    mix_out(XH[:, 4 + m, :], width)
                for m in range(2):
                    mix_out(XH[:, 6 + m, :], width, pa(f"psc{l}")[:, m:m + 1])

                stage(f"wout{l}")
                norm_mod(l, 1, width, lambda c, l=l: freed(act, GEMM[f"wout{l}"].j0 + c))

                for half in range(2):
                    g = GEMM[f"fin{l}{half}"]

                    def silu(i, u, src, free, g=g):
                        if u % 2 == 0:
                            wait(act, bank_free[(g.j0 + u - 1) % 2], (g.j0 + u - 1) // 2 + 2 * i + 1)
                            nc.scalar.activation(fsilu[:, 0:width], src[:, 0:width], ACT.Silu).then_inc(free, 1)

                    def hidden(i, u, g=g):
                        if u % 2:
                            _, b, used, _, _ = where(g, i, u)
                            act.wait_ge(bank_free[b], used + 1)
                            nc.scalar.activation(HH[:, 2 * i + u // 2, 0:width], fh[:, 0:width], ACT.Copy).then_inc(h_hi, 1)

                    def mod_load(i, u, base, count):
                        if isinstance(i, int) and 4 * i + u >= count:
                            return
                        wait(act, mod_step, 4 * (MOD_ALL + base + 4 * i + u))
                        for q in range(2):
                            act.dma_start(mod_half[q][:, :], d["wmod"][MOD_ALL + base + 4 * i + u, :, q * NX:(q + 1) * NX]
                                          ).then_inc(half_landed[q], 16)

                    def hidden_and_mod(i, u, hidden=hidden, half=half):
                        if l == 0:
                            mod_load(i, u, 30 * half, 22)
                        hidden(i, u)

                    stage(g.name, silu, hidden_and_mod)
                    stage(f"fout{l}{half}", None, (lambda i, u, half=half: mod_load(i, u, 22 + 30 * half, 4 if half else 8))
                          if l == 0 else None)

            act.wait_ge(rope_done, 8)
            act.dma_start(sinT[:, :].bitcast(I32), d["pos"]).then_inc(rope_landed, 16)
            norm_plain([X[:, c, 0:NX] for c in range(DC)], 1024, W,
                       lambda c: (freed(act, last("fout11")), freed(act, last("fout11") - 1)) if c == 0 else None, 0)
            act.wait_ge(trig, 2)
            nc.scalar.activation(sinT[:, :], W[0][:, 0:NX], ACT.Sin).then_inc(act_step, 1)
            nc.scalar.activation(cosT[:, :], W[1][:, 0:NX], ACT.Sin).then_inc(act_step, 1)
            stage("eqk", lambda i, u, src, free: nc.scalar.activation(QK[:, 4 * i + u, :], src[:, 0:NX], ACT.Copy).then_inc(free, 1))
            for h in range(2):
                act.dma_start(decay[h][:, :], d["decay"][h]).then_inc(decay_landed[h], 16)

            def value_stage(name, tiles, dst):
                def out(i, u, src, free):
                    nc.scalar.activation(tiles[(GEMM[name].j0 + u) % 2][:, 0:NX], src[:, 0:NX], ACT.Copy).then_inc(free, 1)

                def by_token(p):
                    act.wait_ge(turned, n["turn"] + 1)
                    nc.scalar.activation(dst[:, :, p * P:(p + 1) * P],
                                         M0[:, 512 * (n["turn"] % 2):512 * (n["turn"] % 2) + 512].rearrange("p (b f) -> p b f", b=4),
                                         ACT.Copy).then_inc(turn_copied, 1)
                    n["turn"] += 1
                stage(name, out, lambda i, u: by_token(4 * i + u - 1) if 4 * i + u else None)
                by_token(7)

            value_stage("ev", vfE, VE)
            for h in range(8):
                act.wait_ge(ret_pv, h + 1)
                nc.scalar.activation(RT[:, h, :], (M1, MM)[h % 2][:, 0:NX], ACT.Copy).then_inc(ret_copied, 1)
                if h + 2 < 8:
                    act.wait_ge(ret_masked, h + 1)
                    act.dma_start(decay[h % 2][:, :], d["decay"][h + 2]).then_inc(decay_landed[h % 2], 16)
            for h in range(8):
                rms([RT[:, h, :]], NX, W, lambda _: act.wait_ge(ret_copied, 8))
                root(NX, 128)

            def eg_out(i, u, src, free):
                wait(act, t_ready, n["t"] - 1)
                nc.scalar.activation(W[4 + u % 2][:, 0:NX], src[:, 0:NX], ACT.Silu).then_inc(free, 1)

            def eg_high(i, u):
                act.wait_ge(t_ready, n["t"] + 1)
                n["t"] += 1
                high_operand(MH[:, 4 * i + u, :], W[6 + u % 2][:, 0:NX])
            stage("eg", eg_out, eg_high)
            stage("eout0")
            t0, op0 = n["t"], n["op"]

            def ce_out(i, u, src, free):
                if u == 3:
                    wait(act, t_ready, t0 + i)
                    nc.scalar.activation(ce_s[:, 0:NX], src[:, 0:NX], ACT.Silu).then_inc(free, 1)

            def ce_high(i, u):
                if u == 3:
                    act.wait_ge(t_ready, t0 + i + 1)
                    nc.scalar.activation(MH[:, i, :], ce_z[:, 0:NX], ACT.Copy).then_inc(operand_hi, 1)
            stage("econv", ce_out, ce_high)
            n["t"] += 8
            n["op"] += 8
            stage("eout1")
            rms([Y[:, c, :] for c in range(DC)], NX, W, lambda c: freed(act, last("eout1") - 7 + c))
            root(NX, 1024)

            norm_plain([X[:, c, 0:NX] for c in range(DC)], 1024, W, lambda c: act.wait_ge(resid_ready, c + 1), 0)

            def oin_out(i, u, src, free):
                p = 4 * i + u
                dst = LAT[:, p, :] if p < 5 else kr[:, 0:NX] if p == 5 else SG[:, p - 6, :]
                nc.scalar.activation(dst, src[:, 0:NX], ACT.Silu if p > 5 else ACT.Copy).then_inc(free, 1)
            stage("oin", oin_out)
            norm_plain([LAT[:, c, :] for c in range(3)], 384, WL, lambda c: freed(act, GEMM["oin"].j0 + c), 0)
            norm_plain([LAT[:, c, :] for c in range(3, 5)], 256, WL, lambda c: freed(act, GEMM["oin"].j0 + 3 + c), 3)

            def oq_out(i, u, src, free):
                p = 4 * i + u
                if p < 8:
                    nc.scalar.activation(QN[:, p, :], src[:, 0:NX], ACT.Copy).then_inc(free, 1)
                else:
                    nc.scalar.activation(QR[:, 2 * (p - 8):2 * (p - 8) + 2, :],
                                         src[:, 0:NX].rearrange("p (a t) -> p a t", a=2), ACT.Copy).then_inc(free, 1)
            act.wait_ge(operand_lo, n["op"])
            stage("oq", oq_out)
            stage("ok", lambda i, u, src, free: nc.scalar.activation(KN[:, 4 * i + u, :], src[:, 0:NX], ACT.Copy).then_inc(free, 1))

            act.wait_ge(rope_done, 8 + 8 + 5)
            value_stage("ov", vfD, VO)
            gates = [0]

            def finish2(h, q0, qn):
                gates[0] += 1
                act.wait_ge(gated, gates[0])
                high_operand(XH[:, h, 0:NX], SG[:, h, :])
            attention(units2, 192.0 ** -0.5, (dprobs, dprobsT), finish2)
            stage("oout")
            rms([Y2[:, c, :] for c in range(DC)], NX, WY, lambda c: freed(act, last("oout") - 7 + c))
            root(NX, 1024)

        @block.vector
        def _(dve):
            n = dict(inst=0, op=0, t=0, step=0, rope=0, unit=0)

            def link(ins):
                n["step"] += 1
                ins.then_inc(dve_step, 1)
                dve.wait_ge(dve_step, n["step"])

            def invert(width, Wt, heads=1):
                dve.wait_ge(sd_ready, n["inst"] + 1)
                k, a = heads * width // P, 12 * (n["inst"] % 2)
                r = rootT[:, a:a + k]
                wait(dve, rb_ready, n["inst"] - 1)
                link(nc.vector.reciprocal(r, r))
                nc.vector.tensor_copy(Wt[2 + n["inst"] % 2][:, 0:width].rearrange("p (k f) -> p k f", k=k),
                                      r.unsqueeze(2).broadcast_to([P, k, P // heads])).then_inc(rs_ready, 1)
                n["inst"] += 1
                dve.wait_ge(rb_ready, n["inst"])
                return M0[:, 0:width]

            def low_operand(dst, src, hi, scale=None):
                dve.wait_ge(operand_hi, n["op"] + 1)
                if scale is None:
                    ins = nc.vector.tensor_tensor(dst, src, hi.bitcast(F32), ALU.subtract)
                else:
                    ins = nc.vector.scalar_tensor_tensor(dst, src, scale, hi.bitcast(F32), ALU.mult, ALU.subtract)
                ins.then_inc(operand_lo, 1)
                n["op"] += 1

            def norm_mod(l, which, width):
                r = invert(width, W)
                ws = [s for s in SEGS if s[0] < width]

                def low(c):
                    dve.wait_ge(operand_hi, n["op"] + 1)
                    for s, (t0, tn) in enumerate(ws):
                        m = 2 * ((24 if which else 0) + c) + s
                        ins = nc.vector.scalar_tensor_tensor(XL[:, c, t0:t0 + tn], W[4 + c % 4][:, t0:t0 + tn],
                                                             pa(f"mod{l}")[:, m:m + 1],
                                                             XH[:, c, t0:t0 + tn].bitcast(F32), ALU.add, ALU.subtract)
                    ins.then_inc(operand_lo, 1)
                    n["op"] += 1

                for c in range(DC):
                    if c >= 4:
                        dve.wait_ge(operand_lo, n["op"] - 1)
                    for s, (t0, tn) in enumerate(ws):
                        a = 16 * which + 8 * s + c
                        ins = nc.vector.scalar_tensor_tensor(W[4 + c % 4][:, t0:t0 + tn], X[:, c, t0:t0 + tn], afac[:, a:a + 1],
                                                             r[:, t0:t0 + tn], ALU.mult, ALU.mult)
                    ins.then_inc(t_ready, 1)
                    n["t"] += 1
                    if c:
                        low(c - 1)
                low(DC - 1)

            def norm_plain(sources, gain, Wt, dst):
                r = invert(NX, Wt)
                k = len(sources)
                for c in range(k + 1):
                    if c < k:
                        wait(dve, operand_lo, n["op"] - (1 if c < 2 else 0))
                        nc.vector.scalar_tensor_tensor(Wt[6 + c % 2][:, 0:NX], sources[c], gain[:, c:c + 1], r,
                                                       ALU.mult, ALU.mult).then_inc(t_ready, 1)
                        n["t"] += 1
                    if c:
                        low_operand(XL[:, dst + c - 1, 0:NX], Wt[6 + (c - 1) % 2][:, 0:NX], XH[:, dst + c - 1, 0:NX])

            def norm_post(Yt, gain, Wt):
                r = invert(NX, Wt)
                for c in range(DC):
                    t = Wt[4 + c % 2][:, 0:NX]
                    link(nc.vector.scalar_tensor_tensor(t, Yt[:, c, :], gain[:, c:c + 1], r, ALU.mult, ALU.mult))
                    nc.vector.tensor_tensor(X[:, c, 0:NX], X[:, c, 0:NX], t, ALU.add).then_inc(resid_ready, 1)

            def rope(chunk, tmp, three=False):
                view = (lambda a: a.rearrange("p (a t) -> p a t", a=2)) if three else (lambda a: a)
                dve.wait_ge(rot_ready, n["rope"] + 1)
                n["rope"] += 1
                link(nc.vector.tensor_tensor(view(tmp), view(M1[:, 0:NX]), view(sinT[:, :]), ALU.mult))
                link(nc.vector.tensor_tensor(chunk, chunk, view(cosT[:, :]), ALU.mult))
                nc.vector.tensor_tensor(chunk, chunk, view(tmp), ALU.add).then_inc(rope_done, 1)

            def mod_product(k, u, halves, landed):
                for q in range(2):
                    dve.wait_ge(*landed(q))
                    wait(dve, mod_step, 4 * k + 2 * q)
                    if not (isinstance(k, int) and k in MOD_STARTS):
                        add_sums(k - 1, 1 - u % 2, q)
                    for s in range(2):
                        nc.vector.tensor_tensor_reduce((MM[:, 0:NX], halves[q])[s], halves[q],
                                                       silu_c[:, 1024 * s + NX * q:1024 * s + NX * (q + 1)], 1.0, 0.0, ALU.mult,
                                                       ALU.add, sums[:, 4 * (u % 2) + 2 * q + s:4 * (u % 2) + 2 * q + s + 1]
                                                       ).then_inc(mod_step, 1)

            def add_sums(k, slot, q):
                col = par[:, bass.ds(2 * k + PAR["mod0"][0], 2)]
                return nc.vector.tensor_tensor(col, col, sums[:, 4 * slot + 2 * q:4 * slot + 2 * q + 2], ALU.add)

            def last_sums(k):
                dve.wait_ge(mod_step, 4 * (k + 1))
                for q in range(2):
                    link(add_sums(k, k % 2, q))

            def ring_mod(k):
                r = mod_ring(k)
                src = raw[r % RAW]
                mod_product(k, k, (src[:, 0:NX], src[:, NX:2 * NX]), lambda q: (raw_landed[r % RAW], 16 * (r // RAW + 1)))

            def half_mod(i, u, base, count):
                if isinstance(i, int) and 4 * i + u >= count:
                    return
                mod_product(4 * i + (MOD_ALL + base + u), u, [m[:, :] for m in mod_half],
                            lambda q: (half_landed[q], 64 * i + 16 * (base + u + 1)))
                if isinstance(i, int) and 4 * i + u == count - 1:
                    last_sums(MOD_ALL + base + count - 1)

            def modulation(l, which):
                m3 = pa(f"mod{l}").rearrange("p (m s) -> p m s", s=2)
                for s in range(2):
                    ins = nc.vector.scalar_tensor_tensor(afac[:, 16 * which + 8 * s:16 * which + 8 * s + 8],
                                                         m3[:, 8 + 24 * which:16 + 24 * which, s], 1.0,
                                                         pa(("g1", "g2")[which] + str(l)), ALU.add, ALU.mult)
                link(ins)

            def gated_add(name, l, segs, m0, after=None):
                g = GEMM[name]
                for p in range(g.n):
                    j, b, _, _, _ = where(g, 0, p)
                    dve.wait_ge(panel_done, j + 1)
                    for s, (t0, tn) in enumerate(segs):
                        col = 2 * (m0 + p) + s
                        ins = nc.vector.scalar_tensor_tensor(X[:, p, t0:t0 + tn], G[b][:, t0:t0 + tn],
                                                             pa(f"mod{l}")[:, col:col + 1],
                                                             X[:, p, t0:t0 + tn], ALU.mult, ALU.add)
                    ins.then_inc(bank_free[b], 1)
                    if after is not None:
                        after(p)

            def attention(units, scale, tiles, finish, masked, beside=None):
                ends = head_ends(units)
                base = n["unit"]

                def tops(i):
                    nk = units[i][3]
                    s = (base + i) % 4
                    dve.wait_ge(scores_ready, base + i + 1)
                    if masked:
                        diag = G[i % 2][:, nk - P:nk]
                        link(nc.vector.tensor_tensor(diag, diag, co("mask"), ALU.add))
                    link(nc.vector.tensor_reduce(stat[:, s:s + 1], G[i % 2][:, 0:nk], AX.X, ALU.max))
                    nc.vector.tensor_scalar(stat[:, 4 + s:5 + s], stat[:, s:s + 1], -scale, None, ALU.mult).then_inc(negmax_ready, 1)

                def norms(i):
                    nk = units[i][3]
                    s = (base + i) % 4
                    t = tiles[0][i % 2][:, 0:nk]
                    dve.wait_ge(exp_done, base + i + 1)
                    link(nc.vector.reciprocal(stat[:, 12 + s:13 + s], stat[:, 8 + s:9 + s]))
                    nc.vector.tensor_scalar(t, t, stat[:, 12 + s:13 + s], None, ALU.mult).then_inc(probs_ready, 1)

                tops(0)
                for i in range(len(units)):
                    if i + 1 < len(units):
                        tops(i + 1)
                    norms(i)
                    if beside is not None:
                        beside(i)
                    if i - 1 in ends:
                        finish(base + i, *ends[i - 1])
                finish(base + len(units), *ends[len(units) - 1])
                n["unit"] += len(units)

            dve.wait_ge(par_landed, 32)
            dve.wait_ge(c_ready, 1)
            for k in range(MOD_FIRST):
                ring_mod(k)
            last_sums(MOD_FIRST - 1)
            modulation(0, 0)
            dve.wait_ge(x_landed, 16)
            for l in range(2):
                width, segs = tok(l)
                norm_mod(l, 0, NT)
                g = GEMM[f"win{l}"]
                for c in range(2):
                    for a, b_ in ((0, HALO), (GLU_AT[0] + NX, GLU_AT[1]), (GLU_AT[1] + NC, GLU_W)):
                        nc.vector.memset(glu[:, c, a:b_], 0.0)
                    for a, b_ in ((0, POOLPAD), (PP_AT[0] + NX, PP_AT[1]), (PP_AT[1] + NC, PP_W)):
                        ins = nc.vector.memset(pp[:, c, a:b_], 0.0)
                    if l == 1:
                        nc.vector.memset(glu[:, c, GLU_AT[1]:GLU_AT[1] + NC], 0.0)
                        ins = nc.vector.memset(pp[:, c, PP_AT[1]:PP_AT[1] + NC], 0.0)
                link(ins)
                for c in range(2):
                    j, b = g.j0 + 2 * c + 1, (g.j0 + 2 * c + 1) % 2
                    dve.wait_ge(panel_done, j + 1)
                    freed(dve, j - 1)
                    for s, (t0, tn) in enumerate(segs):
                        ins = nc.vector.tensor_tensor(glu[:, c, GLU_AT[s]:GLU_AT[s] + tn], G[b][:, t0:t0 + tn],
                                                      pA[:, t0:t0 + tn], ALU.mult)
                    ins.then_inc(bank_free[b], 1)
                freed(dve, g.j0 + 1)
                freed(dve, g.j0 + 3)

                runs = [(c, s, t0, tn) for c in range(2) for s, (t0, tn) in enumerate(segs)]
                per, base = len(runs), (CONV * 4 if l else 0)
                dwa, dwba = PAR[f"dw{l}"][0], PAR[f"dwb{l}"][0]
                for c, s, t0, tn in runs:
                    a = GLU_AT[s] - HALO
                    nc.vector.tensor_scalar(acc[:, c, t0:t0 + tn], glu[:, c, a:a + tn], par[:, dwa + c * CONV:dwa + c * CONV + 1],
                                            par[:, dwba + c:dwba + c + 1], ALU.mult, ALU.add).then_inc(conv_tick, 1)
                with dve.Fori(1, CONV) as tap:
                    for k, (c, s, t0, tn) in enumerate(runs):
                        dve.wait_ge(conv_tick, per * tap + (base - per + k + 1))
                        nc.vector.scalar_tensor_tensor(acc[:, c, t0:t0 + tn], glu[:, c, bass.ds(tap + (GLU_AT[s] - HALO), tn)],
                                                       par[:, bass.ds(tap + (dwa + c * CONV), 1)], acc[:, c, t0:t0 + tn],
                                                       ALU.mult, ALU.add).then_inc(conv_tick, 1)

                for c in range(2):
                    freed(dve, g.j0 + 4 + c)
                    u, hi_part, lo_part = pp[:, c, :], slice(64, P), slice(0, 64)
                    e = PP_W
                    link(nc.vector.tensor_tensor(pA[:, 1:e], u[:, 0:e - 1], u[:, 1:e], ALU.add))
                    if c == 0:
                        nc.vector.tensor_tensor(pB[hi_part, 2:e - 2], pA[hi_part, 1:e - 3], pA[hi_part, 3:e - 1], ALU.add)
                        link(nc.vector.tensor_copy(pB[lo_part, 2:e - 2], pA[lo_part, 2:e - 2]))
                    else:
                        link(nc.vector.tensor_tensor(pB[:, 2:e - 2], pA[:, 1:e - 3], pA[:, 3:e - 1], ALU.add))
                        link(nc.vector.tensor_tensor(pA[:, 4:e - 4], pB[:, 2:e - 6], pB[:, 6:e - 2], ALU.add))
                        nc.vector.tensor_tensor(pB[hi_part, 8:e - 8], pA[hi_part, 4:e - 12], pA[hi_part, 12:e - 4], ALU.add)
                        link(nc.vector.tensor_copy(pB[lo_part, 8:e - 8], pA[lo_part, 8:e - 8]))
                    for s, (t0, tn) in enumerate(segs):
                        a = PP_AT[s]
                        for side, q in enumerate((a, a + tn - 8)):
                            tab = co("edge")[:, 16 * c + 8 * side:16 * c + 8 * side + 8]
                            ins = nc.vector.tensor_tensor(pB[:, q:q + 8], pB[:, q:q + 8], tab, ALU.mult)
                    link(ins)
                    for s, (t0, tn) in enumerate(segs):
                        a = PP_AT[s]
                        ins = nc.vector.scalar_tensor_tensor(pp[:, c, a:a + tn], pB[:, a:a + tn], co("invw")[:, c:c + 1],
                                                             pp[:, c, a:a + tn], ALU.mult, ALU.subtract)
                    ins.then_inc(pool_ready, 1)
                dve.wait_ge(pool_ready, 2 * (l + 1))

                for m in range(2):
                    low_operand(XL[:, 2 + m, 0:width], M0[:, 0:width], XH[:, 2 + m, 0:width])

                dve.wait_ge(rope_landed, 32 * (l + 1))
                for c in range(2, 6):
                    tw = NT if l == 0 or c >= 4 else NX
                    r = invert(tw, W, 2)
                    nc.vector.scalar_tensor_tensor(PR[:, c, 0:tw], PR[:, c, 0:tw], pa(f"qg{l}" if c < 4 else f"kg{l}"), r,
                                                   ALU.mult, ALU.mult).then_inc(qk_normed, 1)
                    rope(PR[:, c, 0:NX], W[4][:, 0:NX])

                def finish1(_, h, q0, qn):
                    part = slice(64 * (h % 2), 64 * (h % 2) + 64)
                    low_operand(XL[part, h // 2, q0:q0 + qn], M1[part, 0:qn], XH[part, h // 2, q0:q0 + qn])

                attention(units1(l), 0.125, (W[0:2], W[2:4]), finish1, False,
                          (lambda i: ring_mod(MOD_FIRST + i)) if l == 0 else None)

                dve.wait_ge(ln_sum, l + 1)
                for c in range(2):
                    ins = nc.vector.scalar_tensor_tensor(acc[:, c, 0:width], M0[:, 0:width], -1.0 / 256, acc[:, c, 0:width],
                                                         ALU.mult, ALU.add)
                ins.then_inc(ln_centered, 1)
                dve.wait_ge(ln_centered, l + 1)
                r = invert(width, W)
                for c in range(2):
                    nc.vector.tensor_tensor(acc[:, c, 0:width], acc[:, c, 0:width], r, ALU.mult).then_inc(ln_scaled, 1)
                for m in range(2):
                    low_operand(XL[:, 4 + m, 0:width], M0[:, 0:width], XH[:, 4 + m, 0:width])
                for m in range(2):
                    low_operand(XL[:, 6 + m, 0:width], M0[:, 0:width], XH[:, 6 + m, 0:width], pa(f"psc{l}")[:, m:m + 1])

                if l == 0:
                    last_sums(MOD_ALL - 1)
                    modulation(0, 1)
                gated_add(f"wout{l}", l, segs, 16)
                freed(dve, last(f"wout{l}"))
                freed(dve, last(f"wout{l}") - 1)
                norm_mod(l, 1, width)
                for half in range(2):
                    g = GEMM[f"fin{l}{half}"]

                    def hidden(i, u, g=g, l=l, half=half):
                        if l == 0 and u % 2 == 0:
                            half_mod(i, u, 30 * half, 22)
                        if u % 2 == 0:
                            return
                        j, b, used, _, _ = where(g, i, u)
                        e = FH * (2 * l + half) + 2 * i + u // 2
                        dve.wait_ge(panel_done, j + 1)
                        dve.wait_ge(bank_free[1 - b], (g.j0 + u - 1) // 2 + 2 * i + 1)
                        wait(dve, h_lo, e)
                        nc.vector.tensor_tensor(fh[:, 0:width], fsilu[:, 0:width], G[b][:, 0:width], ALU.mult).then_inc(bank_free[b], 1)
                        dve.wait_ge(h_hi, e + 1)
                        c = 2 * i + u // 2
                        nc.vector.tensor_tensor(HL[:, c, 0:width], fh[:, 0:width], HH[:, c, 0:width].bitcast(F32),
                                                ALU.subtract).then_inc(h_lo, 1)
                        if l == 0:
                            half_mod(i, u, 30 * half, 22)
                    each_panel(dve, g, hidden)
                    gated_add(f"fout{l}{half}", l, segs, 40,
                              (lambda p, half=half: half_mod(0, p, 22 + 30 * half, 4 if half else 8)) if l == 0 else None)
                freed(dve, last(f"fout{l}1"))
                freed(dve, last(f"fout{l}1") - 1)
                if l == 0:
                    modulation(1, 0)
                    modulation(1, 1)

            norm_plain([X[:, c, 0:NX] for c in range(DC)], pa("pre")[:, 0:8], W, 0)
            dve.wait_ge(rope_landed, 80)
            ang, k_, turns = W[4][:, 0:NX], W[5][:, 0:NX], W[6][:, 0:NX]
            magic = 1.5 * 2.0 ** 23
            tau = (6.28125, 0.0019350051879882812, 3.019915981956753e-07)
            link(nc.vector.tensor_copy(ang, sinT[:, :].bitcast(I32)))
            link(nc.vector.tensor_scalar(ang, ang, co("inv"), None, ALU.mult))
            for s in range(2):
                r = W[s][:, 0:NX]
                link(nc.vector.tensor_scalar(turns, ang, 1.0 / (2.0 * np.pi), 0.25 * s, ALU.mult, ALU.add))
                link(nc.vector.tensor_scalar(turns, turns, magic, None, ALU.add))
                link(nc.vector.tensor_scalar(k_, turns, -magic, None, ALU.add))
                link(nc.vector.scalar_tensor_tensor(r, k_, -tau[0], ang, ALU.mult, ALU.add))
                link(nc.vector.scalar_tensor_tensor(r, k_, -tau[1], r, ALU.mult, ALU.add))
                link(nc.vector.scalar_tensor_tensor(r, k_, -tau[2], r, ALU.mult, ALU.add))
                if s:
                    link(nc.vector.tensor_scalar(r, r, float(np.pi / 2), None, ALU.add))
                nc.vector.tensor_scalar(r, r, 3.1415925, -3.1415925, ALU.min, ALU.max).then_inc(trig, 1)
            dve.wait_ge(act_step, 2)
            for c in range(8):
                freed(dve, GEMM["eqk"].j0 + c)
                rope(QK[:, c, :], W[4][:, 0:NX])

            for h in range(8):
                dve.wait_ge(ret_scores, h + 1)
                dve.wait_ge(decay_landed[h % 2], 16 * (h // 2 + 1))
                wait(dve, ret_pv, h - 1)
                for jb, c0, cn in RET_AT:
                    src = G[h % 2][:, c0:c0 + cn] if c0 < 1024 else M0[:, 512 * (h % 2):512 * (h % 2) + cn]
                    ins = nc.vector.tensor_tensor(scT[h % 2][:, c0:c0 + cn], src, decay[h % 2][:, 0:cn], ALU.mult)
                ins.then_inc(ret_masked, 1)
            for h in range(8):
                r = invert(NX, W)
                nc.vector.scalar_tensor_tensor(RT[:, h, :], RT[:, h, :], pa("gn")[:, h:h + 1], r, ALU.mult,
                                               ALU.mult).then_inc(ret_normed, 1)
            dve.wait_ge(ret_normed, 8)
            g = GEMM["eg"]
            for p in range(8):
                freed(dve, g.j0 + p)
                wait(dve, operand_lo, n["op"])
                nc.vector.tensor_tensor(W[6 + p % 2][:, 0:NX], W[4 + p % 2][:, 0:NX], RT[:, p, :], ALU.mult).then_inc(t_ready, 1)
                n["t"] += 1
                low_operand(ML[:, p, :], W[6 + p % 2][:, 0:NX], MH[:, p, :])
            g = GEMM["eout0"]
            for p in range(8):
                j, b = g.j0 + p, (g.j0 + p) % 2
                dve.wait_ge(panel_done, j + 1)
                nc.vector.tensor_copy(Y[:, p, :], G[b][:, 0:NX]).then_inc(bank_free[b], 1)

            g = GEMM["econv"]
            t0, op0, cwa, cba = n["t"], n["op"], PAR["cw"][0], PAR["cb"][0]
            link(nc.vector.memset(ce_u[:, 0:2], 0.0))

            def short_conv(i, u):
                j, b, used, _, _ = where(g, i, u)
                if u < 3:
                    dve.wait_ge(panel_done, j + 1)
                if u == 0:
                    dve.wait_ge(t_ready, t0 + i)
                    nc.vector.tensor_copy(ce_c[:, 0:NX], G[b][:, 0:NX]).then_inc(bank_free[b], 1)
                elif u == 1:
                    dve.wait_ge(bank_free[1 - b], (g.j0 + u - 1) // 2 + 2 * i + 1)
                    nc.vector.tensor_tensor(ce_u[:, 2:NX + 2], G[b][:, 0:NX], ce_c[:, 0:NX], ALU.mult).then_inc(bank_free[b], 1)
                    dve.wait_ge(bank_free[b], used + 1)
                    w = [par[:, bass.ds(3 * i + (cwa + t), 1)] for t in range(3)]
                    nc.vector.tensor_scalar(ce_y[:, 0:NX], ce_u[:, 0:NX], w[0], par[:, bass.ds(i + cba, 1)], ALU.mult,
                                            ALU.add).then_inc(ce_tick, 1)
                    for t in (1, 2):
                        dve.wait_ge(ce_tick, 3 * i + t)
                        nc.vector.scalar_tensor_tensor(ce_y[:, 0:NX], ce_u[:, t:NX + t], w[t], ce_y[:, 0:NX], ALU.mult,
                                                       ALU.add).then_inc(ce_tick, 1)
                elif u == 2:
                    dve.wait_ge(ce_tick, 3 * i + 3)
                    nc.vector.tensor_tensor(ce_c[:, 0:NX], G[b][:, 0:NX], ce_y[:, 0:NX], ALU.mult).then_inc(bank_free[b], 1)
                else:
                    dve.wait_ge(bank_free[1 - b], (g.j0 + u - 1) // 2 + 2 * i + 1)
                    dve.wait_ge(bank_free[b], used + 1)
                    dve.wait_ge(operand_lo, op0 + i)
                    nc.vector.tensor_tensor(ce_z[:, 0:NX], ce_c[:, 0:NX], ce_s[:, 0:NX], ALU.mult).then_inc(t_ready, 1)
                    dve.wait_ge(operand_hi, op0 + i + 1)
                    nc.vector.tensor_tensor(ML[:, i, :], ce_z[:, 0:NX], MH[:, i, :].bitcast(F32), ALU.subtract).then_inc(operand_lo, 1)
            each_panel(dve, g, short_conv)
            n["t"] += 8
            n["op"] += 8
            g = GEMM["eout1"]
            freed(dve, last("eout0"))
            freed(dve, last("eout0") - 1)
            for p in range(8):
                j, b = g.j0 + p, (g.j0 + p) % 2
                dve.wait_ge(panel_done, j + 1)
                nc.vector.tensor_tensor(Y[:, p, :], G[b][:, 0:NX], Y[:, p, :], ALU.add).then_inc(bank_free[b], 1)
            freed(dve, last("eout1"))
            freed(dve, last("eout1") - 1)
            norm_post(Y, pa("post")[:, 0:8], W)

            dve.wait_ge(resid_ready, 8)
            norm_plain([X[:, c, 0:NX] for c in range(DC)], pa("pre")[:, 8:16], W, 0)
            norm_plain([LAT[:, c, :] for c in range(3)], pa("qa"), WL, 0)
            norm_plain([LAT[:, c, :] for c in range(3, 5)], pa("kva"), WL, 3)
            rope(kr[:, 0:NX], dprobs[0][:, 0:NX])
            for c in range(4):
                freed(dve, GEMM["oq"].j0 + 8 + c)
                rope(QR[:, 2 * c:2 * c + 2, :], dprobs[0][:, 0:NX], True)

            def finish2(unit, h, q0, qn):
                o = (M1, MM)[h % 2]
                dve.wait_ge(pv_done, unit)
                nc.vector.tensor_tensor(SG[:, h, :], o[:, 0:NX], SG[:, h, :], ALU.mult).then_inc(gated, 1)
                low_operand(XL[:, h, 0:NX], SG[:, h, :], XH[:, h, 0:NX])
            attention(units2, 192.0 ** -0.5, (dprobs, dprobsT), finish2, True)
            g = GEMM["oout"]
            for p in range(8):
                j, b = g.j0 + p, (g.j0 + p) % 2
                dve.wait_ge(panel_done, j + 1)
                nc.vector.tensor_copy(Y2[:, p, :], G[b][:, 0:NX]).then_inc(bank_free[b], 1)
            freed(dve, last("oout"))
            freed(dve, last("oout") - 1)
            norm_post(Y2, pa("post")[:, 8:16], WY)



def chunked(v):
    return np.ascontiguousarray(np.asarray(v).reshape(-1, P).T)


def panel(w, cols):
    w = np.asarray(w)[:, cols]
    return w.reshape(-1, P, P).transpose(1, 0, 2).reshape(P, -1)


def panels(inp):
    by = {}

    def add(name, items):
        g = GEMM[name]
        assert len(items) == g.n, name
        by.setdefault(g.kc, []).extend(items)

    run = lambda a: np.arange(a, a + P)
    for l in range(2):
        w = inp["w_in"][l]
        k0 = np.arange(256, 320)
        cols = [run(1024), run(768), run(1152), run(896), run(1280), run(1408), run(512), run(640), run(0), run(128),
                np.concatenate([k0, k0]), np.concatenate([k0 + 64, k0 + 64]), run(384)]
        add(f"win{l}", [panel(w, c) for c in cols])
        add(f"wout{l}", [panel(inp["w_out"][l], run(P * m)) for m in range(8)])
        for half in range(2):
            add(f"fin{l}{half}", [panel(inp["w_ffn_in"][l], run(2 * FH * P * s + (FH * half + i) * P))
                                  for i in range(FH) for s in range(2)])
            add(f"fout{l}{half}", [panel(inp["w_ffn_out"][l][FH * P * half:FH * P * (half + 1)], run(P * m)) for m in range(8)])
    w = inp["even_w_in_2"][0]
    add("eqk", [panel(w, run(P * c)) for c in range(8)])
    add("ev", [panel(w, run(1024 + P * c)) for c in range(8)])
    add("eg", [panel(w, run(2048 + P * c)) for c in range(8)])
    add("eout0", [panel(inp["even_w_out_2"][0][0:1024], run(P * m)) for m in range(8)])
    add("econv", [panel(w, run(at + P * c)) for c in range(8) for at in (4096, 5120, 3072, 6144)])
    add("eout1", [panel(inp["even_w_out_2"][0][1024:2048], run(P * m)) for m in range(8)])
    w = inp["odd_w_in_2"][0]
    r0 = np.arange(640, 704)
    add("oin", [panel(w, c) for c in [run(P * c) for c in range(5)] + [np.concatenate([r0, r0])] + [run(704 + P * c) for c in range(8)]])
    w = inp["w_qb_2"][0]
    r0 = np.arange(128, 192)
    add("oq", [panel(w, run(192 * h)) for h in range(8)]
        + [panel(w, np.concatenate([r0 + 192 * 2 * c, r0 + 192 * (2 * c + 1)])) for c in range(4)])
    w = inp["w_kvb_2"][0]
    add("ok", [panel(w, run(256 * h)) for h in range(8)])
    add("ov", [panel(w, run(256 * h + P)) for h in range(8)])
    add("oout", [panel(inp["odd_w_out_2"][0], run(P * m)) for m in range(8)])
    return {kc: np.stack(v) for kc, v in by.items()}


def parameters(inp):
    par = np.zeros((P, NPAR), np.float32)

    def put(name, v):
        a, w = PAR[name]
        par[:, a:a + w] = v
    for l in range(2):
        b = chunked(inp["b_mod"][l])
        put(f"mod{l}", np.repeat(b, 2, axis=1))
        put(f"g1{l}", chunked(inp["g_norm1"][l]))
        put(f"g2{l}", chunked(inp["g_norm2"][l]))
        put(f"qg{l}", np.concatenate([inp["q_norm_g"][l]] * 2)[:, None])
        put(f"kg{l}", np.concatenate([inp["k_norm_g"][l]] * 2)[:, None])
        put(f"dw{l}", inp["conv_dw_w"][l].reshape(CONV, 2, P).transpose(2, 1, 0).reshape(P, -1))
        for key, name in (("dwb", "conv_dw_b"), ("lng", "conv_ln_g"), ("lnb", "conv_ln_b"), ("psc", "pool_scale")):
            put(f"{key}{l}", chunked(inp[name][l]))
    put("pre", np.concatenate([chunked(inp["pre_norm_2"][e]) for e in range(2)], axis=1))
    put("post", np.concatenate([chunked(inp["post_norm_2"][e]) for e in range(2)], axis=1))
    put("cw", inp["even_conv_w_2"][0].reshape(3, 8, P).transpose(2, 1, 0).reshape(P, -1))
    put("cb", chunked(inp["even_conv_b_2"][0]))
    put("gn", chunked(inp["ret_gn_2"][0]))
    put("qa", chunked(inp["q_a_norm_2"][0]))
    put("kva", chunked(inp["kv_a_norm_2"][0]))
    return par


def constants():
    con = np.zeros((P, NCON), np.float64)

    def put(name, v):
        a, w = CON[name]
        con[:, a:a + w] = v
    i = np.arange(P)
    put("ident", np.eye(P))
    put("ones", 1.0)
    put("blk", i[:, None] // 64 == i[None, :] // 64)
    perm1, perm2 = np.zeros((P, P)), np.zeros((P, P))
    for m in range(P):
        perm1[m ^ 1, m] = 1.0 if m % 2 else -1.0
        perm2[m ^ 32, m] = 1.0 if m % 64 >= 32 else -1.0
    put("perm1", perm1)
    put("perm2", perm2)
    put("mask", np.where(i[None, :] <= i[:, None], 0.0, -1e30))
    win = np.array([2, 4, 8, 16])[np.stack([i // 64, 2 + i // 64], axis=1)]
    put("invw", 1.0 / win)
    edge = np.ones((P, 2, 2, 8))
    for c in range(2):
        for q in range(8):
            w = win[:, c]
            edge[:, c, 0, q] = w / np.minimum(w, q + w // 2)
            edge[:, c, 1, q] = w / np.minimum(w, 8 - q + w // 2)
    put("edge", edge.reshape(P, 32))
    put("inv", (10000.0 ** (-(np.arange(0, 64, 2, dtype=np.float32)) / np.float32(64)))[i % 32][:, None])
    put("eps", EPS)
    put("half", i[:, None] // 64 == np.arange(2)[None, :])
    return con.astype(np.float32)


def dft_tables():
    out = []
    for nn in (NX, NC):
        a = 2 * np.pi * (np.outer(np.arange(nn), np.arange(nn)) % nn) / nn
        s = 1.0 / np.sqrt(nn * 64.0)
        t = np.stack([np.cos(a) * s, np.sin(a) * s], axis=1)
        out.append(t.reshape(nn // P, P, 2 * nn).astype(np.float32))
    a = 2 * np.pi * (np.outer(np.arange(64), np.arange(64)) % 64) / 64
    d = np.zeros((2, 64, 2, 2, 64))
    for b in range(2):
        d[b, :, 0, b] = np.cos(a)
        d[b, :, 1, b] = -np.sin(a)
    return out[0], out[1], d.reshape(P, 256).astype(np.float32)


def rope_tables():
    inv = 10000.0 ** (-np.arange(16) / 16.0)
    row, col = np.arange(NX) // 64, np.arange(NX) % 64
    ang = np.concatenate([np.outer(inv, row), np.outer(inv, col)])[(np.arange(P) % 64) // 2]
    return np.cos(ang).astype(np.float32), np.sin(ang).astype(np.float32)


def decay_tables():
    lg = np.log1p(-np.exp2(-5.0 - np.arange(8)))
    rel = np.arange(NX)[None, :] - np.arange(P)[:, None]
    return np.where(rel >= 0, np.exp(lg[:, None, None] * np.maximum(rel, 0)) * 0.125, 0.0).astype(np.float32)


def kernel(**inputs):
    import concourse.bacc as _bacc
    from concourse.bass_utils import run_bass_kernel_spmd as _run

    inp = {k: np.asarray(v) for k, v in inputs.items()}
    w = panels(inp)
    dx, dc, dd = dft_tables()
    cosx, sinx = rope_tables()
    small = np.zeros((2, P, 1536), np.float32)
    for l in range(2):
        small[l, :, 0:512] = inp["w_fourier"][l].reshape(2, P, 256).transpose(1, 0, 2).reshape(P, 512)
        small[l, :, 512:1024] = inp["w_conv_pw"][l].reshape(2, P, 256).transpose(1, 0, 2).reshape(P, 512)
        for q in range(4):
            part, at = 64 * (q % 2), 1024 + P * (q // 2) + 64 * (q % 2)
            small[l, part:part + 64, at:at + 64] = inp["w_pool"][l][q]
        small[l, :, 1280:1536] = dd
    arrays = {
        "par": parameters(inp), "con": constants(),
        "xt": np.concatenate([inp["x"][0], inp["ctx"][0]]).T.reshape(DC, P, NT).transpose(1, 0, 2),
        "wmod": np.asarray(inp["w_mod"]).transpose(0, 2, 1).reshape(96, P, DC * P),
        "c": np.tile(np.concatenate([inp["c"][0], inp["c_ctx"]])[None], (P, 1)),
        "small": small, "dftx": dx, "dftc": dc, "cosx": cosx, "sinx": sinx, "decay": decay_tables(),
        "pos": np.tile(inp["positions_2"].reshape(1, NX), (P, 1)),
    }
    arrays.update({f"w{kc}": v for kc, v in w.items()})
    arrays = {k: np.ascontiguousarray(v) for k, v in arrays.items()}
    nc = _bacc.Bacc("TRN2", target_bir_lowering=False, num_devices=1)
    d = {k: nc.dram_tensor(f"in_{k}", v.shape, mybir.dt.from_np(v.dtype), kind="ExternalInput").ap() for k, v in arrays.items()}
    d["out"] = nc.dram_tensor("out_x", (P, DC, NX), F32, kind="ExternalOutput").ap()
    build_program(nc, d)
    r = _run(nc, [{f"in_{k}": v for k, v in arrays.items()}], core_ids=[0])
    out = r.results[0]["out_x"]
    return np.ascontiguousarray(out.transpose(1, 0, 2).reshape(DC * P, NX).T)[None]
```

```python
from contextlib import ExitStack

import numpy as np

import concourse.bass as bass
from concourse import mybir

F32 = mybir.dt.float32
F32R = mybir.dt.float32r
I32 = mybir.dt.int32
ALU = mybir.AluOpType
ACT = mybir.ActivationFunctionType
AX = mybir.AxisListType

P = 128
NX, NC = 512, 256
NT = NX + NC
DC = 8
FH = 11
EPS = 1e-6
RAW = 4
SBUF_END = 229312
CONV = 31
HALO = CONV // 2
POOLPAD = 8
SEGS = [(0, NX), (NX, NC)]
GLU_AT = [HALO, NX + 3 * HALO]
GLU_W = NT + 4 * HALO
PP_AT = [POOLPAD, NX + 3 * POOLPAD]
PP_W = NT + 4 * POOLPAD



class Gemm:
    def __init__(self, name, kc, n, j0, at):
        self.name, self.kc, self.n, self.j0, self.at = name, kc, n, j0, at


def plan():
    gemms, used = [], {}
    j = 0
    for name, kc, n in (
        [x for l in range(2) for x in (
            (f"win{l}", 8, 13), (f"wout{l}", 8, 8),
            (f"fin{l}0", 8, 2 * FH), (f"fout{l}0", FH, 8),
            (f"fin{l}1", 8, 2 * FH), (f"fout{l}1", FH, 8))]
        + [("eqk", 8, 8), ("ev", 8, 8), ("eg", 8, 8), ("eout0", 8, 8), ("econv", 8, 32), ("eout1", 8, 8),
           ("oin", 8, 6), ("ogate", 8, 8), ("oq", 3, 12), ("ok", 2, 8), ("ov", 2, 8), ("oout", 8, 8)]
    ):
        gemms.append(Gemm(name, kc, n, j, used.get(kc, 0)))
        used[kc] = used.get(kc, 0) + n
        j += n
    return gemms


GEMMS = plan()
GEMM = {g.name: g for g in GEMMS}
MOD_FIRST = 16
MOD_DVE = 8
MOD_ALL = 32
MOD_STARTS = (MOD_DVE, MOD_FIRST, 32, 40, 62, 70, 92)
JMOD = GEMM["wout0"].j0 + 2


def ring_shift(j):
    return (MOD_FIRST if j < JMOD else MOD_ALL) // RAW


def mod_ring(k):
    return 2 * k + 1 if k < MOD_DVE else 2 * (k - MOD_DVE) if k < MOD_FIRST else k + JMOD


def mods_done(k):
    return 4 * (k + 1 - MOD_DVE)


NPANEL = sum(g.n for g in GEMMS)
KC_OF = [g.kc for g in GEMMS for _ in range(g.n)]

PAR = {}


def _par_layout():
    at = 0
    for l in range(2):
        PAR[f"mod{l}"] = (at, 96)
        at += 96
    for l in range(2):
        for name, w in (("g1", 8), ("g2", 8), ("qg", 1), ("kg", 1), ("dw", 2 * CONV), ("dwb", 2),
                        ("lng", 2), ("lnb", 2), ("psc", 2)):
            PAR[name + str(l)] = (at, w)
            at += w
    for name, w in (("pre", 16), ("post", 16), ("cw", 24), ("cb", 8), ("gn", 8), ("qa", 3), ("kva", 2), ("c", 16)):
        PAR[name] = (at, w)
        at += w
    return at


NPAR = _par_layout()

CON = {}


def _con_layout():
    at = 0
    for name, w in (("ident", 128), ("ones", 128), ("perm1", 128), ("perm2", 128), ("mask", 128),
                    ("invw", 2), ("edge", 32), ("inv", 1), ("eps", 1), ("half", 2)):
        CON[name] = (at, w)
        at += w
    return at


NCON = _con_layout()


def wait(eng, sem, value):
    if isinstance(value, int) and value <= 0:
        return
    eng.wait_ge(sem, value)


def build_program(nc, d):
    stack = ExitStack()
    with stack:
        base = nc.sbuf_base
        top = [(base + 63) // 64 * 64]

        def at(name, shape, dt, offset):
            return nc.alloc_sbuf_tensor_at(name, [P, shape], dt, offset=offset)

        def sb(name, width, dt=F32):
            t = at(name, width, dt, top[0])
            top[0] += (width * 4 + 63) // 64 * 64
            return t

        Xf = sb("resid", DC * NT)
        X = Xf[:, :].rearrange("p (c t) -> p c t", c=DC)
        xhi_t, xlo_t = sb("operand_hi", DC * NT, F32R), sb("operand_lo", DC * NT, F32R)
        XH = xhi_t[:, :].rearrange("p (c t) -> p c t", c=DC)
        XL = xlo_t[:, :].rearrange("p (c t) -> p c t", c=DC)
        raw = [sb(f"raw{s}", FH * P) for s in range(RAW)]
        whi = [sb(f"whi{s}", FH * P, F32R) for s in range(2)]
        wlo = [sb(f"wlo{s}", FH * P, F32R) for s in range(2)]
        par = sb("par", NPAR)
        con = sb("con", NCON)
        cosT, sinT = sb("cosT", NX), sb("sinT", NX)
        afac = sb("afac", 32)
        stat = sb("stat", 24)
        sums = sb("mod_sums", 8)
        silu_cp = sb("silu_c_by_feature", 16)
        rootT = sb("rootT", 24)
        region = top[0]
        silu_c = at("silu_c", 2 * DC * P, F32, SBUF_END - 8 * DC * P)
        mod_half = [cosT, sinT]

        def pa(name):
            a, w = PAR[name]
            return par[:, a:a + w]

        def co(name):
            a, w = CON[name]
            return con[:, a:a + w]

        ident, ones = co("ident"), co("ones")

        def phase():
            top[0] = region

        phase()
        projf = sb("proj", 6 * NT)
        PR = projf[:, :].rearrange("p (c t) -> p c t", c=6)
        vtok = sb("vtok", NT)
        gluf = sb("glu", 2 * GLU_W)
        glu = gluf[:, :].rearrange("p (c t) -> p c t", c=2)
        accf = sb("conv_acc", 2 * NT)
        acc = accf[:, :].rearrange("p (c t) -> p c t", c=2)
        ppf = sb("pool_in", 2 * PP_W)
        pp = ppf[:, :].rearrange("p (c t) -> p c t", c=2)
        pA = sb("pool_a", PP_W)
        smallw = sb("smallw", 1536)
        dftd = smallw[:, 1280:1536]
        wf = smallw[:, 0:512].rearrange("p (k m) -> p k m", k=2)
        wpw = smallw[:, 512:1024].rearrange("p (k m) -> p k m", k=2)
        wpl = smallw[:, 1024:1280].rearrange("p (k m) -> p k m", k=2)
        zone = top[0] = max(top[0], region + 24 * NX * 4)
        W = [sb(f"work{s}", NT) for s in range(8)]
        endA = top[0]
        pB = at("pool_b", PP_W, F32, zone + 5120 * 4)
        ftok = at("fourier_tok", 6 * 512, F32, zone)
        dft = [at(f"dft{s}", 1024, F32, zone + (3072 + 1024 * s) * 4) for s in range(3)]

        phase()
        hhi_t, hlo_t = sb("hidden_hi", FH * NT, F32R), sb("hidden_lo", FH * NT, F32R)
        HH = hhi_t[:, :].rearrange("p (c t) -> p c t", c=FH)
        HL = hlo_t[:, :].rearrange("p (c t) -> p c t", c=FH)
        fsilu, fh = sb("ffn_silu", NT), sb("ffn_h", NT)
        endB = top[0]

        phase()
        QK = sb("ret_qk", 8 * NX)[:, :].rearrange("p (c t) -> p c t", c=8)
        VE = sb("ret_v", 4 * 1024)[:, :].rearrange("p (b f) -> p b f", b=4)
        RT = sb("ret_r", 8 * NX)[:, :].rearrange("p (c t) -> p c t", c=8)
        MH = at("mix_hi", 8 * NX, F32R, region)[:, :].rearrange("p (c t) -> p c t", c=8)
        ML = at("mix_lo", 8 * NX, F32R, region + 8 * NX * 4)[:, :].rearrange("p (c t) -> p c t", c=8)
        Y = at("layer_y", 8 * NX, F32, region + 16 * NX * 4)[:, :].rearrange("p (c t) -> p c t", c=8)
        assert zone >= top[0]
        decay = [at(f"decay{s}", NX, F32, zone + s * NX * 4) for s in range(2)]
        scT = [at(f"scoresT{s}", 1280, F32, zone + (2 * NX + 1280 * s) * 4) for s in range(2)]
        ce_c, ce_u, ce_y, ce_s, ce_z = (at(n, NX + 2, F32, zone + i * 2112)
                                        for i, n in enumerate(("ce_c", "ce_u", "ce_y", "ce_s", "ce_z")))

        vfE = W[5:7]

        phase()
        QN = sb("q_nope", 8 * NX)[:, :].rearrange("p (c t) -> p c t", c=8)
        KN = sb("k_nope", 8 * NX)[:, :].rearrange("p (c t) -> p c t", c=8)
        VO = sb("v_lat", 4 * 1024)[:, :].rearrange("p (b f) -> p b f", b=4)
        SG = sb("silu_gate", 8 * NX)[:, :].rearrange("p (c t) -> p c t", c=8)
        QR = X[:, :, NX:NT]
        kr = sb("k_rope", NX)
        dprobs = [sb(f"dprobs{s}", NX) for s in range(2)]
        dprobsT = [sb(f"dprobsT{s}", NX) for s in range(2)]
        vfD = dprobs
        LQH, LQL = (at(f"latent_q_{x}", 3 * NX, F32R, region + 16 * NX * 4 + x_at * 4)[:, :].rearrange("p (c t) -> p c t", c=3)
                    for x, x_at in (("hi", 0), ("lo", 3 * NX)))
        LKH, LKL = (at(f"latent_kv_{x}", 2 * NX, F32R, SBUF_END - 8 * DC * P + x_at * 4)[:, :].rearrange("p (c t) -> p c t", c=2)
                    for x, x_at in (("hi", 0), ("lo", 2 * NX)))
        LAT = at("latent", 5 * NX, F32, region + 8 * NX * 4)[:, :].rearrange("p (c t) -> p c t", c=5)
        WL = [at(f"work_latent{s}", NX, F32, region + s * NX * 4) for s in range(8)]
        WY = [at(f"work_out{s}", NX, F32, region + (8 + s) * NX * 4) for s in range(8)]
        Y2 = at("layer_y2", 8 * NX, F32, region)[:, :].rearrange("p (c t) -> p c t", c=8)
        endD = top[0]
        assert max(endA, endB, endD) <= SBUF_END - 8 * DC * P

        def ps(name, width):
            return stack.enter_context(nc.psum_tensor(name, [P, width], F32))
        G = [ps("prod0", 1024), ps("prod1", 1024)]
        M0, M1, MM = ps("misc0", 1024), ps("misc1", 512), ps("misc2", 512)

        def sem(name):
            return stack.enter_context(nc.semaphore(name))

        raw_landed = [sem(f"raw_landed{s}") for s in range(RAW)]
        hi_ready, lo_ready = sem("hi_ready"), sem("lo_ready")
        panel_done = sem("panel_done")
        bank_free = [sem("bank_free0"), sem("bank_free1")]
        mod_step, shift_used, c_ready, c_landed = sem("mod_step"), sem("shift_used"), sem("c_ready"), sem("c_landed")
        shift_read = sem("shift_read")
        half_landed = [sem("half_landed0"), sem("half_landed1")]
        par_landed, x_landed, small_landed = sem("par_landed"), sem("x_landed"), sem("small_landed")
        rope_landed, out_landed = sem("rope_landed"), sem("out_landed")
        sq_ready, sq_used, sd_ready, rs_ready = sem("sq_ready"), sem("sq_used"), sem("sd_ready"), sem("rs_ready")
        square_ready, square_added = sem("square_ready"), sem("square_added")
        t_ready = sem("t_ready")
        operand_hi, operand_lo, odd_lo = sem("operand_hi"), sem("operand_lo"), sem("odd_lo")
        resid_ready = sem("resid_ready")
        conv_tick, dve_step, act_step = sem("conv_tick"), sem("dve_step"), sem("act_step")
        ft_ready, ft_copied, dft_landed, dft_used, fy_copied = (
            sem("ft_ready"), sem("ft_copied"), [sem("dft_landed0"), sem("dft_landed1"), sem("dft_landed2")], sem("dft_used"), sem("fy_copied"))
        mp_ready, rb_ready, turned, turn_copied = sem("mp_ready"), sem("rb_ready"), sem("turned"), sem("turn_copied")
        qk_normed, rot_ready, rope_done = sem("qk_normed"), sem("rot_ready"), sem("rope_done")
        scores_ready, negmax_ready, exp_done = sem("scores_ready"), sem("negmax_ready"), sem("exp_done")
        probs_ready, probsT_ready, probsT_copied, pv_done = (
            sem("probs_ready"), sem("probsT_ready"), sem("probsT_copied"), sem("pv_done"))
        gated = sem("gated")
        ln_sum, ln_centered, ln_spread, ln_scaled, ln_act, pool_ready = (
            sem("ln_sum"), sem("ln_centered"), sem("ln_spread"), sem("ln_scaled"), sem("ln_act"), sem("pool_ready"))
        h_hi, h_lo = sem("h_hi"), sem("h_lo")
        decay_landed, ret_scores, ret_masked, ret_pv, ret_copied, ret_normed = (
            [sem("decay_landed0"), sem("decay_landed1")], sem("ret_scores"), sem("ret_masked"), sem("ret_pv"), sem("ret_copied"), sem("ret_normed"))
        ce_tick, trig = sem("ce_tick"), sem("trig")


        def where(g, i, u):
            jj = g.j0 + u
            shift = ring_shift(jj + 4 * i if isinstance(i, int) else jj + 4)
            return jj + 4 * i, jj % 2, jj // 2 + 2 * i, jj % RAW, jj // RAW + i + shift

        def each_panel(eng, g, body):
            full = (g.n - 2) // 4 if g.n > 16 else 1
            for u in range(min(4, g.n)):
                body(0, u)
            if full > 1:
                with eng.Fori(1, full) as i:
                    for u in range(4):
                        body(i, u)
            for p in range(4 * full, g.n):
                body(p // 4, p % 4)

        def freed(eng, j):
            wait(eng, bank_free[j % 2], j // 2 + 1)

        def last(name):
            return GEMM[name].j0 + GEMM[name].n - 1

        def tok(l):
            return (NT, SEGS) if l == 0 else (NX, SEGS[:1])

        def small_out(l, m):
            return M0 if m else G[1 - GEMM[f"wout{l}"].j0 % 2]

        def win_width(l, p):
            return NT if l == 0 or p in (6, 7, 8) else NX

        def units1(l):
            out = [(h, 128 * b, 0, NT) for h in range(4) for b in range(4)]
            if l == 0:
                out += [(h, NX + 128 * b, NX, NC) for h in range(4) for b in range(2)]
            return out

        def head_ends(units):
            ends, start = {}, 0
            for n, u in enumerate(units):
                if n + 1 == len(units) or units[n + 1][0] != u[0]:
                    ends[n] = (u[0], units[start][1], u[1] + 128 - units[start][1])
                    start = n + 1
            return ends

        units2 = [(h, 128 * b, 0, 128 * (b + 1)) for h in range(8) for b in range(4)]

        def score_bank(i, ahead):
            return G[i % 2] if ahead == 1 else G[i % 2][:, NX * (i // 2 % 2):NX * (i // 2 % 2) + NX]

        def mixer_steps(l):
            segs = range(len(tok(l)[1]))
            steps = ([("mean", 0, s) for s in segs] + [("square", 0, 0), ("sum", 0, 0)] + [("spread", 0, s) for s in segs]
                     + [("silu", 0, 0)] + [(kind, m, s) for kind in ("pointwise", "pool") for m in range(2) for s in segs])
            return {4 + k: step for k, step in enumerate(steps)}

        def op_order(units, steps):
            ends, order = head_ends(units), []
            for i in range(len(units)):
                if i - 1 in ends:
                    order.append(("end", i - 1))
                if i in steps and steps[i][0] in ("pointwise", "pool"):
                    order.append(("step", i))
            order.append(("end", len(units) - 1))
            return {what: k for k, what in enumerate(order)}
        RET_AT = [(0, 0, 512), (1, 512, 384), (3, 896, 128), (2, 1024, 256)]

        def mix_ops(l):
            return 2 + len(op_order(units1(l), mixer_steps(l)))

        MODULATED = {"win0": 0, "fin00": DC + mix_ops(0), "win1": 2 * DC + mix_ops(0), "fin10": 3 * DC + mix_ops(0) + mix_ops(1)}

        block = stack.enter_context(nc.Block())

        @block.sync
        def _(sp):
            sp.dma_start(silu_c[:, :], d["c"]).then_inc(c_landed, 16)
            sp.dma_start(par[:, :], d["par"]).then_inc(par_landed, 16)
            sp.dma_start(con[:, :], d["con"]).then_inc(par_landed, 16)

            def slot_of_mod(k):
                if k < MOD_DVE:
                    sp.wait_ge(shift_used, k + 1)
                else:
                    sp.wait_ge(mod_step, mods_done(k))

            def first_mod(r):
                return r // 2 + MOD_DVE * (1 - r % 2)

            def mod_panel(k):
                r = mod_ring(k)
                if MOD_FIRST <= k < MOD_FIRST + RAW:
                    wait(sp, lo_ready, JMOD - RAW + (k - MOD_FIRST) + 1)
                elif k < MOD_FIRST and r >= RAW:
                    slot_of_mod(first_mod(r - RAW))
                elif k >= MOD_FIRST:
                    slot_of_mod(k - RAW)
                sp.dma_start(raw[r % RAW][:, 0:DC * P], d["wmod"][k]).then_inc(raw_landed[r % RAW], 16)

            def panels(name, first=0, stop=None):
                g = GEMM[name]

                def body(i, u):
                    j, _, _, slot, _ = where(g, i, u)
                    p = 4 * i + u
                    if isinstance(p, int) and not first <= p < (stop or g.n):
                        return
                    if isinstance(j, int) and j < RAW:
                        slot_of_mod(first_mod(MOD_FIRST - RAW + j))
                    elif isinstance(j, int) and JMOD <= j < JMOD + RAW:
                        slot_of_mod(MOD_ALL - RAW + j - JMOD)
                    else:
                        wait(sp, lo_ready, j - RAW + 1)
                    sp.dma_start(raw[slot][:, 0:g.kc * P], d[f"w{g.kc}"][g.at + 4 * i + u]).then_inc(raw_landed[slot], 16)

                each_panel(sp, g, body)

            for r in range(RAW):
                mod_panel(first_mod(r))
            sp.dma_start(X[:, :, :], d["xt"]).then_inc(x_landed, 16)
            for r in range(RAW, MOD_FIRST):
                mod_panel(first_mod(r))
            panels("win0")
            panels("wout0", 0, 2)
            for k in range(MOD_FIRST, MOD_ALL):
                mod_panel(k)
            panels("wout0", 2)
            for g in GEMMS[2:]:
                panels(g.name)
            for c in range(DC):
                sp.wait_ge(resid_ready, DC + c + 1)
                sp.dma_start(d["out"][:, c, :], X[:, c, 0:NX]).then_inc(out_landed, 16)
            sp.wait_ge(out_landed, 16 * DC)

        @block.gpsimd
        def _(pool):
            for c in range(1, DC):
                pool.wait_ge(square_ready, c + 1)
                wait(pool, square_added, c - 1)
                nc.gpsimd.tensor_tensor(W[1][:, :], W[1][:, :], W[0][:, :], ALU.add).then_inc(square_added, 1)

            def odd_lows(name):
                width = NX if name == "fin10" else NT
                for c in range(1, DC, 2):
                    pool.wait_ge(operand_hi, MODULATED[name] + c + 1)
                    ins = nc.gpsimd.tensor_tensor(XL[:, c, 0:width], W[4 + c % 4][:, 0:width],
                                                  XH[:, c, 0:width].bitcast(F32), ALU.subtract)
                    ins.then_inc(odd_lo, 1)

            for g in GEMMS:
                def body(i, u, g=g):
                    j, b, _, slot, _ = where(g, i, u)
                    w = g.kc * P
                    if g.name in MODULATED and isinstance(i, int) and 4 * i + u == 2:
                        odd_lows(g.name)
                    pool.wait_ge(hi_ready, j + 1)
                    nc.gpsimd.tensor_tensor(wlo[b][:, 0:w], raw[slot][:, 0:w], whi[b][:, 0:w].bitcast(F32),
                                            ALU.subtract).then_inc(lo_ready, 1)
                each_panel(pool, g, body)

        @block.tensor
        def _(pe):
            n = dict(sq=0, inst=0, op=0, rope=0, unit=0, turn=0, added=0, direct=0, spread=0)

            xh, xl = (lambda k: XH[:, k, :]), (lambda k: XL[:, k, :])

            def big(name, xh, xl, width, ready=0, after=None, ready_sem=operand_lo):
                g = GEMM[name]

                def body(i, u):
                    j, b, used, _, _ = where(g, i, u)
                    p = 4 * i + u
                    pe.wait_ge(lo_ready, j + 1)
                    wait(pe, bank_free[b], used)
                    first = isinstance(p, int) and p == 0
                    tw = width(p) if callable(width) else width
                    segs = [s for s in SEGS if s[0] < tw]
                    for k in range(g.kc):
                        if first and name in MODULATED and k % 2:
                            pe.wait_ge(odd_lo, DC // 2 * list(MODULATED).index(name) + k // 2 + 1)
                        elif first:
                            wait(pe, ready_sem, ready - g.kc + k + 1)
                        for q, (w, a) in enumerate(((whi, xh(k)), (whi, xl(k)), (wlo, xh(k)))):
                            for t0, tn in segs:
                                mm = pe.matmul(G[b][:, t0:t0 + tn], w[b][:, k * P:(k + 1) * P], a[:, t0:t0 + tn],
                                               start=(k == 0 and q == 0), stop=(k == g.kc - 1 and q == 2))
                    mm.then_inc(panel_done, 1)
                    if after is not None:
                        after(p)

                each_panel(pe, g, body)

            def sum_squares(nchunks, width, sq_tiles, by_head=False, total=None):
                h, nb = (2, width // P) if by_head else (1, width // P)
                sel = co("half") if by_head else ones[:, 0:1]
                wait(pe, sd_ready, n["inst"])
                if total is not None:
                    n["added"] += DC - 1
                    pe.wait_ge(square_added, n["added"])
                for c in range(nchunks):
                    if total is None:
                        n["direct"] += 1
                        pe.wait_ge(sq_ready, n["direct"])
                    square = sq_tiles[n["sq"] % 2] if total is None else total
                    for tb in range(nb):
                        mm = pe.matmul(MM[:, h * tb:h * tb + h], square[:, tb * P:(tb + 1) * P], sel,
                                       start=(c == 0 and tb == 0), stop=(c == nchunks - 1 and tb == nb - 1),
                                       skip_group_check=True)
                    mm.then_inc(sq_used, 1)
                    n["sq"] += 1
                n["inst"] += 1

            def spread_roots(width, sq_tiles, free=None):
                pe.wait_ge(rs_ready, n["spread"] + 1)
                if free is not None:
                    free()
                r = sq_tiles[2 + n["spread"] % 2]
                for tb in range(width // P):
                    mm = pe.transpose(M0[:, tb * P:(tb + 1) * P], r[:, tb * P:(tb + 1) * P], ident)
                mm.then_inc(rb_ready, 1)
                n["spread"] += 1

            def rms(nchunks, width, sq_tiles, by_head=False, free=None, total=None):
                sum_squares(nchunks, width, sq_tiles, by_head, total)
                spread_roots(width, sq_tiles, free)

            def turn(src, nb, free):
                free()
                half = 512 * (n["turn"] % 2) if nb == 4 else 0
                for tb in range(nb):
                    mm = pe.transpose(M0[:, half + tb * P:half + (tb + 1) * P], src[:, tb * P:(tb + 1) * P], ident)
                mm.then_inc(turned, 1)
                n["turn"] += 1

            def small_product(l, weights, source, segs, kc, m):
                wait(pe, operand_lo, n["op"] - (1 if m else 0))
                o = small_out(l, m)
                for k in range(kc):
                    for s, (t0, tn) in enumerate(segs):
                        mm = pe.matmul(o[:, t0:t0 + tn], weights(k, m), source(k, s), start=(k == 0), stop=(k == kc - 1))
                mm.then_inc(mp_ready, 1)
                n["op"] += 1

            def rotate(chunk, perm):
                wait(pe, rope_done, n["rope"])
                o = M1[:, 0:NX] if len(chunk.shape) == 2 else M1[:, 0:NX].rearrange("p (a t) -> p a t", a=2)
                pe.matmul(o, perm, chunk, start=True, stop=True).then_inc(rot_ready, 1)
                n["rope"] += 1

            def attention(units, score, value, out, keys_tiles, steps={}, step=None, ahead=1):
                ends = head_ends(units)
                order = op_order(units, steps)
                base = n["unit"]

                def scores(i):
                    wait(pe, exp_done, base + max(0, i - 2 * ahead + 1))
                    for mm in score(units[i], score_bank(i, ahead)):
                        pass
                    mm.then_inc(scores_ready, 1)

                def turn(i):
                    pe.wait_ge(probs_ready, base + i + 1)
                    wait(pe, probsT_copied, base + i)
                    for kb in range(units[i][3] // P):
                        mm = pe.transpose(M0[:, kb * P:(kb + 1) * P], keys_tiles[0][i % 2][:, kb * P:(kb + 1) * P], ident)
                    mm.then_inc(probsT_ready, 1)

                def weigh(i):
                    h, q0, k0, nk = units[i]
                    pe.wait_ge(probsT_copied, base + i + 1)
                    first = i == 0 or units[i - 1][0] != h
                    if first:
                        done = [e for e in sorted(ends) if e < i]
                        wait(pe, operand_lo, n["op"] + (order["end", done[-2]] + 1 if len(done) > 1 else 0))
                    o = out(h, q0)
                    for kb in range(nk // P):
                        mm = pe.matmul(o, value(h, k0 // P + kb), keys_tiles[1][i % 2][:, kb * P:(kb + 1) * P],
                                       start=(kb == 0), stop=(kb == nk // P - 1))
                    mm.then_inc(pv_done, 1)

                for i in range(ahead):
                    scores(i)
                for i in range(len(units)):
                    if i + ahead < len(units):
                        scores(i + ahead)
                    if i >= 1:
                        weigh(i - 1)
                    turn(i)
                    if i in steps:
                        step(i, order)
                weigh(len(units) - 1)
                n["unit"] += len(units)
                n["op"] += len(order)

            pe.wait_ge(c_ready, 1)
            for k in range(MOD_DVE):
                r = mod_ring(k)
                pe.wait_ge(raw_landed[r % RAW], 16 * (r // RAW + 1))
                for c in range(DC):
                    mm = pe.matmul(M0[:, 2 * k:2 * k + 2], raw[r % RAW][:, c * P:(c + 1) * P], silu_cp[:, 2 * c:2 * c + 2],
                                   start=(c == 0), stop=(c == DC - 1))
                mm.then_inc(shift_used, 1)

            for l in range(2):
                width, segs = tok(l)
                if l == 0:
                    rms(1, NT, W, free=lambda: pe.wait_ge(shift_read, 1), total=W[1])
                else:
                    rms(1, NT, W, total=fh)
                n["op"] += DC
                def qk_norm(p, l=l):
                    if 2 <= p - 3 <= 5:
                        sum_squares(1, win_width(l, p - 1), W, True)
                    if 2 <= p - 4 <= 5:
                        spread_roots(win_width(l, p - 2), W, lambda: wait(pe, qk_normed, 4 * l + p - 6))
                    if 2 <= p - 5 <= 5:
                        pe.wait_ge(qk_normed, 4 * l + p - 6)
                        rotate(PR[:, p - 5, 0:NX], co("perm1"))
                    if p == 11:
                        freed(pe, GEMM[f"win{l}"].j0 + 8)
                        turn(W[5], NT // P, lambda: None)

                big(f"win{l}", xh, xl, lambda p, l=l: win_width(l, p), ready=n["op"], after=qk_norm)
                g = GEMM[f"win{l}"]

                freed(pe, g.j0 + 9)
                freed(pe, g.j0 + 10)
                pe.wait_ge(small_landed, 16 * (l + 1))
                pe.wait_ge(turn_copied, n["turn"])
                nb = width // P
                fb = 6 * l
                for tb in range(nb):
                    wait(pe, ft_copied, fb + tb - 1)
                    for c in range(2):
                        mm = pe.matmul(M0[:, 512 * (tb % 2) + 256 * c:512 * (tb % 2) + 256 * c + 256],
                                       PR[:, c, tb * P:(tb + 1) * P], dftd, start=True, stop=True)
                    mm.then_inc(ft_ready, 1)
                freed(pe, g.j0 + g.n - 1)
                freed(pe, g.j0 + g.n - 2)
                for tb in range(nb):
                    pe.wait_ge(ft_copied, fb + tb + 1)
                    pe.wait_ge(dft_landed[tb % 3], 16 * (2 * l + tb // 3 + 1))
                    t0, tn = SEGS[tb // 4]
                    lastb = tb == 3 or tb == 5
                    for c in range(2):
                        for q in range(2):
                            mm = pe.matmul(G[c][:, t0:t0 + tn], ftok[:, tb * 512 + c * 256 + q * P:tb * 512 + c * 256 + (q + 1) * P],
                                           dft[tb % 3][:, q * tn:(q + 1) * tn], start=(tb in (0, 4) and q == 0),
                                           stop=(lastb and q == 1))
                    mm.then_inc(dft_used, 1)
                pe.wait_ge(fy_copied, 2 * (l + 1))
                for m in range(2):
                    small_product(l, lambda k, m: wf[:, k, m * P:(m + 1) * P], lambda k, s: PR[:, k, segs[s][0]:segs[s][0] + segs[s][1]],
                                  segs, 2, m)
                wait(pe, operand_lo, n["op"])

                pe.wait_ge(rope_done, n["rope"])

                def score1(unit, o):
                    h, q0, k0, nk = unit
                    part = slice(64 * (h % 2), 64 * (h % 2) + 64)
                    for c0 in range(0, nk, NX):
                        cn = min(NX, nk - c0)
                        yield pe.matmul(o[:, c0:c0 + cn], PR[part, 2 + h // 2, q0:q0 + P],
                                        PR[part, 4 + h // 2, k0 + c0:k0 + c0 + cn], start=True, stop=True)

                steps = mixer_steps(l)
                products = [i for i in steps if steps[i][0] in ("pointwise", "pool")]

                def mixer_step(i, order, l=l, segs=segs, steps=steps, products=products, width=width):
                    kind, m, s = steps[i]
                    t0, tn = segs[s]
                    done = 2 * l + s
                    if kind == "mean":
                        pe.wait_ge(conv_tick, CONV * (2 * len(segs)) + (CONV * 4 if l else 0))
                        wait(pe, sd_ready, n["inst"])
                        wait(pe, ln_centered, done)
                        for c in range(2):
                            mm = pe.matmul(MM[:, 0:tn], ones, acc[:, c, t0:t0 + tn], start=(c == 0), stop=(c == 1))
                        mm.then_inc(ln_sum, 1)
                    elif kind == "sum":
                        sum_squares(2, width, W[4:8])
                    elif kind == "spread":
                        pe.wait_ge(rs_ready, n["spread"] + 1)
                        wait(pe, ln_scaled, done)
                        r = W[4:8][2 + n["spread"] % 2]
                        for tb in range(tn // P):
                            mm = pe.transpose(MM[:, tb * P:(tb + 1) * P], r[:, t0 + tb * P:t0 + (tb + 1) * P], ident)
                        mm.then_inc(rb_ready if s == len(segs) - 1 else ln_spread, 1)
                        n["spread"] += s == len(segs) - 1
                    elif kind in ("pointwise", "pool"):
                        k = products.index(i)
                        if k:
                            pe.wait_ge(operand_lo, n["op"] + order["step", products[k - 1]] + 1)
                        if kind == "pointwise":
                            pe.wait_ge(ln_act, 2 * (l + 1))
                            for c in range(2):
                                mm = pe.matmul(MM[:, 0:tn], wpw[:, c, m * P:(m + 1) * P], acc[:, c, t0:t0 + tn],
                                               start=(c == 0), stop=(c == 1))
                        else:
                            pe.wait_ge(pool_ready, 2 * (l + 1))
                            mm = pe.matmul(MM[:, 0:tn], wpl[:, m, :], pp[:, m, PP_AT[s]:PP_AT[s] + tn], start=True, stop=True)
                        mm.then_inc(mp_ready, 1)

                attention(units1(l), score1,
                          lambda h, kb: vtok[:, kb * P + 64 * (h // 2):kb * P + 64 * (h // 2) + 64],
                          lambda h, q0: M1[64 * (h % 2):64 * (h % 2) + 64, q0 % NX:q0 % NX + P],
                          (W[0:2], W[2:4]), steps, mixer_step)
                wait(pe, operand_lo, n["op"])

                big(f"wout{l}", xh, xl, width, ready=n["op"])
                rms(1, width, W, total=W[1])
                n["op"] += DC
                for half in range(2):
                    big(f"fin{l}{half}", xh, xl, width, ready=n["op"])
                    big(f"fout{l}{half}", lambda k: HH[:, k, :], lambda k: HL[:, k, :], width,
                        ready=FH * (2 * l + half + 1), ready_sem=h_lo)

            rms(1, NX, W, total=fh)
            n["op"] += DC
            big("eqk", xh, xl, NX, ready=n["op"])

            def turn_value(name, j):
                freed(pe, j)
                turn((vfD if name == "ov" else vfE)[j % 2], NX // P, lambda: wait(pe, turn_copied, n["turn"] - 1))

            def ev_after(p):
                if p >= 1:
                    turn_value("ev", GEMM["ev"].j0 + p - 1)
                rotate(QK[:, p, :], co("perm2"))
            big("ev", xh, xl, NX, ready=n["op"], after=ev_after)
            turn_value("ev", last("ev"))
            pe.wait_ge(turn_copied, n["turn"])
            pe.wait_ge(rope_done, n["rope"])

            def ret_score(h):
                part = slice(64 * (h % 2), 64 * (h % 2) + 64)
                wait(pe, ret_masked, h - 1)
                for jb, c0, cn in RET_AT:
                    o = G[h % 2][:, c0:c0 + cn] if c0 < 1024 else M0[:, 512 * (h % 2):512 * (h % 2) + cn]
                    mm = pe.matmul(o, QK[part, 4 + h // 2, jb * P:(jb + 1) * P], QK[part, h // 2, jb * P:NX],
                                   start=True, stop=True)
                mm.then_inc(ret_scores, 1)

            ret_score(0)
            for h in range(8):
                if h < 7:
                    ret_score(h + 1)
                pe.wait_ge(ret_masked, h + 1)
                wait(pe, ret_copied, h - 1)
                o = (M1, MM)[h % 2]
                for q, (jb, c0, cn) in enumerate(RET_AT):
                    mm = pe.matmul(o[:, jb * P:NX], VE[:, jb, h * P:(h + 1) * P], scT[h % 2][:, c0:c0 + cn],
                                   start=(q == 0), stop=(q == 3))
                mm.then_inc(ret_pv, 1)
            def head_norm(p):
                if 1 <= p <= 7:
                    spread_roots(NX, W, lambda: wait(pe, ret_normed, p))
                if p <= 6:
                    sum_squares(1, NX, W)

            sum_squares(1, NX, W)
            spread_roots(NX, W)
            sum_squares(1, NX, W)
            big("eg", xh, xl, NX, ready=n["op"], after=lambda p: head_norm(p + 1))
            n["op"] += 8
            big("eout0", lambda k: MH[:, k, :], lambda k: ML[:, k, :], NX, ready=n["op"])
            big("econv", xh, xl, NX, ready=n["op"])
            n["op"] += 8
            big("eout1", lambda k: MH[:, k, :], lambda k: ML[:, k, :], NX, ready=n["op"])
            rms(1, NX, W, total=W[1])

            rms(DC, NX, W, free=lambda: pe.wait_ge(resid_ready, DC))
            n["op"] += DC
            big("oin", xh, xl, NX, ready=n["op"])

            def latent_norm(p):
                if p in (0, 2):
                    sum_squares(3 - p // 2, NX, WL)
                elif p == 1:
                    spread_roots(NX, WL)
                elif p == 3:
                    spread_roots(NX, WL, lambda: pe.wait_ge(t_ready, 8 * DC + 3))
                elif p == 4:
                    freed(pe, GEMM["oin"].j0 + 5)
                    rotate(kr[:, 0:NX], co("perm2"))
            big("ogate", xh, xl, NX, ready=n["op"], after=latent_norm)
            n["op"] += 5
            big("oq", lambda k: LQH[:, k, :], lambda k: LQL[:, k, :], NX, ready=n["op"] - 2)
            kvh, kvl = (lambda k: LKH[:, k, :]), (lambda k: LKL[:, k, :])

            def rotate_query(p):
                if p % 2 == 0:
                    freed(pe, GEMM["oq"].j0 + 8 + p // 2)
                    rotate(QR[:, p:p + 2, :], co("perm2"))
            big("ok", kvh, kvl, NX, ready=n["op"], after=rotate_query)
            big("ov", kvh, kvl, NX, ready=n["op"],
                after=lambda p: turn_value("ov", GEMM["ov"].j0 + p - 1) if p else None)
            turn_value("ov", last("ov"))
            pe.wait_ge(turn_copied, n["turn"])
            pe.wait_ge(rope_done, n["rope"])

            def score2(unit, o):
                h, q0, _, nk = unit
                part = slice(64 * (h % 2), 64 * (h % 2) + 64)
                yield pe.matmul(o[:, 0:nk], QN[:, h, q0:q0 + P], KN[:, h, 0:nk], start=True, stop=False)
                piece = QR[part, 2 * (h // 2) + q0 // 256, q0 % 256:q0 % 256 + P]
                yield pe.matmul(o[:, 0:nk], piece, kr[part, 0:nk], start=False, stop=True)

            attention(units2, score2, lambda h, kb: VO[:, kb, h * P:(h + 1) * P],
                      lambda h, q0: (M1, MM)[h % 2][:, q0:q0 + P], (dprobs, dprobsT), ahead=2)
            big("oout", xh, xl, NX, ready=n["op"])
            rms(1, NX, WY, total=WY[1])

        @block.scalar
        def _(act):
            n = dict(sq=0, added=0, inst=0, op=0, mp=0, t=0, unit=0, turn=0)
            eps = co("eps")

            def high(j_static, rnd):
                if j_static >= NPANEL:
                    return
                w = KC_OF[j_static] * P
                act.wait_ge(raw_landed[j_static % RAW], 16 * (rnd + 1))
                nc.scalar.activation(whi[j_static % 2][:, 0:w], raw[j_static % RAW][:, 0:w], ACT.Copy).then_inc(hi_ready, 1)

            def stage(name, evac=None, after=None, norm_follows=False):
                g = GEMM[name]

                def body(i, u):
                    j, b, _, _, _ = where(g, i, u)
                    act.wait_ge(panel_done, j + 1)
                    if evac is not None:
                        evac(i, u, G[b], bank_free[b])
                    js = g.j0 + u + (4 * i if isinstance(i, int) else 4)
                    first = norm_follows and 4 * i + u == g.n - 1
                    if first:
                        after(i, u)
                    high(js + 2, (g.j0 + u + 2) // RAW + i + ring_shift(js + 2))
                    if after is not None and not first:
                        after(i, u)

                each_panel(act, g, body)

            def rms(sources, width, Wt, ready):
                for c, src in enumerate(sources):
                    ready(c)
                    wait(act, sq_used, n["sq"] - 1)
                    nc.scalar.activation(Wt[n["sq"] % 2][:, 0:width], src, ACT.Square).then_inc(sq_ready, 1)
                    n["sq"] += 1

            def square(c, src, width, tile, total, ready):
                ready(c)
                if c > 1:
                    act.wait_ge(square_added, n["added"])
                nc.scalar.activation((total if c == 0 else tile)[:, 0:width], src, ACT.Square).then_inc(square_ready, 1)
                n["added"] += c > 0
                n["sq"] += c == DC - 1

            def root(width, dim, heads=1):
                act.wait_ge(sq_used, n["sq"])
                wait(act, rs_ready, n["inst"] - 1)
                k, a = heads * width // P, 12 * (n["inst"] % 2)
                nc.scalar.activation(rootT[:, a:a + k], MM[:, 0:k], ACT.Sqrt, bias=eps,
                                     scale=1.0 / dim).then_inc(sd_ready, 1)
                n["inst"] += 1

            def high_operand(dst, src, scale=None):
                if scale is None:
                    nc.scalar.activation(dst, src, ACT.Copy).then_inc(operand_hi, 1)
                else:
                    nc.scalar.activation(dst, src, ACT.Copy, scale=scale).then_inc(operand_hi, 1)
                n["op"] += 1

            def norm_mod(l, which, width):
                root(width, 1024)
                if l == 0 and which == 0:
                    high(0, ring_shift(0))
                    high(1, ring_shift(0))
                for c in range(DC):
                    act.wait_ge(t_ready, n["t"] + 1)
                    n["t"] += 1
                    for dst in (XH[:, c, :], W[4 + c % 4][:, :])[:1 + c % 2]:
                        for s, (t0, tn) in enumerate([s for s in SEGS if s[0] < width]):
                            m = 2 * ((24 if which else 0) + c) + s
                            ins = nc.scalar.activation(dst[:, t0:t0 + tn], W[4 + c % 4][:, t0:t0 + tn], ACT.Identity,
                                                       bias=pa(f"mod{l}")[:, m:m + 1])
                    ins.then_inc(operand_hi, 1)
                    n["op"] += 1

            def normed_high(dst, Wt):
                for c in range(len(dst)):
                    act.wait_ge(t_ready, n["t"] + 1)
                    n["t"] += 1
                    high_operand(dst[c], Wt[6 + c % 2][:, 0:NX])

            def mix_out(src, dst, scale=None):
                act.wait_ge(mp_ready, n["mp"] + 1)
                n["mp"] += 1
                high_operand(dst, src, scale)

            def attention(units, scale, tiles, finish, steps={}, step=None, ahead=1):
                ends = head_ends(units)
                base = n["unit"]

                def exps(i):
                    nk = units[i][3]
                    act.wait_ge(negmax_ready, base + i + 1)
                    wait(act, probsT_ready, base + i - 1 if i >= 2 else base)
                    s = (base + i) % 4
                    nc.scalar.activation(tiles[0][i % 2][:, 0:nk], score_bank(i, ahead)[:, 0:nk], ACT.Exp, bias=stat[:, 4 + s:5 + s],
                                         scale=scale, accum_out=stat[:, 8 + s:9 + s]).then_inc(exp_done, 1)

                def copies(i):
                    nk = units[i][3]
                    act.wait_ge(probsT_ready, base + i + 1)
                    wait(act, pv_done, base + i - 1 if i >= 2 else base)
                    nc.scalar.activation(tiles[1][i % 2][:, 0:nk], M0[:, 0:nk], ACT.Copy).then_inc(probsT_copied, 1)

                def end(i):
                    if i in ends:
                        act.wait_ge(pv_done, base + i + 1)
                        finish(*ends[i])

                for i in range(ahead):
                    exps(i)
                for i in range(len(units)):
                    if ahead == 1 and i + 1 < len(units):
                        exps(i + 1)
                    copies(i)
                    if ahead == 2 and i + 2 < len(units):
                        exps(i + 2)
                    if i >= 1:
                        end(i - 1)
                    if i in steps:
                        step(*steps[i])
                end(len(units) - 1)
                n["unit"] += len(units)

            act.wait_ge(par_landed, 32)
            nc.scalar.activation(silu_cp[:, :], pa("c"), ACT.Silu)
            act.wait_ge(c_landed, 16)
            nc.scalar.activation(silu_c[:, :], silu_c[:, :], ACT.Silu).then_inc(c_ready, 1)
            act.wait_ge(x_landed, 16)

            for l in range(2):
                width, segs = tok(l)
                nseg = len(segs)

                if l == 0:
                    for c in range(DC):
                        square(c, X[:, c, 0:NT], NT, W[0], W[1], lambda c: None)
                norm_mod(l, 0, NT)
                act.dma_start(cosT[:, :], d["cosx"]).then_inc(rope_landed, 16)
                act.dma_start(sinT[:, :], d["sinx"]).then_inc(rope_landed, 16)
                act.dma_start(smallw[:, :], d["small"][l]).then_inc(small_landed, 16)

                def win_out(i, u, src, free, l=l, segs=segs):
                    p = 4 * i + u
                    tw = win_width(l, p)
                    if p in (0, 2):
                        if p == 2:
                            freed(act, GEMM[f"win{l}"].j0 + 1)
                        ins = nc.scalar.activation(pA[:, 0:tw], src[:, 0:tw], ACT.Sigmoid)
                    elif p in (1, 3):
                        return
                    elif p > 10:
                        for s, (t0, tn) in enumerate(segs):
                            ins = nc.scalar.activation(pp[:, p - 11, PP_AT[s]:PP_AT[s] + tn], src[:, t0:t0 + tn], ACT.Copy)
                    elif p != 8:
                        ins = nc.scalar.activation(PR[:, (p - 2) if p < 8 else (p - 9), 0:tw], src[:, 0:tw], ACT.Copy)
                    else:
                        ins = nc.scalar.activation(W[5][:, 0:tw], src[:, 0:tw], ACT.Copy)
                    ins.then_inc(free, 1)

                def qk_norm(i, u, l=l):
                    p = 4 * i + u
                    if 5 <= p <= 8:
                        root(win_width(l, p - 1), 64, 2)
                    if 4 <= p <= 7:
                        tw = win_width(l, p)
                        rms([PR[:, p - 2, 0:tw]], tw, W, lambda _: freed(act, GEMM[f"win{l}"].j0 + p))
                    if p == 11:
                        n["turn"] += 1
                        act.wait_ge(turned, n["turn"])
                        nc.scalar.activation(vtok[:, 0:NT], M0[:, 0:NT], ACT.Copy).then_inc(turn_copied, 1)

                stage(f"win{l}", win_out, qk_norm)

                nb, fb = width // P, 6 * l
                act.wait_ge(rope_done, 4 * (l + 1))
                def table_load(tb):
                    if tb < 4:
                        act.dma_start(dft[tb % 3][:, 0:1024], d["dftx"][tb]).then_inc(dft_landed[tb % 3], 16)
                    else:
                        act.dma_start(dft[tb % 3][:, 0:512], d["dftc"][tb - 4]).then_inc(dft_landed[tb % 3], 16)

                for tb in range(3):
                    table_load(tb)
                for tb in range(nb):
                    act.wait_ge(ft_ready, fb + tb + 1)
                    nc.scalar.activation(ftok[:, tb * 512:(tb + 1) * 512], M0[:, 512 * (tb % 2):512 * (tb % 2) + 512],
                                         ACT.Copy).then_inc(ft_copied, 1)
                for tb in range(3, nb):
                    act.wait_ge(dft_used, fb + tb - 2)
                    table_load(tb)
                act.wait_ge(dft_used, fb + nb)
                for c in range(2):
                    nc.scalar.activation(PR[:, c, 0:width], G[c][:, 0:width], ACT.Copy).then_inc(fy_copied, 1)
                for m in range(2):
                    mix_out(small_out(l, m)[:, 0:width], XH[:, 2 + m, 0:width])

                def finish1(h, q0, qn):
                    part = slice(64 * (h % 2), 64 * (h % 2) + 64)
                    high_operand(XH[part, h // 2, q0:q0 + qn], M1[part, 0:qn])

                def mixer_step(kind, m, s, l=l, segs=segs, width=width):
                    t0, tn = segs[s]
                    if kind == "square":
                        act.wait_ge(ln_centered, 2 + l)
                        rms([acc[:, c, 0:width] for c in range(2)], width, W[4:8], lambda c: None)
                    elif kind == "sum":
                        root(width, 256)
                    elif kind == "silu":
                        act.wait_ge(ln_scaled, 2 + l)
                        for c in range(2):
                            nc.scalar.activation(acc[:, c, 0:width], acc[:, c, 0:width], ACT.Silu,
                                                 scale=pa(f"lng{l}")[:, c:c + 1], bias=pa(f"lnb{l}")[:, c:c + 1]).then_inc(ln_act, 1)
                    elif kind == "pointwise":
                        mix_out(MM[:, 0:tn], XH[:, 4 + m, t0:t0 + tn])
                    elif kind == "pool":
                        mix_out(MM[:, 0:tn], XH[:, 6 + m, t0:t0 + tn], pa(f"psc{l}")[:, m:m + 1])

                attention(units1(l), 0.125, (W[0:2], W[2:4]), finish1, mixer_steps(l), mixer_step)

                def mod_load(i, u, base, count):
                    if isinstance(i, int) and 4 * i + u >= count:
                        return
                    wait(act, mod_step, 16 * i + mods_done(MOD_ALL + base + u - 1))
                    for q in range(2):
                        act.dma_start(mod_half[q][:, :], d["wmod"][MOD_ALL + base + 4 * i + u, :, q * NX:(q + 1) * NX]
                                      ).then_inc(half_landed[q], 16)

                def chunk_square(c, g, width, tile, total):
                    square(c, X[:, c, 0:width], width, tile, total, lambda c: freed(act, g.j0 + c))

                if l == 0:
                    mod_load(0, 0, 0, 8)

                def mod_and_square(i, u, l=l):
                    if l == 0:
                        mod_load(0, 4 * i + u + 1, 0, 8)
                    chunk_square(4 * i + u, GEMM[f"wout{l}"], width, W[0], W[1])

                stage(f"wout{l}", None, mod_and_square, True)
                norm_mod(l, 1, width)

                for half in range(2):
                    g = GEMM[f"fin{l}{half}"]

                    def silu(i, u, src, free, g=g):
                        if u % 2 == 0:
                            wait(act, bank_free[(g.j0 + u - 1) % 2], (g.j0 + u - 1) // 2 + 2 * i + 1)
                            nc.scalar.activation(fsilu[:, 0:width], src[:, 0:width], ACT.Silu).then_inc(free, 1)

                    def hidden(i, u, g=g):
                        if u % 2:
                            _, b, used, _, _ = where(g, i, u)
                            act.wait_ge(bank_free[b], used + 1)
                            nc.scalar.activation(HH[:, 2 * i + u // 2, 0:width], fh[:, 0:width], ACT.Copy).then_inc(h_hi, 1)

                    def hidden_and_mod(i, u, hidden=hidden, half=half):
                        if l == 0:
                            mod_load(i, u, 8 + 30 * half, 22)
                        hidden(i, u)

                    stage(g.name, silu, hidden_and_mod)
                    def mod_and_square(i, u, half=half):
                        if l == 0:
                            mod_load(i, u, 30 + 30 * half, 4 if half else 8)
                        if half:
                            chunk_square(4 * i + u, GEMM[f"fout{l}1"], width, fsilu, fh)

                    stage(f"fout{l}{half}", None, mod_and_square, half == 1)

            act.wait_ge(rope_done, 8)
            act.dma_start(sinT[:, :].bitcast(I32), d["pos"]).then_inc(rope_landed, 16)
            root(NX, 1024)
            normed_high([XH[:, c, 0:NX] for c in range(DC)], W)

            def sines(i, u):
                if 4 * i + u == 5:
                    act.wait_ge(trig, 2)
                    nc.scalar.activation(sinT[:, :], W[0][:, 0:NX], ACT.Sin).then_inc(act_step, 1)
                    nc.scalar.activation(cosT[:, :], W[1][:, 0:NX], ACT.Sin).then_inc(act_step, 1)
            stage("eqk", lambda i, u, src, free: nc.scalar.activation(QK[:, 4 * i + u, :], src[:, 0:NX], ACT.Copy).then_inc(free, 1),
                  sines)
            act.wait_ge(act_step, 2)
            for h in range(2):
                act.dma_start(decay[h][:, :], d["decay"][h]).then_inc(decay_landed[h], 16)

            def value_stage(name, tiles, dst):
                def out(i, u, src, free):
                    nc.scalar.activation(tiles[(GEMM[name].j0 + u) % 2][:, 0:NX], src[:, 0:NX], ACT.Copy).then_inc(free, 1)

                def by_token(p):
                    act.wait_ge(turned, n["turn"] + 1)
                    nc.scalar.activation(dst[:, :, p * P:(p + 1) * P],
                                         M0[:, 512 * (n["turn"] % 2):512 * (n["turn"] % 2) + 512].rearrange("p (b f) -> p b f", b=4),
                                         ACT.Copy).then_inc(turn_copied, 1)
                    n["turn"] += 1
                stage(name, out, lambda i, u: by_token(4 * i + u - 1) if 4 * i + u else None)
                by_token(7)

            value_stage("ev", vfE, VE)
            for h in range(8):
                act.wait_ge(ret_pv, h + 1)
                nc.scalar.activation(RT[:, h, :], (M1, MM)[h % 2][:, 0:NX], ACT.Copy).then_inc(ret_copied, 1)
                if h + 2 < 8:
                    act.wait_ge(ret_masked, h + 1)
                    act.dma_start(decay[h % 2][:, :], d["decay"][h + 2]).then_inc(decay_landed[h % 2], 16)

            def head_square(h):
                rms([RT[:, h, :]], NX, W, lambda _: act.wait_ge(ret_copied, 8))

            for h in range(2):
                head_square(h)
                root(NX, 128)
            head_square(2)

            def eg_out(i, u, src, free):
                wait(act, t_ready, n["t"] - 1)
                nc.scalar.activation(W[4 + u % 2][:, 0:NX], src[:, 0:NX], ACT.Silu).then_inc(free, 1)

            def eg_high(i, u):
                h = 4 * i + u + 2
                if h < 8:
                    root(NX, 128)
                if h + 1 < 8:
                    head_square(h + 1)
                act.wait_ge(t_ready, n["t"] + 1)
                n["t"] += 1
                high_operand(MH[:, 4 * i + u, :], W[6 + u % 2][:, 0:NX])
            stage("eg", eg_out, eg_high)
            stage("eout0")
            t0, op0 = n["t"], n["op"]

            def ce_out(i, u, src, free):
                if u == 3:
                    wait(act, t_ready, t0 + i)
                    nc.scalar.activation(ce_s[:, 0:NX], src[:, 0:NX], ACT.Silu).then_inc(free, 1)

            def ce_high(i, u):
                if u == 3:
                    act.wait_ge(t_ready, t0 + i + 1)
                    nc.scalar.activation(MH[:, i, :], ce_z[:, 0:NX], ACT.Copy).then_inc(operand_hi, 1)
            stage("econv", ce_out, ce_high)
            n["t"] += 8
            n["op"] += 8
            stage("eout1", None, lambda i, u: square(4 * i + u, Y[:, 4 * i + u, :], NX, W[0], W[1],
                                                     lambda c: freed(act, GEMM["eout1"].j0 + c)), True)
            root(NX, 1024)

            rms([X[:, c, 0:NX] for c in range(DC)], NX, W, lambda c: act.wait_ge(resid_ready, c + 1))
            root(NX, 1024)
            normed_high([XH[:, c, 0:NX] for c in range(DC)], W)

            def oin_out(i, u, src, free):
                p = 4 * i + u
                nc.scalar.activation(LAT[:, p, :] if p < 5 else kr[:, 0:NX], src[:, 0:NX], ACT.Copy).then_inc(free, 1)
            stage("oin", oin_out)
            rms([LAT[:, c, :] for c in range(3)], NX, WL, lambda c: None)

            def latent_norm(i, u):
                p = 4 * i + u
                if p == 0:
                    root(NX, 384)
                    rms([LAT[:, c, :] for c in range(3, 5)], NX, WL, lambda c: None)
                elif p == 2:
                    root(NX, 256)
                    normed_high([LQH[:, c, :] for c in range(3)], WL)
                elif p == 4:
                    normed_high([LKH[:, c, :] for c in range(2)], WL)
            stage("ogate", lambda i, u, src, free: nc.scalar.activation(SG[:, 4 * i + u, :], src[:, 0:NX], ACT.Silu).then_inc(free, 1),
                  latent_norm)

            def oq_out(i, u, src, free):
                p = 4 * i + u
                if p < 8:
                    nc.scalar.activation(QN[:, p, :], src[:, 0:NX], ACT.Copy).then_inc(free, 1)
                else:
                    nc.scalar.activation(QR[:, 2 * (p - 8):2 * (p - 8) + 2, :],
                                         src[:, 0:NX].rearrange("p (a t) -> p a t", a=2), ACT.Copy).then_inc(free, 1)
            act.wait_ge(operand_lo, n["op"])
            stage("oq", oq_out)
            stage("ok", lambda i, u, src, free: nc.scalar.activation(KN[:, 4 * i + u, :], src[:, 0:NX], ACT.Copy).then_inc(free, 1))

            value_stage("ov", vfD, VO)
            gates = [0]

            def finish2(h, q0, qn):
                gates[0] += 1
                act.wait_ge(gated, gates[0])
                high_operand(XH[:, h, 0:NX], SG[:, h, :])
            attention(units2, 192.0 ** -0.5, (dprobs, dprobsT), finish2, ahead=2)
            stage("oout", None, lambda i, u: square(4 * i + u, Y2[:, 4 * i + u, :], NX, WY[0], WY[1],
                                                    lambda c: freed(act, GEMM["oout"].j0 + c)), True)
            root(NX, 1024)

        @block.vector
        def _(dve):
            n = dict(inst=0, op=0, t=0, step=0, rope=0, unit=0, squared=0, added=0, spread=0)

            def link(ins):
                n["step"] += 1
                ins.then_inc(dve_step, 1)
                dve.wait_ge(dve_step, n["step"])

            def add_square(c, width, tile, total):
                n["squared"] += 1
                if c:
                    dve.wait_ge(square_ready, n["squared"])
                    wait(dve, square_added, n["added"])
                    nc.vector.tensor_tensor(total[:, 0:width], total[:, 0:width], tile[:, 0:width], ALU.add).then_inc(square_added, 1)
                    n["added"] += 1

            def invert_roots(width, Wt, heads=1):
                dve.wait_ge(sd_ready, n["inst"] + 1)
                k, a = heads * width // P, 12 * (n["inst"] % 2)
                r = rootT[:, a:a + k]
                wait(dve, rb_ready, n["inst"] - 1)
                link(nc.vector.reciprocal(r, r))
                nc.vector.tensor_copy(Wt[2 + n["inst"] % 2][:, 0:width].rearrange("p (k f) -> p k f", k=k),
                                      r.unsqueeze(2).broadcast_to([P, k, P // heads])).then_inc(rs_ready, 1)
                n["inst"] += 1

            def inverted(width):
                n["spread"] += 1
                dve.wait_ge(rb_ready, n["spread"])
                return M0[:, 0:width]

            def invert(width, Wt):
                invert_roots(width, Wt)
                return inverted(width)

            def low_operand(dst, src, hi, scale=None):
                dve.wait_ge(operand_hi, n["op"] + 1)
                if scale is None:
                    ins = nc.vector.tensor_tensor(dst, src, hi.bitcast(F32), ALU.subtract)
                else:
                    ins = nc.vector.scalar_tensor_tensor(dst, src, scale, hi.bitcast(F32), ALU.mult, ALU.subtract)
                ins.then_inc(operand_lo, 1)
                n["op"] += 1

            def norm_mod(l, which, width):
                r = invert(width, W)
                ws = [s for s in SEGS if s[0] < width]

                op0, odd0 = n["op"], DC // 2 * (2 * l + which)

                def low(c):
                    dve.wait_ge(operand_hi, op0 + c + 1)
                    for s, (t0, tn) in enumerate(ws):
                        m = 2 * ((24 if which else 0) + c) + s
                        ins = nc.vector.scalar_tensor_tensor(XL[:, c, t0:t0 + tn], W[4 + c % 4][:, t0:t0 + tn],
                                                             pa(f"mod{l}")[:, m:m + 1],
                                                             XH[:, c, t0:t0 + tn].bitcast(F32), ALU.add, ALU.subtract)
                    ins.then_inc(operand_lo, 2)

                for c in range(DC):
                    if c >= 4:
                        if c % 2:
                            dve.wait_ge(odd_lo, odd0 + (c - 4) // 2 + 1)
                        else:
                            dve.wait_ge(operand_lo, op0 + c - 2)
                    for s, (t0, tn) in enumerate(ws):
                        a = 16 * which + 8 * s + c
                        ins = nc.vector.scalar_tensor_tensor(W[4 + c % 4][:, t0:t0 + tn], X[:, c, t0:t0 + tn], afac[:, a:a + 1],
                                                             r[:, t0:t0 + tn], ALU.mult, ALU.mult)
                    ins.then_inc(t_ready, 1)
                    n["t"] += 1
                    if c % 2:
                        low(c - 1)
                n["op"] += DC

            def norm_plain(sources, gain, Wt, high, low):
                r = invert(NX, Wt)
                k = len(sources)
                for c in range(k + 1):
                    if c < k:
                        wait(dve, operand_lo, n["op"] - (1 if c < 2 else 0))
                        nc.vector.scalar_tensor_tensor(Wt[6 + c % 2][:, 0:NX], sources[c], gain[:, c:c + 1], r,
                                                       ALU.mult, ALU.mult).then_inc(t_ready, 1)
                        n["t"] += 1
                    if c:
                        low_operand(low[:, c - 1, 0:NX], Wt[6 + (c - 1) % 2][:, 0:NX], high[:, c - 1, 0:NX])

            def norm_post(Yt, gain, Wt):
                r = invert(NX, Wt)
                for c in range(DC):
                    t = Wt[4 + c % 2][:, 0:NX]
                    link(nc.vector.scalar_tensor_tensor(t, Yt[:, c, :], gain[:, c:c + 1], r, ALU.mult, ALU.mult))
                    nc.vector.tensor_tensor(X[:, c, 0:NX], X[:, c, 0:NX], t, ALU.add).then_inc(resid_ready, 1)

            def rope(chunk, tmp, three=False):
                view = (lambda a: a.rearrange("p (a t) -> p a t", a=2)) if three else (lambda a: a)
                dve.wait_ge(rot_ready, n["rope"] + 1)
                n["rope"] += 1
                link(nc.vector.tensor_tensor(view(tmp), view(M1[:, 0:NX]), view(sinT[:, :]), ALU.mult))
                link(nc.vector.tensor_tensor(chunk, chunk, view(cosT[:, :]), ALU.mult))
                nc.vector.tensor_tensor(chunk, chunk, view(tmp), ALU.add).then_inc(rope_done, 1)

            def mod_product(k, u, halves, landed):
                junk = PR[:, 0, :] if isinstance(k, int) and MOD_FIRST <= k < MOD_ALL else M1
                for q in range(2):
                    dve.wait_ge(*landed(q))
                    wait(dve, mod_step, 4 * (k - MOD_DVE) + 2 * q)
                    if not (isinstance(k, int) and k in MOD_STARTS):
                        add_sums(k - 1, 1 - u % 2, q)
                    for s in range(2):
                        nc.vector.tensor_tensor_reduce((junk[:, 0:NX], halves[q])[s], halves[q],
                                                       silu_c[:, 1024 * s + NX * q:1024 * s + NX * (q + 1)], 1.0, 0.0, ALU.mult,
                                                       ALU.add, sums[:, 4 * (u % 2) + 2 * q + s:4 * (u % 2) + 2 * q + s + 1]
                                                       ).then_inc(mod_step, 1)

            def add_sums(k, slot, q):
                col = par[:, bass.ds(2 * k + PAR["mod0"][0], 2)]
                return nc.vector.tensor_tensor(col, col, sums[:, 4 * slot + 2 * q:4 * slot + 2 * q + 2], ALU.add)

            def last_sums(k):
                dve.wait_ge(mod_step, mods_done(k))
                for q in range(2):
                    link(add_sums(k, k % 2, q))

            def ring_mod(k):
                r = mod_ring(k)
                src = raw[r % RAW]
                mod_product(k, k, (src[:, 0:NX], src[:, NX:2 * NX]), lambda q: (raw_landed[r % RAW], 16 * (r // RAW + 1)))

            def half_mod(i, u, base, count):
                if isinstance(i, int) and 4 * i + u >= count:
                    return
                mod_product(4 * i + (MOD_ALL + base + u), u, [m[:, :] for m in mod_half],
                            lambda q: (half_landed[q], 64 * i + 16 * (base + u + 1)))
                if isinstance(i, int) and 4 * i + u == count - 1:
                    last_sums(MOD_ALL + base + count - 1)

            def modulation(l, which):
                m3 = pa(f"mod{l}").rearrange("p (m s) -> p m s", s=2)
                for s in range(2):
                    ins = nc.vector.scalar_tensor_tensor(afac[:, 16 * which + 8 * s:16 * which + 8 * s + 8],
                                                         m3[:, 8 + 24 * which:16 + 24 * which, s], 1.0,
                                                         pa(("g1", "g2")[which] + str(l)), ALU.add, ALU.mult)
                link(ins)

            def gated_add(name, l, segs, m0, after=None, squares=None, before=None):
                g = GEMM[name]
                for p in range(g.n):
                    j, b, _, _, _ = where(g, 0, p)
                    if p and squares is not None:
                        add_square(p - 1, *squares)
                    if before is not None:
                        before(p)
                    dve.wait_ge(panel_done, j + 1)
                    for s, (t0, tn) in enumerate(segs):
                        col = 2 * (m0 + p) + s
                        ins = nc.vector.scalar_tensor_tensor(X[:, p, t0:t0 + tn], G[b][:, t0:t0 + tn],
                                                             pa(f"mod{l}")[:, col:col + 1],
                                                             X[:, p, t0:t0 + tn], ALU.mult, ALU.add)
                    ins.then_inc(bank_free[b], 1)
                    if after is not None:
                        after(p)
                if squares is not None:
                    add_square(7, *squares)

            def attention(units, scale, tiles, finish, masked, beside=None, steps={}, step=None, ahead=1):
                ends = head_ends(units)
                base = n["unit"]

                def tops(i):
                    nk = units[i][3]
                    s = (base + i) % 4
                    dve.wait_ge(scores_ready, base + i + 1)
                    if masked:
                        diag = score_bank(i, ahead)[:, nk - P:nk]
                        link(nc.vector.tensor_tensor(diag, diag, co("mask"), ALU.add))
                    link(nc.vector.tensor_reduce(stat[:, s:s + 1], score_bank(i, ahead)[:, 0:nk], AX.X, ALU.max))
                    nc.vector.tensor_scalar(stat[:, 4 + s:5 + s], stat[:, s:s + 1], -scale, None, ALU.mult).then_inc(negmax_ready, 1)

                def norms(i):
                    nk = units[i][3]
                    s = (base + i) % 4
                    t = tiles[0][i % 2][:, 0:nk]
                    dve.wait_ge(exp_done, base + i + 1)
                    link(nc.vector.reciprocal(stat[:, 12 + s:13 + s], stat[:, 8 + s:9 + s]))
                    nc.vector.tensor_scalar(t, t, stat[:, 12 + s:13 + s], None, ALU.mult).then_inc(probs_ready, 1)

                for i in range(ahead):
                    tops(i)
                for i in range(len(units)):
                    norms(i)
                    if i + ahead < len(units):
                        tops(i + ahead)
                    if beside is not None:
                        beside(i)
                    if i - 1 in ends:
                        finish(base + i, *ends[i - 1])
                    if i in steps:
                        step(*steps[i])
                finish(base + len(units), *ends[len(units) - 1])
                n["unit"] += len(units)

            dve.wait_ge(par_landed, 32)
            dve.wait_ge(c_ready, 1)
            for k in range(MOD_DVE, MOD_FIRST):
                ring_mod(k)
            last_sums(MOD_FIRST - 1)
            dve.wait_ge(shift_used, MOD_DVE)
            shift = pa("mod0")[:, 0:2 * MOD_DVE]
            nc.vector.tensor_tensor(shift, shift, M0[:, 0:2 * MOD_DVE], ALU.add).then_inc(shift_read, 1)
            dve.wait_ge(shift_read, 1)
            n["squared"] += DC
            n["added"] += DC - 1
            modulation(0, 0)
            dve.wait_ge(x_landed, 16)
            for l in range(2):
                width, segs = tok(l)
                norm_mod(l, 0, NT)
                g = GEMM[f"win{l}"]
                for c in range(2):
                    for a, b_ in ((0, HALO), (GLU_AT[0] + NX, GLU_AT[1]), (GLU_AT[1] + NC, GLU_W)):
                        nc.vector.memset(glu[:, c, a:b_], 0.0)
                    for a, b_ in ((0, POOLPAD), (PP_AT[0] + NX, PP_AT[1]), (PP_AT[1] + NC, PP_W)):
                        ins = nc.vector.memset(pp[:, c, a:b_], 0.0)
                    if l == 1:
                        nc.vector.memset(glu[:, c, GLU_AT[1]:GLU_AT[1] + NC], 0.0)
                        ins = nc.vector.memset(pp[:, c, PP_AT[1]:PP_AT[1] + NC], 0.0)
                link(ins)
                for c in range(2):
                    j, b = g.j0 + 2 * c + 1, (g.j0 + 2 * c + 1) % 2
                    dve.wait_ge(panel_done, j + 1)
                    freed(dve, j - 1)
                    for s, (t0, tn) in enumerate(segs):
                        ins = nc.vector.tensor_tensor(glu[:, c, GLU_AT[s]:GLU_AT[s] + tn], G[b][:, t0:t0 + tn],
                                                      pA[:, t0:t0 + tn], ALU.mult)
                    ins.then_inc(bank_free[b], 1)
                freed(dve, g.j0 + 1)
                freed(dve, g.j0 + 3)

                runs = [(c, s, t0, tn) for c in range(2) for s, (t0, tn) in enumerate(segs)]
                per, base = len(runs), (CONV * 4 if l else 0)
                dwa, dwba = PAR[f"dw{l}"][0], PAR[f"dwb{l}"][0]
                for c, s, t0, tn in runs:
                    a = GLU_AT[s] - HALO
                    nc.vector.tensor_scalar(acc[:, c, t0:t0 + tn], glu[:, c, a:a + tn], par[:, dwa + c * CONV:dwa + c * CONV + 1],
                                            par[:, dwba + c:dwba + c + 1], ALU.mult, ALU.add).then_inc(conv_tick, 1)

                def conv_taps(first, stop):
                    with dve.Fori(first, stop) as tap:
                        for k, (c, s, t0, tn) in enumerate(runs):
                            dve.wait_ge(conv_tick, per * tap + (base - per + k + 1))
                            nc.vector.scalar_tensor_tensor(acc[:, c, t0:t0 + tn],
                                                           glu[:, c, bass.ds(tap + (GLU_AT[s] - HALO), tn)],
                                                           par[:, bass.ds(tap + (dwa + c * CONV), 1)], acc[:, c, t0:t0 + tn],
                                                           ALU.mult, ALU.add).then_inc(conv_tick, 1)

                conv_taps(1, 6)
                dve.wait_ge(rope_landed, 32 * (l + 1))
                for p in range(5, 11):
                    if 2 <= p - 3 <= 5:
                        invert_roots(win_width(l, p - 1), W, 2)
                    if 2 <= p - 4 <= 5:
                        c, tw = p - 4, win_width(l, p - 2)
                        r = inverted(tw)
                        nc.vector.scalar_tensor_tensor(PR[:, c, 0:tw], PR[:, c, 0:tw], pa(f"qg{l}" if c < 4 else f"kg{l}"), r,
                                                       ALU.mult, ALU.mult).then_inc(qk_normed, 1)
                    if 2 <= p - 5 <= 5:
                        rope(PR[:, p - 5, 0:NX], W[4][:, 0:NX])
                    conv_taps(p + 1, p + 2)
                conv_taps(12, CONV)

                def pooling(c, g=g, segs=segs):
                    freed(dve, g.j0 + 11 + c)
                    u, hi_part, lo_part = pp[:, c, :], slice(64, P), slice(0, 64)
                    e = PP_W
                    link(nc.vector.tensor_tensor(pA[:, 1:e], u[:, 0:e - 1], u[:, 1:e], ALU.add))
                    if c == 0:
                        nc.vector.tensor_tensor(pB[hi_part, 2:e - 2], pA[hi_part, 1:e - 3], pA[hi_part, 3:e - 1], ALU.add)
                        link(nc.vector.tensor_copy(pB[lo_part, 2:e - 2], pA[lo_part, 2:e - 2]))
                    else:
                        link(nc.vector.tensor_tensor(pB[:, 2:e - 2], pA[:, 1:e - 3], pA[:, 3:e - 1], ALU.add))
                        link(nc.vector.tensor_tensor(pA[:, 4:e - 4], pB[:, 2:e - 6], pB[:, 6:e - 2], ALU.add))
                        nc.vector.tensor_tensor(pB[hi_part, 8:e - 8], pA[hi_part, 4:e - 12], pA[hi_part, 12:e - 4], ALU.add)
                        link(nc.vector.tensor_copy(pB[lo_part, 8:e - 8], pA[lo_part, 8:e - 8]))
                    for s, (t0, tn) in enumerate(segs):
                        a = PP_AT[s]
                        for side, q in enumerate((a, a + tn - 8)):
                            tab = co("edge")[:, 16 * c + 8 * side:16 * c + 8 * side + 8]
                            ins = nc.vector.tensor_tensor(pB[:, q:q + 8], pB[:, q:q + 8], tab, ALU.mult)
                    link(ins)
                    for s, (t0, tn) in enumerate(segs):
                        a = PP_AT[s]
                        ins = nc.vector.scalar_tensor_tensor(pp[:, c, a:a + tn], pB[:, a:a + tn], co("invw")[:, c:c + 1],
                                                             pp[:, c, a:a + tn], ALU.mult, ALU.subtract)
                    ins.then_inc(pool_ready, 1)

                for m in range(2):
                    low_operand(XL[:, 2 + m, 0:width], small_out(l, m)[:, 0:width], XH[:, 2 + m, 0:width])

                def finish1(_, h, q0, qn):
                    part = slice(64 * (h % 2), 64 * (h % 2) + 64)
                    low_operand(XL[part, h // 2, q0:q0 + qn], M1[part, 0:qn], XH[part, h // 2, q0:q0 + qn])

                def beside(i, l=l):
                    if i in (1, 3):
                        pooling(i // 2)
                    if l == 0 and i < MOD_ALL - MOD_FIRST:
                        ring_mod(MOD_FIRST + i)

                def mixer_step(kind, m, s, l=l, segs=segs, width=width):
                    t0, tn = segs[s]
                    done = 2 * l + s
                    if kind == "mean":
                        dve.wait_ge(ln_sum, done + 1)
                        for c in range(2):
                            ins = nc.vector.scalar_tensor_tensor(acc[:, c, t0:t0 + tn], MM[:, 0:tn], -1.0 / 256,
                                                                 acc[:, c, t0:t0 + tn], ALU.mult, ALU.add)
                        ins.then_inc(ln_centered, 1)
                    elif kind == "sum":
                        invert_roots(width, W[4:8])
                    elif kind == "spread":
                        if s == len(segs) - 1:
                            inverted(tn)
                        else:
                            dve.wait_ge(ln_spread, 1)
                        for c in range(2):
                            ins = nc.vector.tensor_tensor(acc[:, c, t0:t0 + tn], acc[:, c, t0:t0 + tn], MM[:, 0:tn], ALU.mult)
                        ins.then_inc(ln_scaled, 1)
                    elif kind == "pointwise":
                        low_operand(XL[:, 4 + m, t0:t0 + tn], MM[:, 0:tn], XH[:, 4 + m, t0:t0 + tn])
                    elif kind == "pool":
                        low_operand(XL[:, 6 + m, t0:t0 + tn], MM[:, 0:tn], XH[:, 6 + m, t0:t0 + tn], pa(f"psc{l}")[:, m:m + 1])

                attention(units1(l), 0.125, (W[0:2], W[2:4]), finish1, False, beside, mixer_steps(l), mixer_step)

                if l == 0:
                    last_sums(MOD_ALL - 1)
                gated_add(f"wout{l}", l, segs, 16, None, (width, W[0], W[1]),
                          (lambda p: half_mod(0, p, 0, 8)) if l == 0 else None)
                if l == 0:
                    modulation(0, 1)
                freed(dve, last(f"wout{l}"))
                freed(dve, last(f"wout{l}") - 1)
                norm_mod(l, 1, width)
                for half in range(2):
                    g = GEMM[f"fin{l}{half}"]

                    def hidden(i, u, g=g, l=l, half=half):
                        if l == 0 and u % 2 == 0:
                            half_mod(i, u, 8 + 30 * half, 22)
                        if u % 2 == 0:
                            return
                        j, b, used, _, _ = where(g, i, u)
                        e = FH * (2 * l + half) + 2 * i + u // 2
                        dve.wait_ge(panel_done, j + 1)
                        dve.wait_ge(bank_free[1 - b], (g.j0 + u - 1) // 2 + 2 * i + 1)
                        wait(dve, h_lo, e)
                        nc.vector.tensor_tensor(fh[:, 0:width], fsilu[:, 0:width], G[b][:, 0:width], ALU.mult).then_inc(bank_free[b], 1)
                        dve.wait_ge(h_hi, e + 1)
                        c = 2 * i + u // 2
                        nc.vector.tensor_tensor(HL[:, c, 0:width], fh[:, 0:width], HH[:, c, 0:width].bitcast(F32),
                                                ALU.subtract).then_inc(h_lo, 1)
                        if l == 0:
                            half_mod(i, u, 8 + 30 * half, 22)
                    each_panel(dve, g, hidden)
                    gated_add(f"fout{l}{half}", l, segs, 40,
                              (lambda p, half=half: half_mod(0, p, 30 + 30 * half, 4 if half else 8)) if l == 0 else None,
                              (width, fsilu, fh) if half else None)
                freed(dve, last(f"fout{l}1"))
                freed(dve, last(f"fout{l}1") - 1)
                if l == 0:
                    modulation(1, 0)
                    modulation(1, 1)

            norm_plain([X[:, c, 0:NX] for c in range(DC)], pa("pre")[:, 0:8], W, XH, XL)
            dve.wait_ge(rope_landed, 80)
            ang, k_, turns = W[4][:, 0:NX], W[5][:, 0:NX], W[6][:, 0:NX]
            magic = 1.5 * 2.0 ** 23
            tau = (6.28125, 0.0019350051879882812, 3.019915981956753e-07)
            link(nc.vector.tensor_copy(ang, sinT[:, :].bitcast(I32)))
            link(nc.vector.tensor_scalar(ang, ang, co("inv"), None, ALU.mult))
            for s in range(2):
                r = W[s][:, 0:NX]
                link(nc.vector.tensor_scalar(turns, ang, 1.0 / (2.0 * np.pi), 0.25 * s, ALU.mult, ALU.add))
                link(nc.vector.tensor_scalar(turns, turns, magic, None, ALU.add))
                link(nc.vector.tensor_scalar(k_, turns, -magic, None, ALU.add))
                link(nc.vector.scalar_tensor_tensor(r, k_, -tau[0], ang, ALU.mult, ALU.add))
                link(nc.vector.scalar_tensor_tensor(r, k_, -tau[1], r, ALU.mult, ALU.add))
                link(nc.vector.scalar_tensor_tensor(r, k_, -tau[2], r, ALU.mult, ALU.add))
                if s:
                    link(nc.vector.tensor_scalar(r, r, float(np.pi / 2), None, ALU.add))
                nc.vector.tensor_scalar(r, r, 3.1415925, -3.1415925, ALU.min, ALU.max).then_inc(trig, 1)
            dve.wait_ge(act_step, 2)
            for c in range(8):
                freed(dve, GEMM["eqk"].j0 + c)
                rope(QK[:, c, :], W[4][:, 0:NX])

            for h in range(8):
                dve.wait_ge(ret_scores, h + 1)
                dve.wait_ge(decay_landed[h % 2], 16 * (h // 2 + 1))
                wait(dve, ret_pv, h - 1)
                for jb, c0, cn in RET_AT:
                    src = G[h % 2][:, c0:c0 + cn] if c0 < 1024 else M0[:, 512 * (h % 2):512 * (h % 2) + cn]
                    ins = nc.vector.tensor_tensor(scT[h % 2][:, c0:c0 + cn], src, decay[h % 2][:, 0:cn], ALU.mult)
                ins.then_inc(ret_masked, 1)
            def head_normed(h):
                r = inverted(NX)
                nc.vector.scalar_tensor_tensor(RT[:, h, :], RT[:, h, :], pa("gn")[:, h:h + 1], r, ALU.mult,
                                               ALU.mult).then_inc(ret_normed, 1)

            invert_roots(NX, W)
            g = GEMM["eg"]
            for p in range(8):
                head_normed(p)
                if p < 7:
                    invert_roots(NX, W)
                dve.wait_ge(ret_normed, p + 1)
                freed(dve, g.j0 + p)
                wait(dve, operand_lo, n["op"])
                nc.vector.tensor_tensor(W[6 + p % 2][:, 0:NX], W[4 + p % 2][:, 0:NX], RT[:, p, :], ALU.mult).then_inc(t_ready, 1)
                n["t"] += 1
                low_operand(ML[:, p, :], W[6 + p % 2][:, 0:NX], MH[:, p, :])
            g = GEMM["eout0"]
            for p in range(8):
                j, b = g.j0 + p, (g.j0 + p) % 2
                dve.wait_ge(panel_done, j + 1)
                nc.vector.tensor_copy(Y[:, p, :], G[b][:, 0:NX]).then_inc(bank_free[b], 1)

            g = GEMM["econv"]
            t0, op0, cwa, cba = n["t"], n["op"], PAR["cw"][0], PAR["cb"][0]
            link(nc.vector.memset(ce_u[:, 0:2], 0.0))

            def short_conv(i, u):
                j, b, used, _, _ = where(g, i, u)
                if u < 3:
                    dve.wait_ge(panel_done, j + 1)
                if u == 0:
                    dve.wait_ge(t_ready, t0 + i)
                    nc.vector.tensor_copy(ce_c[:, 0:NX], G[b][:, 0:NX]).then_inc(bank_free[b], 1)
                elif u == 1:
                    dve.wait_ge(bank_free[1 - b], (g.j0 + u - 1) // 2 + 2 * i + 1)
                    nc.vector.tensor_tensor(ce_u[:, 2:NX + 2], G[b][:, 0:NX], ce_c[:, 0:NX], ALU.mult).then_inc(bank_free[b], 1)
                    dve.wait_ge(bank_free[b], used + 1)
                    w = [par[:, bass.ds(3 * i + (cwa + t), 1)] for t in range(3)]
                    nc.vector.tensor_scalar(ce_y[:, 0:NX], ce_u[:, 0:NX], w[0], par[:, bass.ds(i + cba, 1)], ALU.mult,
                                            ALU.add).then_inc(ce_tick, 1)
                    for t in (1, 2):
                        dve.wait_ge(ce_tick, 3 * i + t)
                        nc.vector.scalar_tensor_tensor(ce_y[:, 0:NX], ce_u[:, t:NX + t], w[t], ce_y[:, 0:NX], ALU.mult,
                                                       ALU.add).then_inc(ce_tick, 1)
                elif u == 2:
                    dve.wait_ge(ce_tick, 3 * i + 3)
                    nc.vector.tensor_tensor(ce_c[:, 0:NX], G[b][:, 0:NX], ce_y[:, 0:NX], ALU.mult).then_inc(bank_free[b], 1)
                else:
                    dve.wait_ge(bank_free[1 - b], (g.j0 + u - 1) // 2 + 2 * i + 1)
                    dve.wait_ge(bank_free[b], used + 1)
                    dve.wait_ge(operand_lo, op0 + i)
                    nc.vector.tensor_tensor(ce_z[:, 0:NX], ce_c[:, 0:NX], ce_s[:, 0:NX], ALU.mult).then_inc(t_ready, 1)
                    dve.wait_ge(operand_hi, op0 + i + 1)
                    nc.vector.tensor_tensor(ML[:, i, :], ce_z[:, 0:NX], MH[:, i, :].bitcast(F32), ALU.subtract).then_inc(operand_lo, 1)
            each_panel(dve, g, short_conv)
            n["t"] += 8
            n["op"] += 8
            g = GEMM["eout1"]
            freed(dve, last("eout0"))
            freed(dve, last("eout0") - 1)
            for p in range(8):
                j, b = g.j0 + p, (g.j0 + p) % 2
                dve.wait_ge(panel_done, j + 1)
                nc.vector.tensor_tensor(Y[:, p, :], G[b][:, 0:NX], Y[:, p, :], ALU.add).then_inc(bank_free[b], 1)
                add_square(p, NX, W[0], W[1])
            freed(dve, last("eout1"))
            freed(dve, last("eout1") - 1)
            norm_post(Y, pa("post")[:, 0:8], W)

            dve.wait_ge(resid_ready, 8)
            norm_plain([X[:, c, 0:NX] for c in range(DC)], pa("pre")[:, 8:16], W, XH, XL)
            norm_plain([LAT[:, c, :] for c in range(3)], pa("qa"), WL, LQH, LQL)
            norm_plain([LAT[:, c, :] for c in range(3, 5)], pa("kva"), WL, LKH, LKL)
            rope(kr[:, 0:NX], dprobsT[0][:, 0:NX])
            for c in range(4):
                freed(dve, GEMM["oq"].j0 + 8 + c)
                rope(QR[:, 2 * c:2 * c + 2, :], dprobsT[0][:, 0:NX], True)

            def finish2(unit, h, q0, qn):
                o = (M1, MM)[h % 2]
                dve.wait_ge(pv_done, unit)
                nc.vector.tensor_tensor(SG[:, h, :], o[:, 0:NX], SG[:, h, :], ALU.mult).then_inc(gated, 1)
                low_operand(XL[:, h, 0:NX], SG[:, h, :], XH[:, h, 0:NX])
            attention(units2, 192.0 ** -0.5, (dprobs, dprobsT), finish2, True, ahead=2)
            g = GEMM["oout"]
            for p in range(8):
                j, b = g.j0 + p, (g.j0 + p) % 2
                dve.wait_ge(panel_done, j + 1)
                nc.vector.tensor_copy(Y2[:, p, :], G[b][:, 0:NX]).then_inc(bank_free[b], 1)
                add_square(p, NX, WY[0], WY[1])
            freed(dve, last("oout"))
            freed(dve, last("oout") - 1)
            norm_post(Y2, pa("post")[:, 8:16], WY)



def chunked(v):
    return np.ascontiguousarray(np.asarray(v).reshape(-1, P).T)


def panel(w, cols):
    w = np.asarray(w)[:, cols]
    return w.reshape(-1, P, P).transpose(1, 0, 2).reshape(P, -1)


def panels(inp):
    by = {}

    def add(name, items):
        g = GEMM[name]
        assert len(items) == g.n, name
        by.setdefault(g.kc, []).extend(items)

    run = lambda a: np.arange(a, a + P)
    for l in range(2):
        w = inp["w_in"][l]
        k0 = np.arange(256, 320)
        cols = [run(1024), run(768), run(1152), run(896), run(0), run(128), np.concatenate([k0, k0]),
                np.concatenate([k0 + 64, k0 + 64]), run(384), run(512), run(640), run(1280), run(1408)]
        add(f"win{l}", [panel(w, c) for c in cols])
        add(f"wout{l}", [panel(inp["w_out"][l], run(P * m)) for m in range(8)])
        for half in range(2):
            add(f"fin{l}{half}", [panel(inp["w_ffn_in"][l], run(2 * FH * P * s + (FH * half + i) * P))
                                  for i in range(FH) for s in range(2)])
            add(f"fout{l}{half}", [panel(inp["w_ffn_out"][l][FH * P * half:FH * P * (half + 1)], run(P * m)) for m in range(8)])
    w = inp["even_w_in_2"][0]
    add("eqk", [panel(w, run(P * c)) for c in range(8)])
    add("ev", [panel(w, run(1024 + P * c)) for c in range(8)])
    add("eg", [panel(w, run(2048 + P * c)) for c in range(8)])
    add("eout0", [panel(inp["even_w_out_2"][0][0:1024], run(P * m)) for m in range(8)])
    add("econv", [panel(w, run(at + P * c)) for c in range(8) for at in (4096, 5120, 3072, 6144)])
    add("eout1", [panel(inp["even_w_out_2"][0][1024:2048], run(P * m)) for m in range(8)])
    w = inp["odd_w_in_2"][0]
    r0 = np.arange(640, 704)
    add("oin", [panel(w, c) for c in [run(P * c) for c in range(5)] + [np.concatenate([r0, r0])]])
    add("ogate", [panel(w, run(704 + P * c)) for c in range(8)])
    w = inp["w_qb_2"][0]
    r0 = np.arange(128, 192)
    add("oq", [panel(w, run(192 * h)) for h in range(8)]
        + [panel(w, np.concatenate([r0 + 192 * 2 * c, r0 + 192 * (2 * c + 1)])) for c in range(4)])
    w = inp["w_kvb_2"][0]
    add("ok", [panel(w, run(256 * h)) for h in range(8)])
    add("ov", [panel(w, run(256 * h + P)) for h in range(8)])
    add("oout", [panel(inp["odd_w_out_2"][0], run(P * m)) for m in range(8)])
    return {kc: np.stack(v) for kc, v in by.items()}


def parameters(inp):
    par = np.zeros((P, NPAR), np.float32)

    def put(name, v):
        a, w = PAR[name]
        par[:, a:a + w] = v
    for l in range(2):
        b = chunked(inp["b_mod"][l])
        put(f"mod{l}", np.repeat(b, 2, axis=1))
        put(f"g1{l}", chunked(inp["g_norm1"][l]))
        put(f"g2{l}", chunked(inp["g_norm2"][l]))
        put(f"qg{l}", np.concatenate([inp["q_norm_g"][l]] * 2)[:, None])
        put(f"kg{l}", np.concatenate([inp["k_norm_g"][l]] * 2)[:, None])
        put(f"dw{l}", inp["conv_dw_w"][l].reshape(CONV, 2, P).transpose(2, 1, 0).reshape(P, -1))
        for key, name in (("dwb", "conv_dw_b"), ("lng", "conv_ln_g"), ("lnb", "conv_ln_b"), ("psc", "pool_scale")):
            put(f"{key}{l}", chunked(inp[name][l]))
    put("pre", np.concatenate([chunked(inp["pre_norm_2"][e]) for e in range(2)], axis=1))
    put("post", np.concatenate([chunked(inp["post_norm_2"][e]) for e in range(2)], axis=1))
    put("cw", inp["even_conv_w_2"][0].reshape(3, 8, P).transpose(2, 1, 0).reshape(P, -1))
    put("cb", chunked(inp["even_conv_b_2"][0]))
    put("gn", chunked(inp["ret_gn_2"][0]))
    put("qa", chunked(inp["q_a_norm_2"][0]))
    put("c", np.stack([chunked(inp["c"][0]), chunked(inp["c_ctx"])], axis=2).reshape(P, 16))
    put("kva", chunked(inp["kv_a_norm_2"][0]))
    return par


def constants():
    con = np.zeros((P, NCON), np.float64)

    def put(name, v):
        a, w = CON[name]
        con[:, a:a + w] = v
    i = np.arange(P)
    put("ident", np.eye(P))
    put("ones", 1.0)
    perm1, perm2 = np.zeros((P, P)), np.zeros((P, P))
    for m in range(P):
        perm1[m ^ 1, m] = 1.0 if m % 2 else -1.0
        perm2[m ^ 32, m] = 1.0 if m % 64 >= 32 else -1.0
    put("perm1", perm1)
    put("perm2", perm2)
    put("mask", np.where(i[None, :] <= i[:, None], 0.0, -1e30))
    win = np.array([2, 4, 8, 16])[np.stack([i // 64, 2 + i // 64], axis=1)]
    put("invw", 1.0 / win)
    edge = np.ones((P, 2, 2, 8))
    for c in range(2):
        for q in range(8):
            w = win[:, c]
            edge[:, c, 0, q] = w / np.minimum(w, q + w // 2)
            edge[:, c, 1, q] = w / np.minimum(w, 8 - q + w // 2)
    put("edge", edge.reshape(P, 32))
    put("inv", (10000.0 ** (-(np.arange(0, 64, 2, dtype=np.float32)) / np.float32(64)))[i % 32][:, None])
    put("eps", EPS)
    put("half", i[:, None] // 64 == np.arange(2)[None, :])
    return con.astype(np.float32)


def dft_tables():
    out = []
    for nn in (NX, NC):
        a = 2 * np.pi * (np.outer(np.arange(nn), np.arange(nn)) % nn) / nn
        s = 1.0 / np.sqrt(nn * 64.0)
        t = np.stack([np.cos(a) * s, np.sin(a) * s], axis=1)
        out.append(t.reshape(nn // P, P, 2 * nn).astype(np.float32))
    a = 2 * np.pi * (np.outer(np.arange(64), np.arange(64)) % 64) / 64
    d = np.zeros((2, 64, 2, 2, 64))
    for b in range(2):
        d[b, :, 0, b] = np.cos(a)
        d[b, :, 1, b] = -np.sin(a)
    return out[0], out[1], d.reshape(P, 256).astype(np.float32)


def rope_tables():
    inv = 10000.0 ** (-np.arange(16) / 16.0)
    row, col = np.arange(NX) // 64, np.arange(NX) % 64
    ang = np.concatenate([np.outer(inv, row), np.outer(inv, col)])[(np.arange(P) % 64) // 2]
    return np.cos(ang).astype(np.float32), np.sin(ang).astype(np.float32)


def decay_tables():
    lg = np.log1p(-np.exp2(-5.0 - np.arange(8)))
    rel = np.arange(NX)[None, :] - np.arange(P)[:, None]
    return np.where(rel >= 0, np.exp(lg[:, None, None] * np.maximum(rel, 0)) * 0.125, 0.0).astype(np.float32)


def kernel(**inputs):
    import concourse.bacc as _bacc
    from concourse.bass_utils import run_bass_kernel_spmd as _run

    inp = {k: np.asarray(v) for k, v in inputs.items()}
    w = panels(inp)
    dx, dc, dd = dft_tables()
    cosx, sinx = rope_tables()
    small = np.zeros((2, P, 1536), np.float32)
    for l in range(2):
        small[l, :, 0:512] = inp["w_fourier"][l].reshape(2, P, 256).transpose(1, 0, 2).reshape(P, 512)
        small[l, :, 512:1024] = inp["w_conv_pw"][l].reshape(2, P, 256).transpose(1, 0, 2).reshape(P, 512)
        for q in range(4):
            part, at = 64 * (q % 2), 1024 + P * (q // 2) + 64 * (q % 2)
            small[l, part:part + 64, at:at + 64] = inp["w_pool"][l][q]
        small[l, :, 1280:1536] = dd
    arrays = {
        "par": parameters(inp), "con": constants(),
        "xt": np.concatenate([inp["x"][0], inp["ctx"][0]]).T.reshape(DC, P, NT).transpose(1, 0, 2),
        "wmod": np.concatenate([np.stack([panel(inp["w_mod"][0], np.arange(P * m, P * m + P)) for m in range(MOD_DVE)]),
                                np.asarray(inp["w_mod"]).transpose(0, 2, 1).reshape(96, P, DC * P)[MOD_DVE:]]),
        "c": np.tile(np.concatenate([inp["c"][0], inp["c_ctx"]])[None], (P, 1)),
        "small": small, "dftx": dx, "dftc": dc, "cosx": cosx, "sinx": sinx, "decay": decay_tables(),
        "pos": np.tile(inp["positions_2"].reshape(1, NX), (P, 1)),
    }
    arrays.update({f"w{kc}": v for kc, v in w.items()})
    arrays = {k: np.ascontiguousarray(v) for k, v in arrays.items()}
    nc = _bacc.Bacc("TRN2", target_bir_lowering=False, num_devices=1)
    d = {k: nc.dram_tensor(f"in_{k}", v.shape, mybir.dt.from_np(v.dtype), kind="ExternalInput").ap() for k, v in arrays.items()}
    d["out"] = nc.dram_tensor("out_x", (P, DC, NX), F32, kind="ExternalOutput").ap()
    build_program(nc, d)
    r = _run(nc, [{f"in_{k}": v for k, v in arrays.items()}], core_ids=[0])
    out = r.results[0]["out_x"]
    return np.ascontiguousarray(out.transpose(1, 0, 2).reshape(DC * P, NX).T)[None]
```
